# Optimizing a Trainium2 kernel written in Bass

```python
import math
import jax, jax.numpy as jnp
from jax import lax
import numpy as np

D_MODEL = 1024
BATCH = 1
SEQ = 1024
DEPTH = 1

N_MIXERS = 3
DN_ALPHA = (2 * DEPTH) ** 0.25
DN_BETA = (8 * DEPTH) ** -0.25
LN_EPS = 1e-5
RMS_EPS = 1e-6

FOX_HEADS = 16
FOX_HEAD_DIM = D_MODEL // FOX_HEADS
FOX_Q_BLOCK = 128

GLA_HEADS = 4
GLA_DK = D_MODEL // 2
GLA_DV = D_MODEL
GLA_HK = GLA_DK // GLA_HEADS
GLA_HV = GLA_DV // GLA_HEADS
GLA_GATE_RANK = 16
GLA_GATE_TAU = 16.0
GLA_CHUNK = 64

SSD_D_INNER = 2 * D_MODEL
SSD_HEAD_DIM = 64
SSD_HEADS = SSD_D_INNER // SSD_HEAD_DIM
SSD_GROUPS = 8
SSD_STATE = 128
SSD_CONV = 4
SSD_CHUNK = 128
SSD_CONV_DIM = SSD_D_INNER + 2 * SSD_GROUPS * SSD_STATE

N_EXPERTS = 64
TOP_K = 8
N_EXPERT_GROUPS = 8
TOPK_GROUPS = 4
EXPERT_FF = 256
SHARED_FF = 256
ROUTED_SCALE = 2.5
MOE_BLOCK = 128

N_FOX = len(range(0, DEPTH, N_MIXERS))
N_GLA = len(range(1, DEPTH, N_MIXERS))
N_SSD = len(range(2, DEPTH, N_MIXERS))

kernel_name = 'hybrid_fox_gla_ssd_moe_deepnorm'

def layer_norm(x, g, b):
    xf = x.astype(jnp.float32)
    mu = jnp.mean(xf, -1, keepdims=True)
    var = jnp.mean(jnp.square(xf - mu), -1, keepdims=True)
    return ((xf - mu) * lax.rsqrt(var + LN_EPS) * g + b).astype(x.dtype)

def rms_norm(x, g):
    xf = x.astype(jnp.float32)
    return xf * lax.rsqrt(jnp.mean(xf * xf, -1, keepdims=True) + RMS_EPS) * g

def fox_mixer(x, w_in, b_f, w_out):
    B_, S, _ = x.shape
    H, Dh, Q = FOX_HEADS, FOX_HEAD_DIM, FOX_Q_BLOCK
    proj = x @ w_in
    q, k, v, f_logit = jnp.split(proj, [D_MODEL, 2 * D_MODEL, 3 * D_MODEL], axis=-1)
    q = q.reshape(B_, S, H, Dh)
    k = k.reshape(B_, S, H, Dh)
    v = v.reshape(B_, S, H, Dh)
    log_f = jax.nn.log_sigmoid(f_logit.astype(jnp.float32) + b_f.astype(jnp.float32))
    c = jnp.cumsum(log_f, axis=1).transpose(0, 2, 1)
    scale = Dh ** -0.5
    outs = []
    for qb in range(S // Q):
        t0, t1 = qb * Q, (qb + 1) * Q
        logits = jnp.einsum('bqhd,bkhd->bhqk', q[:, t0:t1], k[:, :t1],
                            preferred_element_type=jnp.float32) * scale
        logits = logits + c[:, :, t0:t1, None] - c[:, :, None, :t1]
        causal = (t0 + jnp.arange(Q))[:, None] >= jnp.arange(t1)[None, :]
        p = jax.nn.softmax(jnp.where(causal, logits, -jnp.inf), axis=-1)
        outs.append(jnp.einsum('bhqk,bkhd->bqhd', p.astype(v.dtype), v[:, :t1]))
    o = jnp.concatenate(outs, axis=1).reshape(B_, S, D_MODEL)
    return o @ w_out

def gla_mixer(x, w_in, w_gate_up, b_gate, norm_g, w_out):
    B_, S, _ = x.shape
    H, dk, dv, C = GLA_HEADS, GLA_HK, GLA_HV, GLA_CHUNK
    n = S // C
    proj = x @ w_in
    q, k, v, r, g_low = jnp.split(
        proj, [GLA_DK, 2 * GLA_DK, 2 * GLA_DK + GLA_DV, 2 * GLA_DK + 2 * GLA_DV], axis=-1)
    log_a = jax.nn.log_sigmoid((g_low @ w_gate_up + b_gate).astype(jnp.float32)) / GLA_GATE_TAU

    def chunks(t, d):
        return t.reshape(B_, n, C, H, d).astype(jnp.float32)

    qc = chunks(q, dk) * (dk ** -0.5)
    kc = chunks(k, dk)
    vc = chunks(v, dv)
    bcum = jnp.cumsum(chunks(log_a, dk), axis=2)
    b_last = bcum[:, :, -1:]
    q_dec = qc * jnp.exp(bcum)
    k_inv = kc * jnp.exp(-bcum)
    k_to_end = kc * jnp.exp(b_last - bcum)
    att = jnp.einsum('bnthk,bnshk->bnhts', q_dec, k_inv)
    att = jnp.where(jnp.tril(jnp.ones((C, C), bool)), att, 0.0)
    o_intra = jnp.einsum('bnhts,bnshv->bnthv', att, vc)
    chunk_kv = jnp.einsum('bnshk,bnshv->bnhkv', k_to_end, vc)
    decay = jnp.exp(b_last[:, :, 0])

    def step(state, inp):
        kv, dec = inp
        return state * dec[..., None] + kv, state

    s0 = jnp.zeros((B_, H, dk, dv), jnp.float32)
    _, prev = lax.scan(step, s0, (jnp.moveaxis(chunk_kv, 1, 0), jnp.moveaxis(decay, 1, 0)))
    prev = jnp.moveaxis(prev, 0, 1)
    o_inter = jnp.einsum('bnthk,bnhkv->bnthv', q_dec, prev)
    o = rms_norm(o_intra + o_inter, norm_g)
    o = o.reshape(B_, S, GLA_DV).astype(x.dtype) * jax.nn.silu(r)
    return o @ w_out

def ssd_mixer(x, w_in, conv_w, conv_b, dt_bias, a_log, d_skip, norm_g, w_out):
    B_, S, _ = x.shape
    G, Hg, P, N, L = SSD_GROUPS, SSD_HEADS // SSD_GROUPS, SSD_HEAD_DIM, SSD_STATE, SSD_CHUNK
    n = S // L
    proj = x @ w_in
    z, xbc, dt_raw = jnp.split(proj, [SSD_D_INNER, SSD_D_INNER + SSD_CONV_DIM], axis=-1)
    xbc = lax.conv_general_dilated(xbc, conv_w[:, None, :], (1,), [(SSD_CONV - 1, 0)],
                                   dimension_numbers=('NWC', 'WIO', 'NWC'),
                                   feature_group_count=SSD_CONV_DIM)
    xbc = jax.nn.silu(xbc + conv_b).astype(jnp.float32)
    xs, bm, cm = jnp.split(xbc, [SSD_D_INNER, SSD_D_INNER + G * N], axis=-1)
    xs = xs.reshape(B_, n, L, G, Hg, P)
    bm = bm.reshape(B_, n, L, G, N)
    cm = cm.reshape(B_, n, L, G, N)
    dt = jax.nn.softplus(dt_raw.astype(jnp.float32) + dt_bias).reshape(B_, n, L, G, Hg)
    a = dt * (-jnp.exp(a_log.astype(jnp.float32))).reshape(G, Hg)
    acum = jnp.cumsum(a, axis=2)
    xdt = xs * dt[..., None]
    ac = jnp.moveaxis(acum, 2, -1)
    seg = ac[..., :, None] - ac[..., None, :]
    decay = jnp.exp(jnp.where(jnp.tril(jnp.ones((L, L), bool)), seg, -jnp.inf))
    cb = jnp.einsum('bctgn,bcsgn->bcgts', cm, bm)
    y_diag = jnp.einsum('bcghts,bcsghp->bctghp', cb[:, :, :, None] * decay, xdt)
    a_last = acum[:, :, -1]
    to_end = jnp.exp(a_last[:, :, None] - acum)
    states = jnp.einsum('bcsgn,bcsghp->bcghpn', bm, xdt * to_end[..., None])

    def step(h, inp):
        st, dec = inp
        return h * dec[..., None, None] + st, h

    h0 = jnp.zeros((B_, G, Hg, P, N), jnp.float32)
    _, prev = lax.scan(step, h0, (jnp.moveaxis(states, 1, 0), jnp.moveaxis(jnp.exp(a_last), 1, 0)))
    prev = jnp.moveaxis(prev, 0, 1)
    y_off = jnp.einsum('bctgn,bcghpn->bctghp', cm, prev) * jnp.exp(acum)[..., None]
    y = y_diag + y_off + xs * d_skip.astype(jnp.float32).reshape(G, Hg, 1)
    y = y.reshape(B_, S, G, Hg * P) * jax.nn.silu(z.astype(jnp.float32)).reshape(B_, S, G, Hg * P)
    y = rms_norm(y, norm_g.reshape(G, Hg * P))
    return y.reshape(B_, S, SSD_D_INNER).astype(x.dtype) @ w_out

def moe(x, w_router, router_bias, w_gate, w_up, w_down, ws_gate, ws_up, ws_down):
    B_, S, D = x.shape
    T = B_ * S
    xf = x.reshape(T, D)
    scores = jax.nn.sigmoid((xf @ w_router).astype(jnp.float32))
    sel = scores + router_bias.astype(jnp.float32)
    grp_score = lax.top_k(sel.reshape(T, N_EXPERT_GROUPS, -1), 2)[0].sum(-1)
    _, top_grp = lax.top_k(grp_score, TOPK_GROUPS)
    grp_mask = jnp.any(top_grp[..., None] == jnp.arange(N_EXPERT_GROUPS), axis=-2)
    exp_mask = jnp.repeat(grp_mask, N_EXPERTS // N_EXPERT_GROUPS, axis=-1)
    _, top_e = lax.top_k(jnp.where(exp_mask, sel, -jnp.inf), TOP_K)
    w = jnp.take_along_axis(scores, top_e, axis=-1)
    w = w / jnp.sum(w, -1, keepdims=True) * ROUTED_SCALE

    A = T * TOP_K
    e_flat = top_e.reshape(-1)
    tok_flat = jnp.repeat(jnp.arange(T, dtype=jnp.int32), TOP_K)
    w_flat = w.reshape(-1)
    order = jnp.argsort(e_flat)
    e_sorted = e_flat[order]
    counts = jnp.bincount(e_flat, length=N_EXPERTS)
    padded = (counts + MOE_BLOCK - 1) // MOE_BLOCK * MOE_BLOCK
    start = jnp.cumsum(counts) - counts
    pend = jnp.cumsum(padded)
    pstart = pend - padded
    dest = pstart[e_sorted] + jnp.arange(A) - start[e_sorted]
    n_blocks = -(-A // MOE_BLOCK) + N_EXPERTS
    rows_total = n_blocks * MOE_BLOCK
    row_tok = jnp.full((rows_total,), T, jnp.int32).at[dest].set(tok_flat[order])
    row_w = jnp.zeros((rows_total,), jnp.float32).at[dest].set(w_flat[order])
    block_exp = jnp.clip(jnp.searchsorted(pend, jnp.arange(n_blocks) * MOE_BLOCK, side='right'),
                         0, N_EXPERTS - 1)
    x_pad = jnp.concatenate([xf, jnp.zeros((1, D), xf.dtype)], axis=0)

    def body(acc, blk):
        rows, rw, e = blk
        xb = x_pad[rows]
        h = jax.nn.silu(xb @ w_gate[e]) * (xb @ w_up[e])
        yb = (h @ w_down[e]) * rw[:, None].astype(xb.dtype)
        return acc.at[rows].add(yb), None

    acc, _ = lax.scan(body, jnp.zeros((T + 1, D), xf.dtype),
                      (row_tok.reshape(n_blocks, MOE_BLOCK), row_w.reshape(n_blocks, MOE_BLOCK), block_exp))
    shared = (jax.nn.silu(xf @ ws_gate) * (xf @ ws_up)) @ ws_down
    return (acc[:T] + shared).reshape(B_, S, D)

def setup_inputs(seed: int = 0) -> dict:
    key = jax.random.key(seed)
    ks = iter(jax.random.split(key, 32))
    D = D_MODEL

    def nrm(shape, fan_in, scale=1.0):
        return jax.random.normal(next(ks), shape, jnp.float32) * (scale * fan_in ** -0.5)

    def small(shape, s=0.01):
        return jax.random.normal(next(ks), shape, jnp.float32) * s

    x = jax.random.normal(next(ks), (BATCH, SEQ, D), jnp.float32)

    fox_w_in = nrm((N_FOX, D, 3 * D + FOX_HEADS), D)
    fox_w_in = fox_w_in.at[:, :, 2 * D:3 * D].multiply(DN_BETA)
    fox_b_f = jax.random.uniform(next(ks), (N_FOX, FOX_HEADS), jnp.float32, 1.0, 4.0)
    fox_w_out = nrm((N_FOX, D, D), D, DN_BETA)

    gla_w_in = nrm((N_GLA, D, 2 * GLA_DK + 2 * GLA_DV + GLA_GATE_RANK), D)
    gla_w_in = gla_w_in.at[:, :, 2 * GLA_DK:2 * GLA_DK + GLA_DV].multiply(DN_BETA)
    gla_w_gate_up = nrm((N_GLA, GLA_GATE_RANK, GLA_DK), GLA_GATE_RANK)
    gla_b_gate = small((N_GLA, GLA_DK), 0.1)
    gla_norm = 1.0 + small((N_GLA, GLA_HV))
    gla_w_out = nrm((N_GLA, GLA_DV, D), GLA_DV, DN_BETA)

    ssd_w_in = nrm((N_SSD, D, SSD_D_INNER + SSD_CONV_DIM + SSD_HEADS), D)
    ssd_w_in = ssd_w_in.at[:, :, SSD_D_INNER:2 * SSD_D_INNER].multiply(DN_BETA)
    ssd_conv_w = nrm((N_SSD, SSD_CONV, SSD_CONV_DIM), SSD_CONV)
    ssd_conv_b = small((N_SSD, SSD_CONV_DIM), 0.02)
    dt0 = jnp.exp(jax.random.uniform(next(ks), (N_SSD, SSD_HEADS), jnp.float32,
                                     math.log(1e-3), math.log(1e-1)))
    ssd_dt_bias = dt0 + jnp.log(-jnp.expm1(-dt0))
    ssd_a_log = jnp.log(jax.random.uniform(next(ks), (N_SSD, SSD_HEADS), jnp.float32, 1.0, 16.0))
    ssd_d = 1.0 + small((N_SSD, SSD_HEADS), 0.1)
    ssd_norm = 1.0 + small((N_SSD, SSD_D_INNER))
    ssd_w_out = nrm((N_SSD, SSD_D_INNER, D), SSD_D_INNER, DN_BETA)

    ln1_g = 1.0 + small((DEPTH, D))
    ln1_b = small((DEPTH, D))

    moe_router = nrm((DEPTH, D, N_EXPERTS), D)
    moe_router_bias = small((DEPTH, N_EXPERTS), 0.01)
    moe_w_gate = nrm((DEPTH, N_EXPERTS, D, EXPERT_FF), D)
    moe_w_up = nrm((DEPTH, N_EXPERTS, D, EXPERT_FF), D)
    moe_w_down = nrm((DEPTH, N_EXPERTS, EXPERT_FF, D), EXPERT_FF, DN_BETA)
    moe_ws_gate = nrm((DEPTH, D, SHARED_FF), D)
    moe_ws_up = nrm((DEPTH, D, SHARED_FF), D)
    moe_ws_down = nrm((DEPTH, SHARED_FF, D), SHARED_FF, DN_BETA)

    ln2_g = 1.0 + small((DEPTH, D))
    ln2_b = small((DEPTH, D))

    return {'x': x,
            'fox_w_in': fox_w_in, 'fox_b_f': fox_b_f, 'fox_w_out': fox_w_out,
            'gla_w_in': gla_w_in, 'gla_w_gate_up': gla_w_gate_up, 'gla_b_gate': gla_b_gate,
            'gla_norm': gla_norm, 'gla_w_out': gla_w_out,
            'ssd_w_in': ssd_w_in, 'ssd_conv_w': ssd_conv_w, 'ssd_conv_b': ssd_conv_b,
            'ssd_dt_bias': ssd_dt_bias, 'ssd_a_log': ssd_a_log, 'ssd_d': ssd_d,
            'ssd_norm': ssd_norm, 'ssd_w_out': ssd_w_out,
            'ln1_g': ln1_g, 'ln1_b': ln1_b,
            'moe_router': moe_router, 'moe_router_bias': moe_router_bias,
            'moe_w_gate': moe_w_gate, 'moe_w_up': moe_w_up, 'moe_w_down': moe_w_down,
            'moe_ws_gate': moe_ws_gate, 'moe_ws_up': moe_ws_up, 'moe_ws_down': moe_ws_down,
            'ln2_g': ln2_g, 'ln2_b': ln2_b}

def reference(x, fox_w_in, fox_b_f, fox_w_out, gla_w_in, gla_w_gate_up, gla_b_gate, gla_norm,
              gla_w_out, ssd_w_in, ssd_conv_w, ssd_conv_b, ssd_dt_bias, ssd_a_log, ssd_d,
              ssd_norm, ssd_w_out, ln1_g, ln1_b, moe_router, moe_router_bias, moe_w_gate,
              moe_w_up, moe_w_down, moe_ws_gate, moe_ws_up, moe_ws_down, ln2_g, ln2_b):
    for i in range(DEPTH):
        kind, j = i % N_MIXERS, i // N_MIXERS
        if kind == 0:
            y = fox_mixer(x, fox_w_in[j], fox_b_f[j], fox_w_out[j])
        elif kind == 1:
            y = gla_mixer(x, gla_w_in[j], gla_w_gate_up[j], gla_b_gate[j], gla_norm[j], gla_w_out[j])
        else:
            y = ssd_mixer(x, ssd_w_in[j], ssd_conv_w[j], ssd_conv_b[j], ssd_dt_bias[j],
                          ssd_a_log[j], ssd_d[j], ssd_norm[j], ssd_w_out[j])
        x = layer_norm(DN_ALPHA * x + y, ln1_g[i], ln1_b[i])
        y = moe(x, moe_router[i], moe_router_bias[i], moe_w_gate[i], moe_w_up[i], moe_w_down[i],
                moe_ws_gate[i], moe_ws_up[i], moe_ws_down[i])
        x = layer_norm(DN_ALPHA * x + y, ln2_g[i], ln2_b[i])
    return x


_drawn_inputs = setup_inputs


def setup_inputs(seed=0):
    import zlib

    import numpy as np

    out = dict(_drawn_inputs(seed))
    spreads = {}
    factors = {}
    for name, (base, spread) in spreads.items():
        noise = np.random.default_rng([zlib.crc32(name.encode()), seed]).standard_normal(out[name].shape)
        drawn = base * np.exp(spread * noise) if base else spread * noise
        out[name] = __import__('jax').numpy.asarray(drawn.astype(out[name].dtype))
    for name, factor in factors.items():
        out[name] = (out[name] * factor).astype(out[name].dtype)
    return out
```

```python
from contextlib import ExitStack

import concourse.bass as bass
from concourse import mybir

P = 128
BANK = 512
ALU = mybir.AluOpType
ACT = mybir.ActivationFunctionType
F32 = mybir.dt.float32
F32R = mybir.dt.float32r
BF16 = mybir.dt.bfloat16
AX_X = mybir.AxisListType.X
NEVER = -1e30

T, D, HEADS, DH = 1024, 1024, 16, 64
TT = T // P
DC = D // P
PAIRS = HEADS // 2
VC = 256
NVC = D // VC
ONE_ROW, MAX_ROW = 64, 96
SCALE = DH ** -0.5

BY_QUERY = [(t, k0, min(BANK, (t + 1) * P - k0)) for t in range(TT) for k0 in range(0, (t + 1) * P, BANK)]
BY_KEY = []
for _t in range(TT):
    for _q0, _q1 in ((_t * P, BANK), (max(_t * P, BANK), T)):
        if _q0 < _q1:
            BY_KEY.append((_t, _q0, _q1 - _q0, sum(b[2] for b in BY_KEY)))
PROBS = sum(b[2] for b in BY_KEY)
NQ, NR, NK = len(BY_QUERY), 2, len(BY_KEY)
SLOTS = NQ + NR + NK


ALPHA = 2.0 ** 0.25
LN_EPS = 1e-5
E, GROUPS, TOP_GROUPS, TOP_K, FF = 64, 8, 4, 8, 256
GE = E // GROUPS
ROUTED_SCALE = 2.5
FC = FF // P
TAB_BLOCKS = T // P
TAB = E * TAB_BLOCKS
ROWS = T + P
ROW_W = D + E
STAGES = 6
OUT = -3e38
I32 = mybir.dt.int32
U32 = mybir.dt.uint32


def split_matmul(pe, out, w_hi, w_lo, m_hi, m_lo, start, stop):
    pe.matmul(out, w_hi, m_hi, start=start, stop=False, skip_group_check=True)
    pe.matmul(out, w_hi, m_lo, start=False, stop=False, skip_group_check=True)
    return pe.matmul(out, w_lo, m_hi, start=False, stop=stop, skip_group_check=True)


def build(nc, x, w_in, b_f, w_out, ln1_g, ln1_b, router, router_bias, w_gate, w_up, w_down, ws_gate, ws_up,
          ws_down, ln2_g, ln2_b, out):
    with ExitStack() as ctx:
        def sem(n):
            return ctx.enter_context(nc.semaphore(n))

        def sb(n, s, d=F32, c=ctx):
            return c.enter_context(nc.sbuf_tensor(n, s, d))

        banks = [ctx.enter_context(nc.psum_tensor(f"bank{i}", [P, BANK], F32)) for i in range(2)]
        out_ps = ctx.enter_context(nc.psum_tensor("out_ps", [P, T], F32))
        q_ps = ctx.enter_context(nc.psum_tensor("q_ps", [P, T], F32))
        k_ps = ctx.enter_context(nc.psum_tensor("k_ps", [P, T], F32))

        v_dram = nc.dram_tensor("v_scratch", (T, D), F32, kind="Internal").ap()
        c_dram = nc.dram_tensor("c_scratch", (2, HEADS, T), F32, kind="Internal").ap()

        rows_dram = nc.dram_tensor("rows_scratch", (ROWS, ROW_W), F32, kind="Internal").ap()
        acc_dram = nc.dram_tensor("acc_scratch", (ROWS, D), F32, kind="Internal").ap()
        tab_dram = nc.dram_tensor("tab_scratch", (P * TAB, 1), I32, kind="Internal").ap()

        ident = sb("ident", [P, P])
        identb = sb("identb", [P, P], BF16)
        mask_qk = sb("mask_qk", [P, P], BF16)
        mask_kq = sb("mask_kq", [P, P], BF16)
        before = sb("before", [P, P], BF16)
        ones_b = sb("ones_b", [P, P], BF16)
        extra_at = sb("extra_at", [1, E + 2], I32)
        extra_n = sb("extra_n", [1, E], I32)
        with ExitStack() as early:
            attn = sb("xs", [P, PAIRS, T], c=early)
            xs = attn
            with ExitStack() as x1s:
                xt_hi = sb("xt_hi", [P, DC, T], F32R, c=x1s)
                xt_lo = sb("xt_lo", [P, DC, T], F32R, c=x1s)
                wqk = sb("wqk", [P, DC, 2, P], c=x1s)
                wqk_hi = sb("wqk_hi", [P, DC, 2, P], F32R, c=x1s)
                wqk_lo = sb("wqk_lo", [P, DC, 2, P], F32R, c=x1s)
                with ExitStack() as a:
                    wv = sb("wv", [P, 2, DC, VC], c=a)
                    wv_hi = sb("wv_hi", [P, 2, DC, VC], F32R, c=a)
                    wv_lo = sb("wv_lo", [P, 2, DC, VC], F32R, c=a)
                    v_out = sb("v_out", [P, 2, 2, VC], c=a)
                    wf = sb("wf", [P, DC, HEADS], c=a)
                    wf_hi = sb("wf_hi", [P, DC, HEADS], F32R, c=a)
                    wf_lo = sb("wf_lo", [P, DC, HEADS], F32R, c=a)
                    bf = sb("bf", [P, HEADS], c=a)
                    z = sb("z", [P, TT, HEADS], c=a)
                    zabs = sb("zabs", [P, TT, HEADS], c=a)
                    zexp = sb("zexp", [P, TT, HEADS], c=a)
                    zlog = sb("zlog", [P, TT, HEADS], c=a)
                    zmin = sb("zmin", [P, TT, HEADS], c=a)
                    gate8 = sb("gate8", [P, TT, HEADS], c=a)
                    upto = sb("upto", [P, T], c=a)
                    c_hi = sb("c_hi", [HEADS, T], F32R, c=a)
                    c_lo = sb("c_lo", [HEADS, T], F32R, c=a)
                with ExitStack() as b:
                    q_hi = [sb(f"q_hi{i}", [P, T], F32R, c=b) for i in range(2)]
                    q_lo = [sb(f"q_lo{i}", [P, T], F32R, c=b) for i in range(2)]
                    k_hi = [sb(f"k_hi{i}", [P, T], F32R, c=b) for i in range(2)]
                    k_lo = [sb(f"k_lo{i}", [P, T], F32R, c=b) for i in range(2)]
                    va = [sb(f"va{i}", [P, TT, P], c=b) for i in range(2)]
                    probs = sb("probs", [P, PROBS], c=b)
                    mx2 = sb("mx2", [P, TT, 2], c=b)
                    mx = sb("mx", [P, TT], c=b)
                    rec = sb("rec", [DH, T], c=b)
            with ExitStack() as d:
                wo_hi = sb("wo_hi", [P, DC, D], F32R, c=d)
                wo_lo = sb("wo_lo", [P, DC, D], F32R, c=d)
                wo = sb("wo", [P, STAGES, D], c=d)
                ot_hi = sb("ot_hi", [P, DC, P], F32R, c=d)
                ot_lo = sb("ot_lo", [P, DC, P], F32R, c=d)
                x_res = sb("x_res", [P, D], c=d)
                r1 = sb("r1", [P, D], c=d)
                xn = sb("xn", [P, D], c=d)
                xg1 = sb("xg1", [P, D], c=d)
                x1 = sb("x1", [P, D], c=d)
                x1t_hi = sb("x1t_hi", [P, DC, P], F32R, c=d)
                x1t_lo = sb("x1t_lo", [P, DC, P], F32R, c=d)
                g1 = sb("g1", [P, D], c=d)
                b1 = sb("b1", [P, D], c=d)
                wr = sb("wr", [P, DC, E], c=d)
                wr_hi = sb("wr_hi", [P, DC, E], F32R, c=d)
                wr_lo = sb("wr_lo", [P, DC, E], F32R, c=d)
                rb = sb("rb", [P, E], c=d)
                stat = sb("stat", [P, 2, 6], c=d)
                mv = sb("mv", [P, 2], c=d)
                rstd = sb("rstd", [P, 1], c=d)
                std = sb("std", [P, 1], c=d)
                eps = sb("eps", [P, 1], c=d)
                ex = sb("ex", [P, E], c=d)
                ex1 = sb("ex1", [P, E], c=d)
                score = sb("score_e", [P, E], c=d)
                sel = sb("sel", [P, E], c=d)
                top_g = sb("top_g", [P, GROUPS, 8], c=d)
                gsum = sb("gsum", [P, GROUPS], c=d)
                gsort = sb("gsort", [P, GROUPS], c=d)
                gtop = sb("gtop", [P, GROUPS], c=d)
                gleft = sb("gleft", [P, GROUPS], c=d)
                gpen = sb("gpen", [P, GROUPS], c=d)
                selm = sb("selm", [P, E], c=d)
                top8 = sb("top8", [P, 8], c=d)
                left = sb("left", [P, E], c=d)
                chosen = sb("chosen", [P, E], c=d)
                chosen_b = sb("chosen_b", [P, E], BF16, c=d)
                wraw = sb("wraw", [P, E], c=d)
                wsum = sb("wsum", [P, 1], c=d)
                wrec = sb("wrec", [P, 1], c=d)
                wts = sb("wts", [P, E], c=d)
                base = sb("base", [P, E], c=d)
                pos = sb("pos", [P, E], I32, c=d)
                pos_m = sb("pos_m", [P, E], I32, c=d)
                pos_q = sb("pos_q", [P, E], I32, c=d)
                pos_b = sb("pos_b", [P, E], c=d)
                dest = sb("dest", [P, E], c=d)
                dest1 = sb("dest1", [P, E], c=d)
                dest8 = sb("dest8", [P, 8], c=d)
                dest_i = sb("dest_i", [P, 8], I32, c=d)
                e8 = sb("e8", [P, E], c=d)
                tok_all = sb("tok_all", [P, TT], I32, c=d)
                tok = sb("tok", [P, 1], I32, c=d)
                tab0 = sb("tab0", [P, TAB], I32, c=d)
                zeros = sb("zeros", [P, ROW_W], c=d)
                nblk = [sb(f"nblk{i}", [1, E], c=d) for i in range(2)]
                nblk_i = [sb(f"nblk_i{i}", [1, E], I32, c=d) for i in range(2)]
        with ExitStack() as m:
            raw_gu = [sb(f"raw_gu{i}", [P, 2, DC, FF], c=m) for i in range(2)]
            raw_dn = [sb(f"raw_dn{i}", [P, FC, D], c=m) for i in range(2)]
            split = []
            for i in range(2):
                split.append((sb(f"gu_hi{i}", [P, 2, DC, FF], F32R, c=m), sb(f"gu_lo{i}", [P, 2, DC, FF], F32R, c=m),
                              sb(f"dn_hi{i}", [P, FC, D], F32R, c=m), sb(f"dn_lo{i}", [P, FC, D], F32R, c=m)))
            xg = [sb(f"x_rows{i}", [P, ROW_W], c=m) for i in range(3)]
            xb_hi = [sb(f"xb_hi{i}", [P, DC, P], F32R, c=m) for i in range(3)]
            xb_lo = [sb(f"xb_lo{i}", [P, DC, P], F32R, c=m) for i in range(3)]
            ys = [sb(f"ys{i}", [P, D], c=m) for i in range(3)]
            sg = sb("sg", [P, FF], c=m)
            hh = sb("hh", [P, FF], c=m)
            ht_hi = sb("ht_hi", [P, FC, P], F32R, c=m)
            ht_lo = sb("ht_lo", [P, FC, P], F32R, c=m)
            wcol = [sb(f"wcol{i}", [P, 1], c=m) for i in range(3)]
            tab = sb("tab", [P, TAB], I32, c=m)
            gidx = [sb(f"gidx{i}", [P, 1], I32, c=m) for i in range(3)]
            sidx = [sb(f"sidx{i}", [P, 1], I32, c=m) for i in range(3)]
        with ExitStack() as f:
            g2 = sb("g2", [P, D], c=f)
            b2 = sb("b2", [P, D], c=f)
            fin = [sb(f"fin{i}", [P, D], c=f) for i in range(2)]
            fn = [sb(f"fn{i}", [P, D], c=f) for i in range(2)]
            fo = [sb(f"fo{i}", [P, D], c=f) for i in range(2)]
            fstat = [sb(f"fstat{i}", [P, 2, 6], c=f) for i in range(2)]
            fmv = [sb(f"fmv{i}", [P, 2], c=f) for i in range(2)]
            feps = sb("feps", [P, 1], c=f)
            fstd = [sb(f"fstd{i}", [P, 1], c=f) for i in range(2)]
            frstd = [sb(f"frstd{i}", [P, 1], c=f) for i in range(2)]
            fnm = [sb(f"fnm{i}", [P, 1], c=f) for i in range(2)]

        S = {}
        for n in ("consts masks xt_ps xt_hi_ok xt_lo_ok wf_in wf_ok bf_in z_ps z_ok zabs_ok zexp_ok zlog_ok zmin_ok gate_ok"
                  " c_ps c_hi_ok c_lo_ok c_stored wv_hi_ok wv_lo_ok v_ps v_ok aug aug0 mx20"
                  " wqk_in wqk_hi_ok wqk_lo_ok proj score maxed mx_ok r_hi r_lo exped pv rec_ok normed"
                  " wo_hi_ok wo_lo_ok c_loads wr_ok ot_hi_ok ot_lo_ok oproj r1_ok ln_step x1_ok x_res_in x1_stored wts_stored"
                  " x1t_ps x1t_hi_ok x1t_lo_ok logit_ps ex_ok route_step chosen_ok wts_ok pos_ps pos_step dest_ok c_const c_fill"
                  " tok_ok listed route0 extra_ok"
                  " w_hi_ok w_lo_ok tab_in idx_ok m_start m_gu m_t m_xhi m_xlo m_sg m_h m_ht m_hthi m_htlo m_dn m_y m_sent"
                  " x_in_ok x_t x_xhi x_xlo x_gu x_sg x_h x_ht x_hthi x_htlo x_dn x_y x_sent summed"
                  " stands g2_in std_ok var_ok f_var f_std f_step f_mv f_norm f_g f_out").split():
            S[n] = sem(n)
        x_in = [sem(f"x_in{t}") for t in range(TT)]
        wv_in = [sem(f"wv_in{i}") for i in range(2)]
        v_stored = [sem(f"v_stored{i}") for i in range(2)]
        c_in = [sem(f"c_in{i}") for i in range(2)]
        va_in = [sem(f"va_in{i}") for i in range(2)]
        ev_hi = [sem(f"ev_hi{i}") for i in range(2)]
        ev_lo = [sem(f"ev_lo{i}") for i in range(2)]
        wo_in = [sem(f"wo_in{i}") for i in range(STAGES)]
        w_raw = [sem(f"w_raw{i}") for i in range(2)]
        got = [sem(f"got{i}") for i in range(2)]
        put = [sem(f"put{i}") for i in range(2)]
        fin_in = [sem(f"fin_in{i}") for i in range(2)]
        stored = [sem(f"stored{i}") for i in range(2)]

        w_rows = w_in.rearrange("(c p) n -> p c n", p=P)
        v_rows = v_dram.rearrange("(t p) n -> p t n", p=P)
        NXT = DC * 2
        idx_ok = {k: sem(f"idx_{k}") for k in ("g", "s", "xg", "xs")}

        def load_wqk(sp, p):
            for j in range(2):
                sp.dma_start(wqk[:, :, j, :], w_rows[:, :, bass.ds(j * D + p * P, P)]).then_inc(S["wqk_in"], 16)

        def load_c(sp, p, par):
            for j, k in enumerate((k_hi[par], k_lo[par])):
                sp.dma_start(k[ONE_ROW:ONE_ROW + 1, :].bitcast(F32), c_dram[j, bass.ds(2 * p + par, 1), :]).then_inc(c_in[par], 16)

        def load_v(sp, p, par):
            sp.dma_start(va[par][:, :, 0:DH], v_rows[:, :, bass.ds((2 * p + par) * DH, DH)]).then_inc(va_in[par], 16)

        ds = bass.ds
        PIECES = 6
        SH = TT

        def piece(j, k):
            g_hi, g_lo, d_hi, d_lo = split[j]
            if k < 4:
                return tuple(w[:, k // 2, (k % 2) * 4:(k % 2) * 4 + 4, :] for w in (raw_gu[j], g_hi, g_lo))
            return tuple(w[:, k - 4, :] for w in (raw_dn[j], d_hi, d_lo))

        def strided(a):
            return a.rearrange("p (k c) -> p c k", k=P)

        def static(e):
            return isinstance(e, int)

        def stand(eng):
            eng.sem_inc(S["stands"], 1)

        block = ctx.enter_context(nc.Block())

        @block.sync
        def _(sp):
            for t in range(TT):
                sp.dma_start(xs[:, t, :], x[t * P:(t + 1) * P, :]).then_inc(x_in[t], 16)
            sp.dma_start(wf[:], w_rows[:, :, 3 * D:3 * D + HEADS]).then_inc(S["wf_in"], 16)
            sp.dma_start(bf[:], b_f.to_broadcast([P, HEADS])).then_inc(S["bf_in"], 16)
            for n in range(NVC):
                if n >= 2:
                    sp.wait_ge(S["wv_lo_ok"], n - 1)
                sp.dma_start(wv[:, n % 2], w_rows[:, :, 2 * D + n * VC:2 * D + (n + 1) * VC]).then_inc(wv_in[n % 2], 16)
            load_wqk(sp, 0)
            for n in range(NVC * TT // 2):
                sp.wait_ge(S["v_ok"], n + 1)
                c, t = n // (TT // 2), n % (TT // 2)
                sp.dma_start(v_rows[:, 2 * t:2 * t + 2, c * VC:(c + 1) * VC], v_out[:, n % 2]).then_inc(v_stored[n % 2], 16)
            sp.wait_ge(S["c_lo_ok"], 2)
            sp.dma_start(c_dram[0], c_hi[:].bitcast(F32)).then_inc(S["c_stored"], 16)
            sp.dma_start(c_dram[1], c_lo[:].bitcast(F32)).then_inc(S["c_stored"], 16)
            sp.wait_ge(S["c_stored"], 32)
            for i in range(2):
                sp.wait_ge(v_stored[i], 16 * NVC * TT // 4)
            sp.wait_ge(S["wqk_lo_ok"], 1)
            load_wqk(sp, 1)
            sp.wait_ge(S["aug"], 2)
            for par in range(2):
                load_c(sp, 0, par)
                load_v(sp, 0, par)

            def pair(p):
                sp.wait_ge(S["score"], SLOTS * (2 * p + 1))
                load_c(sp, p + 1, 0)
                sp.wait_ge(S["pv"], 2 * p + 1)
                load_v(sp, p + 1, 0)
                sp.wait_ge(S["score"], SLOTS * (2 * p + 2))
                load_c(sp, p + 1, 1)
                sp.wait_ge(S["pv"], 2 * p + 2)
                load_v(sp, p + 1, 1)
            with sp.Fori(0, PAIRS - 2) as p:
                sp.wait_ge(S["wqk_lo_ok"], p + 2)
                load_wqk(sp, p + 2)
                pair(p)
            pair(PAIRS - 2)

            sp.wait_ge(S["proj"], PAIRS)
            for c in range(DC):
                if c >= STAGES:
                    sp.wait_ge(S["wo_lo_ok"], c - STAGES + 1)
                sp.dma_start(wo[:, c % STAGES], w_out[c * P:(c + 1) * P, :]).then_inc(wo_in[c % STAGES], 16)
            sp.wait_ge(S["normed"], HEADS)
            sp.dma_start(x_res[:], x[0:P, :]).then_inc(S["x_res_in"], 16)
            sp.dma_start(g1[:], ln1_g.to_broadcast([P, D])).then_inc(S["c_loads"], 16)
            sp.dma_start(b1[:], ln1_b.to_broadcast([P, D])).then_inc(S["c_loads"], 16)
            sp.dma_start(wr[:], router.rearrange("(c p) n -> p c n", p=P)).then_inc(S["c_loads"], 16)
            sp.dma_start(rb[:], router_bias.to_broadcast([P, E])).then_inc(S["c_loads"], 16)

            def tile(t):
                if not (static(t) and t == TT - 1):
                    sp.wait_ge(S["r1_ok"], t + 1)
                    sp.dma_start(x_res[:], x[ds(t * P + P, P), :]).then_inc(S["x_res_in"], 16)
                sp.wait_ge(S["x1_ok"], t + 1)
                sp.dma_start(rows_dram[ds(t * P, P), 0:D], x1[:]).then_inc(S["x1_stored"], 16)

            def weights_out(t):
                sp.wait_ge(S["wts_ok"], t + 1)
                sp.dma_start(rows_dram[ds(t * P, P), D:ROW_W], wts[:]).then_inc(S["wts_stored"], 16)
            tile(0)
            with sp.Fori(1, TT - 1) as t:
                tile(t)
                weights_out(t - 1)
            tile(TT - 1)
            weights_out(TT - 2)

            def load_expert(par, gate, up, down):
                for k, w in enumerate((gate, up)):
                    sp.dma_start(raw_gu[par][:, k], w.rearrange("(p c) n -> p c n", c=DC)).then_inc(w_raw[par], 16)
                sp.dma_start(raw_dn[par][:], down.rearrange("(p c) n -> p c n", c=FC)).then_inc(w_raw[par], 16)

            sp.wait_ge(S["ot_lo_ok"], TT)
            sp.wait_ge(S["oproj"], TT)
            load_expert(0, ws_gate, ws_up, ws_down)
            load_expert(1, w_gate[0], w_up[0], w_down[0])
            weights_out(TT - 1)
            sp.wait_ge(S["extra_ok"], 2)
            sp.wait_ge(S["listed"], 16 * TT * TOP_K)
            sp.wait_ge(S["c_fill"], 48)
            sp.wait_ge(S["x1_stored"], 16 * TT)
            sp.wait_ge(S["wts_stored"], 16 * TT)
            sp.dma_start(tab[:], tab_dram.rearrange("(p n) o -> p (n o)", p=P)).then_inc(S["tab_in"], 16)

            def next_expert(e, par):
                sp.wait_ge(S["w_lo_ok"], PIECES * e)
                load_expert(par, *(w[ds(e, 1)].rearrange("o k n -> (o k) n") for w in (w_gate, w_up, w_down)))
            next_expert(1, 0)
            with sp.Fori(0, E // 2 - 1) as i:
                next_expert(2 * i + 2, 1)
                next_expert(2 * i + 3, 0)
            sp.wait_ge(S["w_lo_ok"], PIECES * (E + 1))
            sp.dma_start(g2[:], ln2_g.to_broadcast([P, D])).then_inc(S["g2_in"], 16)
            sp.dma_start(b2[:], ln2_b.to_broadcast([P, D])).then_inc(S["g2_in"], 16)
            sp.wait_ge(S["summed"], 1)
            for t in range(TT + 1):
                if t < TT:
                    if t >= 2:
                        sp.wait_ge(S["f_norm"], t - 1)
                        sp.wait_ge(S["f_mv"], t - 1)
                    sp.dma_start(fin[t % 2][:], acc_dram[t * P:(t + 1) * P, :]).then_inc(fin_in[t % 2], 16)
                if t >= 1:
                    sp.wait_ge(S["f_out"], t)
                    sp.dma_start(out[(t - 1) * P:t * P, :], fo[(t - 1) % 2][:]).then_inc(stored[(t - 1) % 2], 16)
            for i in range(2):
                sp.wait_ge(stored[i], 16 * TT // 2)

        @block.gpsimd
        def _(pool):
            g = nc.gpsimd
            g.memset(ident[:], 0.0).then_inc(S["consts"], 1)
            g.memset(mask_qk[:], 0.0).then_inc(S["consts"], 1)
            g.memset(mask_kq[:], 0.0).then_inc(S["consts"], 1)
            g.memset(upto[:], 1.0).then_inc(S["consts"], 1)
            pool.wait_ge(S["consts"], 4)
            g.affine_select(out=ident[:], in_=ident[:], compare_op=ALU.not_equal, fill=1.0, base=0,
                            pattern=[[-1, P]], channel_multiplier=1).then_inc(S["masks"], 1)
            pool.wait_ge(S["masks"], 1)
            g.tensor_copy(identb[:], ident[:]).then_inc(S["masks"], 1)
            g.affine_select(out=mask_qk[:], in_=mask_qk[:], compare_op=ALU.is_ge, fill=NEVER, base=0,
                            pattern=[[-1, P]], channel_multiplier=1).then_inc(S["masks"], 1)
            g.affine_select(out=mask_kq[:], in_=mask_kq[:], compare_op=ALU.is_ge, fill=NEVER, base=0,
                            pattern=[[1, P]], channel_multiplier=-1).then_inc(S["masks"], 1)
            g.affine_select(out=upto[:], in_=upto[:], compare_op=ALU.is_ge, fill=0.0, base=0,
                            pattern=[[1, T]], channel_multiplier=-1).then_inc(S["masks"], 1)
            pool.wait_ge(S["v_ok"], NVC * TT // 2)
            for i in range(2):
                pool.wait_ge(v_stored[i], 16 * NVC * TT // 4)
            pool.wait_ge(S["c_stored"], 32)
            pool.wait_ge(S["v_ps"], NVC * TT // 2)
            n = 0
            for par in range(2):
                for buf in (q_hi, q_lo, k_hi, k_lo):
                    g.memset(buf[par][DH:P, :].bitcast(F32), 0.0).then_inc(S["aug0"], 1)
                    n += 1
                    pool.wait_ge(S["aug0"], n)
                g.memset(va[par][:, :, DH:P], 1.0).then_inc(S["aug0"], 1)
                n += 1
                pool.wait_ge(S["aug0"], n)
                g.memset(q_hi[par][ONE_ROW:ONE_ROW + 1, :].bitcast(F32), 1.0).then_inc(S["aug0"], 1)
                n += 1
                pool.wait_ge(S["aug0"], n)
                g.memset(k_hi[par][MAX_ROW:MAX_ROW + 1, :].bitcast(F32), 1.0).then_inc(S["aug"], 1)
                pool.wait_ge(S["aug"], par + 1)
            g.memset(ones_b[:], 1.0).then_inc(S["c_const"], 1)
            pool.wait_ge(S["c_const"], 1)
            g.affine_select(out=before[:], in_=ones_b[:], compare_op=ALU.is_gt, fill=0.0, base=0,
                            pattern=[[1, P]], channel_multiplier=-1).then_inc(S["c_const"], 1)

            pool.wait_ge(S["normed"], HEADS)
            g.iota(e8[:], pattern=[[TAB_BLOCKS, E]], base=0, channel_multiplier=0, allow_small_or_imprecise_dtypes=True).then_inc(S["c_const"], 1)
            g.iota(tok_all[:], pattern=[[P, TT]], base=0, channel_multiplier=1).then_inc(S["c_const"], 1)
            g.iota(tab0[:], pattern=[[0, TAB]], base=T, channel_multiplier=1).then_inc(S["c_const"], 1)
            g.memset(zeros[:], 0.0).then_inc(S["c_const"], 1)
            g.memset(gtop[:], 3e38).then_inc(S["c_const"], 1)
            g.memset(base[:], 0.0).then_inc(S["c_const"], 1)
            pool.wait_ge(S["c_const"], 8)
            pool.dma_start(tab_dram.rearrange("(p n) o -> p (n o)", p=P), tab0[:]).then_inc(S["c_fill"], 16)
            pool.dma_start(rows_dram[T:ROWS, :], zeros[:]).then_inc(S["c_fill"], 16)
            pool.dma_start(acc_dram[T:ROWS, :], zeros[:, 0:D]).then_inc(S["c_fill"], 16)
            pool.wait_ge(S["c_fill"], 48)

            def list_tokens(t):
                if not (static(t) and t == 0):
                    pool.wait_ge(S["listed"], 16 * TOP_K * t)
                g.tensor_copy(tok[:], tok_all[:, ds(t, 1)]).then_inc(S["tok_ok"], 1)
                pool.wait_ge(S["tok_ok"], t + 1)
                pool.wait_ge(S["dest_ok"], t + 1)
                for k in range(TOP_K):
                    g.indirect_dma_start(out=tab_dram, out_offset=bass.IndirectOffsetOnAxis(ap=dest_i[:, k:k + 1], axis=0),
                                         in_=tok[:], in_offset=None).then_inc(S["listed"], 16)
            list_tokens(0)
            for t in range(1, TT):
                list_tokens(t)

            def wait_routed():
                pool.wait_ge(S["listed"], 16 * TT * TOP_K)
                pool.wait_ge(S["extra_ok"], 2)
                pool.wait_ge(S["x1_stored"], 16 * TT)
                pool.wait_ge(S["wts_stored"], 16 * TT)

            def gather(idx, buf, col, done, n):
                stand(pool)
                g.tensor_copy(idx[:], tab[:, ds(col, 1)]).then_inc(done[0], 1)
                pool.wait_ge(done[0], n)
                stand(pool)
                g.indirect_dma_start(out=buf[:], out_offset=None, in_=rows_dram,
                                     in_offset=bass.IndirectOffsetOnAxis(ap=idx[:, 0:1], axis=0)).then_inc(done[1], 16)

            def add(idx, buf, col, done, n):
                stand(pool)
                g.tensor_copy(idx[:], tab[:, ds(col, 1)]).then_inc(done[0], 1)
                pool.wait_ge(done[0], n)
                stand(pool)
                g.indirect_dma_start(out=acc_dram, out_offset=bass.IndirectOffsetOnAxis(ap=idx[:, 0:1], axis=0),
                                     in_=buf[:], in_offset=None, compute_op=ALU.add).then_inc(done[1], 16)

            wait_routed()
            for b in range(2):
                pool.dma_start(xg[b][:], rows_dram[b * P:(b + 1) * P, :]).then_inc(got[b], 16)
            for b in range(SH):
                pool.wait_ge(S["m_y"], b + 1)
                pool.dma_start(acc_dram[b * P:(b + 1) * P, :], ys[b % 2][:]).then_inc(put[b % 2], 16)
                if b + 2 < SH:
                    pool.dma_start(xg[b % 2][:], rows_dram[(b + 2) * P:(b + 3) * P, :]).then_inc(got[b % 2], 16)
                else:
                    pool.wait_ge(S["tab_in"], 16)
                    gather(gidx[b % 2], xg[b % 2], (b + 2 - SH) * TAB_BLOCKS, (idx_ok["g"], got[b % 2]), b + 3 - SH)
            for b in range(2):
                pool.wait_ge(put[b], 16 * SH // 2)

            def expert(e, par, last=False):
                b = SH + e
                if not last:
                    pool.wait_ge(S["m_xlo"], b + 1)
                    gather(gidx[par], xg[par], (e + 2) * TAB_BLOCKS, (idx_ok["g"], got[par]), e + 3)
                n0 = pool.value_load(extra_at[0:1, ds(e, 1)], min_val=0, max_val=E * TAB_BLOCKS)
                nx = pool.value_load(extra_n[0:1, ds(e, 1)], min_val=0, max_val=TAB_BLOCKS - 1)
                with pool.If(nx > 0):
                    pool.wait_ge(S["x_y"], n0 + 1)
                    gather(gidx[2], xg[2], e * TAB_BLOCKS + 1, (idx_ok["xg"], S["x_in_ok"]), n0 + 1)
                pool.wait_ge(S["m_y"], b + 1)
                if not (static(e) and e == 0):
                    pool.wait_ge(S["m_sent"], 16 * e)
                add(sidx[par], ys[par], e * TAB_BLOCKS, (idx_ok["s"], S["m_sent"]), e + 1)
                with pool.If(nx > 0):
                    pool.wait_ge(S["x_y"], n0 + 2)
                    pool.wait_ge(S["m_sent"], 16 * e + 16)
                    add(sidx[2], ys[2], e * TAB_BLOCKS + 1, (idx_ok["xs"], S["x_sent"]), n0 + 1)
                    pool.wait_ge(S["x_sent"], 16 * n0 + 16)
                    stand(pool)
                    with pool.If(nx > 1):
                        with pool.Fori(1, nx) as k:
                            col, i = e * TAB_BLOCKS + 1 + k, n0 + k
                            gather(gidx[2], xg[2], col, (idx_ok["xg"], S["x_in_ok"]), i + 1)
                            pool.wait_ge(S["x_y"], i + 2)
                            add(sidx[2], ys[2], col, (idx_ok["xs"], S["x_sent"]), i + 1)
                            pool.wait_ge(S["x_sent"], 16 * i + 16)
                            stand(pool)
            for par in range(2):
                expert(par, par)
            with pool.Fori(1, E // 2 - 1) as i:
                for par in range(2):
                    expert(2 * i + par, par)
            for par in range(2):
                expert(E - 2 + par, par, last=True)
            pool.wait_ge(S["m_sent"], 16 * E)
            pool.nop().then_inc(S["summed"], 1)

        @block.tensor
        def _(pe):
            pe.wait_ge(S["masks"], 1)
            for g in range(NXT):
                c, half = g // 2, g % 2
                if c == 0:
                    for t in range(4):
                        pe.wait_ge(x_in[half * 4 + t], 16)
                if g >= 2:
                    pe.wait_ge(S["xt_lo_ok"], g - 1)
                for t in range(4):
                    i = pe.transpose(banks[g % 2][:, t * P:(t + 1) * P], xs[:, half * 4 + t, c * P:(c + 1) * P], ident[:])
                i.then_inc(S["xt_ps"], 1)
            pe.wait_ge(S["xt_lo_ok"], NXT)
            pe.wait_ge(S["wf_ok"], 2)
            for t in range(TT):
                for c in range(DC):
                    i = split_matmul(pe, banks[0][:, t * HEADS:(t + 1) * HEADS], xt_hi[:, c, t * P:(t + 1) * P],
                                     xt_lo[:, c, t * P:(t + 1) * P], wf_hi[:, c], wf_lo[:, c], c == 0, c == DC - 1)
            i.then_inc(S["z_ps"], 1)

            def gate_sums():
                pe.wait_ge(S["gate_ok"], 1)
                pe.wait_ge(S["masks"], 5)
                for half in range(2):
                    last = 4 * half + 3
                    for j in range(last + 1):
                        t0 = max(half * BANK, j * P)
                        i = pe.matmul(q_ps[0:HEADS, t0:(half + 1) * BANK], gate8[:, j, :], upto[:, t0 - j * P:(half + 1) * BANK - j * P],
                                      start=j == 0, stop=j == last, skip_group_check=True)
                i.then_inc(S["c_ps"], 1)

            for n in range(NVC * TT // 2):
                c0, t2 = n // (TT // 2), n % (TT // 2)
                if n == 4:
                    gate_sums()
                if t2 == 0:
                    pe.wait_ge(S["wv_lo_ok"], c0 + 1)
                if n == 0:
                    pe.wait_ge(S["z_ok"], 1)
                if n >= 2:
                    pe.wait_ge(S["v_ok"], n - 1)
                for j in range(2):
                    t = 2 * t2 + j
                    for c in range(DC):
                        i = split_matmul(pe, banks[n % 2][:, j * VC:(j + 1) * VC], xt_hi[:, c, t * P:(t + 1) * P],
                                         xt_lo[:, c, t * P:(t + 1) * P], wv_hi[:, c0 % 2, c], wv_lo[:, c0 % 2, c], c == 0, c == DC - 1)
                i.then_inc(S["v_ps"], 1)

            def project(p):
                pe.wait_ge(S["wqk_lo_ok"], p + 1)
                for j, ps in enumerate((q_ps, k_ps)):
                    for half in range(2):
                        r = slice(half * BANK, (half + 1) * BANK)
                        for c in range(DC):
                            i = split_matmul(pe, ps[:, r], wqk_hi[:, c, j], wqk_lo[:, c, j], xt_hi[:, c, r], xt_lo[:, c, r],
                                             c == 0, c == DC - 1)
                i.then_inc(S["proj"], 1)

            def slot_free(h, n):
                m = n - 2
                if m < 0:
                    if not (isinstance(h, int) and h == 0):
                        pe.wait_ge(S["exped"], h * NK + m + 1)
                elif m < NQ:
                    pe.wait_ge(S["maxed"], h * NQ + m + 1)
                elif m < NQ + NR:
                    pe.wait_ge(S["r_lo"], h * NR + m - NQ + 1)
                else:
                    pe.wait_ge(S["exped"], h * NK + m - NQ - NR + 1)

            def scores_by_query(p, par):
                h = 2 * p + par
                pe.wait_ge(ev_lo[par], p + 1)
                pe.wait_ge(c_in[par], 32 * (p + 1))
                for n, (t, k0, w) in enumerate(BY_QUERY):
                    slot_free(h, n)
                    s = banks[n % 2]
                    diag = k0 + w == (t + 1) * P
                    q, k = slice(t * P, (t + 1) * P), slice(k0, k0 + w)
                    i = split_matmul(pe, s[:, 0:w], q_hi[par][0:MAX_ROW, q], q_lo[par][0:MAX_ROW, q],
                                     k_hi[par][0:MAX_ROW, k], k_lo[par][0:MAX_ROW, k], True, not diag)
                    if diag:
                        i = pe.matmul(s[:, w - P:w], identb[:], mask_qk[:], start=False, stop=True, skip_group_check=True)
                    i.then_inc(S["score"], 1)

            def max_rows(p, par):
                h = 2 * p + par
                pe.wait_ge(S["mx_ok"], h + 1)
                for n in range(NR):
                    slot_free(h, NQ + n)
                    for t in range(4):
                        i = pe.transpose(banks[n % 2][:, t * P:(t + 1) * P], mx[:, 4 * n + t:4 * n + t + 1].to_broadcast([P, P]), ident[:])
                    i.then_inc(S["score"], 1)

            def scores_by_key(p, par):
                h = 2 * p + par
                pe.wait_ge(S["r_lo"], h * NR + NR)
                for n, (t, q0, w, _) in enumerate(BY_KEY):
                    slot_free(h, NQ + NR + n)
                    s = banks[n % 2]
                    diag = q0 == t * P
                    q, k = slice(q0, q0 + w), slice(t * P, (t + 1) * P)
                    i = split_matmul(pe, s[:, 0:w], k_hi[par][0:MAX_ROW + 1, k], k_lo[par][0:MAX_ROW + 1, k],
                                     q_hi[par][0:MAX_ROW + 1, q], q_lo[par][0:MAX_ROW + 1, q], True, not diag)
                    if diag:
                        i = pe.matmul(s[:, 0:P], identb[:], mask_kq[:], start=False, stop=True, skip_group_check=True)
                    i.then_inc(S["score"], 1)

            def weigh_v(p, par, tiles):
                h = 2 * p + par
                if 0 in tiles:
                    pe.wait_ge(S["exped"], h * NK + NK)
                    pe.wait_ge(va_in[par], 16 * (p + 1))
                    if not (isinstance(h, int) and h == 0):
                        pe.wait_ge(S["normed"], h)
                for (t, q0, w, at) in BY_KEY:
                    if t in tiles:
                        i = pe.matmul(out_ps[:, q0:q0 + w], va[par][:, t, :], probs[:, at:at + w], start=t == 0,
                                      stop=t == (3 if q0 < BANK else TT - 1), skip_group_check=True)
                if TT - 1 in tiles:
                    i.then_inc(S["pv"], 1)

            def pair(p, first=False, last=False):
                scores_by_query(p, 0)
                if not first:
                    weigh_v(p - 1, 1, range(TT))
                max_rows(p, 0)
                if not last:
                    pe.wait_ge(ev_lo[1], p + 1)
                    project(p + 1)
                scores_by_key(p, 0)
                scores_by_query(p, 1)
                weigh_v(p, 0, range(0, 4))
                max_rows(p, 1)
                weigh_v(p, 0, range(4, TT))
                scores_by_key(p, 1)

            pe.wait_ge(S["c_lo_ok"], 2)
            project(0)
            pe.wait_ge(S["v_ok"], NVC * TT // 2)
            pe.wait_ge(S["aug"], 2)
            pair(0, first=True)
            with pe.Fori(1, PAIRS - 1) as p:
                pair(p)
            pair(PAIRS - 1, last=True)
            weigh_v(PAIRS - 1, 1, range(TT))

            def out_projection(t):
                pe.wait_ge(S["ot_lo_ok"], t + 1)
                if not (static(t) and t == 0):
                    pe.wait_ge(S["r1_ok"], t)
                else:
                    pe.wait_ge(S["wo_lo_ok"], DC)
                for half in range(2):
                    r = slice(half * BANK, (half + 1) * BANK)
                    for c in range(DC):
                        i = split_matmul(pe, q_ps[:, r], ot_hi[:, c], ot_lo[:, c], wo_hi[:, c, r], wo_lo[:, c, r], c == 0, c == DC - 1)
                i.then_inc(S["oproj"], 1)

            def turn_x1(t):
                pe.wait_ge(S["x1_ok"], t + 1)
                for c in range(DC):
                    i = pe.transpose(k_ps[:, c * P:(c + 1) * P], x1[:, c * P:(c + 1) * P], ident[:])
                i.then_inc(S["x1t_ps"], 1)

            def logits(t):
                pe.wait_ge(S["x1t_lo_ok"], t + 1)
                if static(t) and t == 0:
                    pe.wait_ge(S["wr_ok"], 2)
                else:
                    pe.wait_ge(S["ex_ok"], t)
                for c in range(DC):
                    i = split_matmul(pe, banks[0][:, 0:E], x1t_hi[:, c], x1t_lo[:, c], wr_hi[:, c], wr_lo[:, c], c == 0, c == DC - 1)
                i.then_inc(S["logit_ps"], 1)

            def places(t):
                pe.wait_ge(S["chosen_ok"], t + 1)
                if not (static(t) and t == 0):
                    pe.wait_ge(S["route0"], t)
                pe.matmul(banks[1][:, 0:E], before[:], chosen_b[:], start=True, stop=True, skip_group_check=True)
                pe.matmul(banks[1][:, E:2 * E], ones_b[:], chosen_b[:], start=True, stop=True, skip_group_check=True).then_inc(S["pos_ps"], 1)

            out_projection(0)
            out_projection(1)
            turn_x1(0)
            logits(0)
            for t in range(2, TT):
                out_projection(t)
                turn_x1(t - 1)
                places(t - 2)
                logits(t - 1)
            turn_x1(TT - 1)
            places(TT - 2)
            logits(TT - 1)
            places(TT - 1)

            def turn_rows(src, cs):
                v = strided(src[:, 0:D])
                for c in cs:
                    i = pe.transpose(q_ps[:, c * P:(c + 1) * P], v[:, c], ident[:])
                return i

            def gate_up(s, w, first=None):
                g_hi, g_lo = split[w][0:2]
                for c in range(DC):
                    a, h = (xb_hi[s][:, c], xb_lo[s][:, c]), (g_hi[:, :, c], g_lo[:, :, c])
                    o3 = banks[0][:].rearrange("p (g f) -> p g f", g=2)
                    i = pe.matmul(o3, a[0], h[0], start=c == 0, stop=False, skip_group_check=True)
                    if c == 0 and first is not None:
                        i.then_inc(first, 1)
                    pe.matmul(o3, a[0], h[1], start=False, stop=False, skip_group_check=True)
                    i = pe.matmul(o3, a[1], h[0], start=False, stop=c == DC - 1, skip_group_check=True)
                return i

            def turn_h():
                v = strided(hh[:])
                for c in range(FC):
                    i = pe.transpose(banks[1][:, c * P:(c + 1) * P], v[:, c], ident[:])
                return i

            def down(w):
                d_hi, d_lo = split[w][2:4]
                for half in range(2):
                    r = slice(half * BANK, (half + 1) * BANK)
                    for c in range(FC):
                        i = split_matmul(pe, k_ps[:, r], ht_hi[:, c], ht_lo[:, c], d_hi[:, c, r], d_lo[:, c, r], c == 0, c == FC - 1)
                return i

            def block_main(b, par, w, nset, last=False):
                pe.wait_ge(S["m_xlo"], b + 1)
                pe.wait_ge(S["w_lo_ok"], PIECES * nset)
                gate_up(par, w, S["m_start"]).then_inc(S["m_gu"], 1)
                if not last:
                    pe.wait_ge(got[1 - par], 16 * ((b + 1 - (1 - par)) // 2 + 1) if static(b) else 8 * (b + 1 - (1 - par)) + 16)
                    turn_rows(xg[1 - par], range(0, DC // 2))
                pe.wait_ge(S["m_h"], b + 1)
                turn_h().then_inc(S["m_ht"], 1)
                if not last:
                    turn_rows(xg[1 - par], range(DC // 2, DC)).then_inc(S["m_t"], 1)
                pe.wait_ge(S["m_htlo"], b + 1)
                if not (static(b) and b == 0):
                    pe.wait_ge(S["m_y"], b)

            def further(e, w, last):
                b = SH + e
                stand(pe)
                n0 = pe.value_load(extra_at[0:1, ds(e, 1)], min_val=0, max_val=E * TAB_BLOCKS)
                n1 = pe.value_load(extra_at[0:1, ds(e + 1, 1)], min_val=0, max_val=E * TAB_BLOCKS)
                pe.wait_ge(S["x_y"], n0 + 1)
                down(w).then_inc(S["m_dn"], 1)
                with pe.If(n1 > n0):
                    if not last:
                        pe.wait_ge(S["m_xlo"], b + 2)
                    stand(pe)
                    with pe.Fori(n0, n1) as i:
                        pe.wait_ge(S["x_in_ok"], 16 * i + 16)
                        turn_rows(xg[2], range(DC)).then_inc(S["x_t"], 1)
                        pe.wait_ge(S["x_xlo"], i + 1)
                        gate_up(2, w).then_inc(S["x_gu"], 1)
                        pe.wait_ge(S["x_h"], i + 1)
                        turn_h().then_inc(S["x_ht"], 1)
                        pe.wait_ge(S["x_htlo"], i + 1)
                        pe.wait_ge(S["m_y"], b + 1)
                        pe.wait_ge(S["x_y"], i + 1)
                        down(w).then_inc(S["x_dn"], 1)

            def expert(e, par, last=False):
                block_main(SH + e, par, 1 - par, e + 2, last)
                further(e, 1 - par, last)

            pe.wait_ge(got[0], 16)
            turn_rows(xg[0], range(DC)).then_inc(S["m_t"], 1)
            for b in range(SH):
                block_main(b, b % 2, 0, 1)
                down(0).then_inc(S["m_dn"], 1)
            with pe.Fori(0, E // 2 - 1) as i:
                for par in range(2):
                    expert(2 * i + par, par)
            expert(E - 2, 0)
            expert(E - 1, 1, last=True)

        @block.scalar
        def _(act):
            a = nc.scalar
            act.wait_ge(S["wf_in"], 16)
            a.copy(wf_hi[:], wf[:]).then_inc(S["wf_ok"], 1)
            for g in range(NXT):
                c, half = g // 2, g % 2
                act.wait_ge(S["xt_ps"], g + 1)
                a.copy(xt_hi[:, c, half * BANK:(half + 1) * BANK], banks[g % 2][:]).then_inc(S["xt_hi_ok"], 1)

            def split_wv(n):
                act.wait_ge(wv_in[n % 2], 16 * (n // 2 + 1))
                if n >= 2:
                    act.wait_ge(S["v_ps"], (n - 1) * TT // 2)
                a.copy(wv_hi[:, n % 2], wv[:, n % 2]).then_inc(S["wv_hi_ok"], 1)

            split_wv(0)
            split_wv(1)
            act.wait_ge(S["zabs_ok"], 1)
            a.activation(zexp[:], zabs[:], ACT.Exp, scale=-1.0).then_inc(S["zexp_ok"], 1)
            act.wait_ge(S["zexp_ok"], 2)
            a.activation(zlog[:], zexp[:], ACT.Ln).then_inc(S["zlog_ok"], 1)
            act.wait_ge(S["wqk_in"], 32)
            a.copy(wqk_hi[:], wqk[:]).then_inc(S["wqk_hi_ok"], 1)
            for n in range(NVC * TT // 2):
                if n and n % (TT // 2) == 0 and n // (TT // 2) + 1 < NVC:
                    split_wv(n // (TT // 2) + 1)
                if n == 5:
                    act.wait_ge(S["c_ps"], 1)
                    a.copy(c_hi[:], q_ps[0:HEADS, :]).then_inc(S["c_hi_ok"], 1)
                act.wait_ge(S["v_ps"], n + 1)
                if n >= 2:
                    act.wait_ge(v_stored[n % 2], 16 * (n // 2))
                a.copy(v_out[:, n % 2], banks[n % 2][:]).then_inc(S["v_ok"], 1)

            def take(p, par):
                act.wait_ge(S["proj"], p + 1)
                rows = slice(par * DH, (par + 1) * DH)
                a.copy(q_hi[par][0:DH, :], q_ps[rows, :])
                a.copy(k_hi[par][0:DH, :], k_ps[rows, :]).then_inc(ev_hi[par], 1)

            def max_row(p, par):
                h = 2 * p + par
                for n in range(NR):
                    act.wait_ge(S["score"], h * SLOTS + NQ + n + 1)
                    a.mul(q_hi[par][MAX_ROW:MAX_ROW + 1, n * BANK:(n + 1) * BANK], banks[n % 2][MAX_ROW:MAX_ROW + 1, :],
                          -1.0).then_inc(S["r_hi"], 1)

            def exponentials(p, par):
                h = 2 * p + par
                if not (isinstance(h, int) and h == 0):
                    act.wait_ge(S["pv"], h)
                for n, (_, _, w, at) in enumerate(BY_KEY):
                    act.wait_ge(S["score"], h * SLOTS + NQ + NR + n + 1)
                    a.activation(probs[:, at:at + w], banks[n % 2][:, 0:w], ACT.Exp, scale=SCALE).then_inc(S["exped"], 1)

            def pair(p, first=False, last=False):
                if not first:
                    act.wait_ge(S["score"], 2 * p * SLOTS)
                take(p, 1)
                if not last:
                    act.wait_ge(S["wqk_in"], 32 * (p + 2))
                    act.wait_ge(S["proj"], p + 1)
                    a.copy(wqk_hi[:], wqk[:]).then_inc(S["wqk_hi_ok"], 1)
                max_row(p, 0)
                exponentials(p, 0)
                if not last:
                    act.wait_ge(S["score"], (2 * p + 1) * SLOTS)
                    take(p + 1, 0)
                max_row(p, 1)
                exponentials(p, 1)

            act.wait_ge(S["aug"], 2)
            take(0, 0)
            pair(0, first=True)
            with act.Fori(1, PAIRS - 1) as p:
                pair(p)
            pair(PAIRS - 1, last=True)

            for c in range(DC):
                act.wait_ge(wo_in[c % STAGES], 16 * (c // STAGES + 1))
                a.copy(wo_hi[:, c], wo[:, c % STAGES]).then_inc(S["wo_hi_ok"], 1)
            act.wait_ge(S["normed"], HEADS)

            def heads_hi(t):
                if not (static(t) and t == 0):
                    act.wait_ge(S["oproj"], t)
                a.copy(ot_hi[:], attn[:, :, ds(t * P, P)]).then_inc(S["ot_hi_ok"], 1)

            def x1t_hi_of(t):
                act.wait_ge(S["x1t_ps"], t + 1)
                if not (static(t) and t == 0):
                    act.wait_ge(S["logit_ps"], t)
                a.copy(x1t_hi[:], k_ps[:].rearrange("p (c t) -> p c t", c=DC)).then_inc(S["x1t_hi_ok"], 1)

            def exp_of(t):
                act.wait_ge(S["logit_ps"], t + 1)
                if not (static(t) and t == 0):
                    act.wait_ge(S["chosen_ok"], t)
                a.activation(ex[:], banks[0][:, 0:E], ACT.Exp, scale=-1.0).then_inc(S["ex_ok"], 1)

            def std_of(t):
                act.wait_ge(S["var_ok"], t + 2)
                a.activation(std[:], mv[:, 1:2], ACT.Sqrt, bias=eps[:, 0:1]).then_inc(S["std_ok"], 1)

            heads_hi(0)
            act.wait_ge(S["c_loads"], 64)
            a.copy(wr_hi[:], wr[:]).then_inc(S["wr_ok"], 1)
            heads_hi(1)
            std_of(0)
            for t in range(1, TT):
                if t < TT - 1:
                    heads_hi(t + 1)
                x1t_hi_of(t - 1)
                std_of(t)
                exp_of(t - 1)
            x1t_hi_of(TT - 1)
            exp_of(TT - 1)

            def w_high(w, ks, n):
                for k in ks:
                    raw, hi, _ = piece(w, k)
                    a.copy(hi, raw).then_inc(S["w_hi_ok"], 1)

            act.wait_ge(S["oproj"], TT)
            act.wait_ge(w_raw[0], 48)
            w_high(0, range(PIECES), 0)
            act.wait_ge(S["extra_ok"], 2)
            act.wait_ge(S["listed"], 16 * TT * TOP_K)
            act.wait_ge(S["wts_stored"], 16 * TT)
            act.wait_ge(S["x1_stored"], 16 * TT)
            act.nop().then_inc(S["x_y"], 1)

            def rows_hi(s, wait, n, done):
                act.wait_ge(wait, n)
                a.copy(xb_hi[s][:], q_ps[:].rearrange("p (c t) -> p c t", c=DC)).then_inc(done, 1)

            def silu(wait, n, done):
                act.wait_ge(wait, n)
                a.activation(sg[:], banks[0][:, 0:FF], ACT.Silu).then_inc(done, 1)

            def h_hi(wait, n, done):
                act.wait_ge(wait, n)
                a.copy(ht_hi[:], banks[1][:, 0:FF].rearrange("p (c t) -> p c t", c=FC)).then_inc(done, 1)

            def scale_rows(s, wait, n, done):
                act.wait_ge(wait, n)
                a.activation(ys[s][:], k_ps[:], ACT.Copy, scale=wcol[s][:, 0:1]).then_inc(done, 1)

            def block_main(b, par, w, nxt, last=False):
                if nxt is not None:
                    act.wait_ge(S["m_start"], b + 1)
                    act.wait_ge(w_raw[1 - w], 48 * (nxt // 2 + 1) if static(nxt) else 24 * (nxt - (1 - w)) + 48)
                    w_high(1 - w, range(0, 3), nxt)
                silu(S["m_gu"], b + 1, S["m_sg"])
                h_hi(S["m_ht"], b + 1, S["m_hthi"])
                if not last:
                    rows_hi(1 - par, S["m_t"], b + 2, S["m_xhi"])
                if nxt is not None:
                    w_high(1 - w, range(3, PIECES), nxt)

            def expert(e, par, last=False):
                b = SH + e
                block_main(b, par, 1 - par, None if last else e + 2, last)
                n0 = act.value_load(extra_at[0:1, ds(e, 1)], min_val=0, max_val=E * TAB_BLOCKS)
                n1 = act.value_load(extra_at[0:1, ds(e + 1, 1)], min_val=0, max_val=E * TAB_BLOCKS)
                if static(e) and e < 2:
                    act.wait_ge(put[par], 16 * SH // 2)
                else:
                    act.wait_ge(S["m_sent"], 16 * (e - 1))
                scale_rows(par, S["m_dn"], b + 1, S["m_y"])
                with act.If(n1 > n0):
                    with act.Fori(n0, n1) as i:
                        rows_hi(2, S["x_t"], i + 1, S["x_xhi"])
                        silu(S["x_gu"], i + 1, S["x_sg"])
                        h_hi(S["x_ht"], i + 1, S["x_hthi"])
                        scale_rows(2, S["x_dn"], i + 1, S["x_y"])

            rows_hi(0, S["m_t"], 1, S["m_xhi"])
            for b in range(SH):
                block_main(b, b % 2, 0, 1 if b == SH - 1 else None)
            for e in range(2):
                expert(e, e)
            with act.Fori(1, E // 2 - 1) as i:
                for par in range(2):
                    expert(2 * i + par, par)
            expert(E - 2, 0)
            expert(E - 1, 1, last=True)

            for t in range(TT):
                act.wait_ge(S["f_var"], t + 2)
                a.activation(fstd[t % 2][:], fmv[t % 2][:, 1:2], ACT.Sqrt, bias=feps[:, 0:1]).then_inc(S["f_std"], 1)
                act.wait_ge(S["f_mv"], t + 1)
                if t >= 2:
                    act.wait_ge(S["f_g"], t - 1)
                a.activation(fn[t % 2][:], fin[t % 2][:], ACT.Identity, bias=fnm[t % 2][:, 0:1], scale=frstd[t % 2][:, 0:1]).then_inc(S["f_norm"], 1)

        @block.vector
        def _(dve):
            dve.wait_ge(S["wf_ok"], 1)
            dve.tensor_tensor(wf_lo[:], wf[:], wf_hi[:], ALU.subtract).then_inc(S["wf_ok"], 1)
            for g in range(NXT):
                c, half = g // 2, g % 2
                dve.wait_ge(S["xt_hi_ok"], g + 1)
                r = slice(half * BANK, (half + 1) * BANK)
                dve.tensor_tensor(xt_lo[:, c, r], banks[g % 2][:], xt_hi[:, c, r], ALU.subtract).then_inc(S["xt_lo_ok"], 1)

            def split_wv(n):
                dve.wait_ge(S["wv_hi_ok"], n + 1)
                dve.tensor_tensor(wv_lo[:, n % 2], wv[:, n % 2], wv_hi[:, n % 2], ALU.subtract).then_inc(S["wv_lo_ok"], 1)

            split_wv(0)
            dve.wait_ge(S["z_ps"], 1)
            dve.wait_ge(S["bf_in"], 16)
            dve.tensor_tensor(z[:], banks[0][:, 0:TT * HEADS].rearrange("p (t h) -> p t h", t=TT),
                              bf[:, None, :].to_broadcast([P, TT, HEADS]), ALU.add).then_inc(S["z_ok"], 1)
            dve.wait_ge(S["z_ok"], 1)
            dve.scalar_tensor_tensor(out=zabs[:], in0=z[:], scalar=-1.0, in1=z[:], op0=ALU.mult, op1=ALU.max).then_inc(S["zabs_ok"], 1)
            dve.tensor_scalar(zmin[:], z[:], 0.0, None, ALU.min).then_inc(S["zmin_ok"], 1)
            split_wv(1)
            dve.wait_ge(S["zexp_ok"], 1)
            dve.tensor_scalar(zexp[:], zexp[:], 1.0, None, ALU.add).then_inc(S["zexp_ok"], 1)
            dve.wait_ge(S["zlog_ok"], 1)
            dve.wait_ge(S["zmin_ok"], 1)
            dve.tensor_tensor(z[:], zlog[:], zmin[:], ALU.subtract).then_inc(S["z_ok"], 1)
            dve.wait_ge(S["z_ok"], 2)
            dve.tensor_scalar(gate8[:], z[:], 1.0 / SCALE, None, ALU.mult).then_inc(S["gate_ok"], 1)
            dve.wait_ge(S["wqk_hi_ok"], 1)
            dve.tensor_tensor(wqk_lo[:], wqk[:], wqk_hi[:], ALU.subtract).then_inc(S["wqk_lo_ok"], 1)
            split_wv(2)
            dve.wait_ge(S["c_hi_ok"], 1)
            for half in range(2):
                r = slice(half * BANK, (half + 1) * BANK)
                dve.tensor_tensor(c_lo[:, r], q_ps[0:HEADS, r], c_hi[:, r], ALU.subtract).then_inc(S["c_lo_ok"], 1)
            split_wv(3)
            dve.wait_ge(S["aug"], 2)
            dve.memset(mx2[:], -3e38).then_inc(S["mx20"], 1)
            dve.wait_ge(S["mx20"], 1)

            def take(p, par):
                dve.wait_ge(ev_hi[par], p + 1)
                rows = slice(par * DH, (par + 1) * DH)
                dve.tensor_tensor(q_lo[par][0:DH, :], q_ps[rows, :], q_hi[par][0:DH, :], ALU.subtract)
                dve.tensor_tensor(k_lo[par][0:DH, :], k_ps[rows, :], k_hi[par][0:DH, :], ALU.subtract).then_inc(ev_lo[par], 1)

            def maxima(p, par):
                h = 2 * p + par
                for n, (t, k0, w) in enumerate(BY_QUERY):
                    dve.wait_ge(S["score"], h * SLOTS + n + 1)
                    dve.tensor_reduce(mx2[:, t, k0 // BANK:k0 // BANK + 1], banks[n % 2][:, 0:w], AX_X, ALU.max).then_inc(S["maxed"], 1)
                dve.wait_ge(S["maxed"], h * NQ + NQ)
                dve.tensor_reduce(mx[:], mx2[:], AX_X, ALU.max).then_inc(S["mx_ok"], 1)

            def max_row(p, par):
                h = 2 * p + par
                for n in range(NR):
                    dve.wait_ge(S["r_hi"], h * NR + n + 1)
                    at = slice(n * BANK, (n + 1) * BANK)
                    dve.scalar_tensor_tensor(out=q_lo[par][MAX_ROW:MAX_ROW + 1, at], in0=banks[n % 2][MAX_ROW:MAX_ROW + 1, :], scalar=-1.0,
                                             in1=q_hi[par][MAX_ROW:MAX_ROW + 1, at], op0=ALU.mult, op1=ALU.subtract).then_inc(S["r_lo"], 1)

            def normalise(p, par):
                h = 2 * p + par
                dve.wait_ge(S["pv"], h + 1)
                dve.reciprocal(rec[:], out_ps[DH:P, :]).then_inc(S["rec_ok"], 1)
                dve.wait_ge(S["rec_ok"], h + 1)
                dve.tensor_tensor(attn[par * DH:(par + 1) * DH, bass.ds(p, 1), :], out_ps[0:DH, None, :], rec[:, None, :],
                                  ALU.mult).then_inc(S["normed"], 1)

            def pair(p, first=False, last=False):
                maxima(p, 0)
                take(p, 1)
                if not last:
                    dve.wait_ge(S["wqk_hi_ok"], p + 2)
                    dve.tensor_tensor(wqk_lo[:], wqk[:], wqk_hi[:], ALU.subtract).then_inc(S["wqk_lo_ok"], 1)
                max_row(p, 0)
                if not first:
                    normalise(p - 1, 1)
                maxima(p, 1)
                if not last:
                    take(p + 1, 0)
                max_row(p, 1)
                normalise(p, 0)

            take(0, 0)
            pair(0, first=True)
            with dve.Fori(1, PAIRS - 1) as p:
                pair(p)
            pair(PAIRS - 1, last=True)
            normalise(PAIRS - 1, 1)

            for c in range(DC):
                dve.wait_ge(S["wo_hi_ok"], c + 1)
                dve.tensor_tensor(wo_lo[:, c], wo[:, c % STAGES], wo_hi[:, c], ALU.subtract).then_inc(S["wo_lo_ok"], 1)

            def heads_lo(t):
                dve.wait_ge(S["ot_hi_ok"], t + 1)
                dve.tensor_tensor(ot_lo[:], attn[:, :, ds(t * P, P)], ot_hi[:], ALU.subtract).then_inc(S["ot_lo_ok"], 1)

            def steps(name, base_count):
                n = [0]

                def step(ins):
                    n[0] += 1
                    ins.then_inc(S[name], 1)
                    dve.wait_ge(S[name], base_count + n[0])
                return step, n

            def residual(t):
                dve.wait_ge(S["x_res_in"], 16 * (t + 1))
                dve.wait_ge(S["oproj"], t + 1)
                dve.scalar_tensor_tensor(out=r1[:], in0=x_res[:], scalar=ALPHA, in1=q_ps[:], op0=ALU.mult, op1=ALU.add).then_inc(S["r1_ok"], 1)

            LN_STEPS = 4

            def layer_norm(t):
                dve.wait_ge(S["r1_ok"], t + 1)
                step, n = steps("ln_step", LN_STEPS * t)
                dve.bn_stats(stat[:, 0, :], r1[:, 0:BANK])
                step(dve.bn_stats(stat[:, 1, :], r1[:, BANK:D]))
                dve.bn_aggr(mv[:], stat[:]).then_inc(S["var_ok"], 1)
                dve.wait_ge(S["std_ok"], t + 1)
                step(dve.reciprocal(rstd[:], std[:]))
                step(dve.tensor_scalar(xn[:], r1[:], mv[:, 0:1], rstd[:, 0:1], ALU.subtract, ALU.mult))
                if static(t) and t == 0:
                    dve.wait_ge(S["c_loads"], 64)
                step(dve.tensor_tensor(xg1[:], xn[:], g1[:], ALU.mult))
                assert n[0] == LN_STEPS
                if not (static(t) and t == 0):
                    dve.wait_ge(S["x1_stored"], 16 * t)
                    dve.wait_ge(S["x1t_ps"], t)
                dve.tensor_tensor(x1[:], xg1[:], b1[:], ALU.add).then_inc(S["x1_ok"], 1)

            def x1t_lo_of(t):
                dve.wait_ge(S["x1t_hi_ok"], t + 1)
                dve.tensor_tensor(x1t_lo[:], k_ps[:].rearrange("p (c t) -> p c t", c=DC), x1t_hi[:], ALU.subtract).then_inc(S["x1t_lo_ok"], 1)

            ROUTE_STEPS = 15

            def route(t):
                step, n = steps("route_step", ROUTE_STEPS * t)
                dve.wait_ge(S["ex_ok"], t + 1)
                step(dve.tensor_scalar(ex1[:], ex[:], 1.0, None, ALU.add))
                step(dve.reciprocal(score[:], ex1[:]))
                step(dve.tensor_tensor(sel[:], score[:], rb[:], ALU.add))
                for g in range(GROUPS):
                    i = dve.max(top_g[:, g, :], sel[:, g * GE:(g + 1) * GE])
                step(i)
                step(dve.tensor_tensor(gsum[:], top_g[:, :, 0], top_g[:, :, 1], ALU.add))
                step(dve.max(gsort[:], gsum[:]))
                step(dve.tensor_copy(gtop[:, 0:TOP_GROUPS], gsort[:, 0:TOP_GROUPS]))
                step(dve.match_replace(gleft[:], gtop[:], gsum[:], OUT))
                step(dve.tensor_scalar(gpen[:], gleft[:], OUT / 2, NEVER, ALU.is_ge, ALU.mult))
                step(dve.tensor_tensor(selm[:].rearrange("p (g e) -> p g e", g=GROUPS), sel[:].rearrange("p (g e) -> p g e", g=GROUPS),
                                       gpen[:, :, None].to_broadcast([P, GROUPS, GE]), ALU.add))
                step(dve.max(top8[:], selm[:]))
                step(dve.match_replace(left[:], top8[:], selm[:], OUT))
                step(dve.tensor_scalar(chosen[:], left[:], OUT / 2, None, ALU.is_lt))
                if not (static(t) and t == 0):
                    dve.wait_ge(S["pos_ps"], t)
                dve.tensor_copy(chosen_b[:], chosen[:]).then_inc(S["chosen_ok"], 1)
                step(dve.tensor_tensor_reduce(out=wraw[:], in0=score[:], in1=chosen[:], scale=1.0, scalar=0.0, op0=ALU.mult,
                                              op1=ALU.add, accum_out=wsum[:]))
                step(dve.reciprocal(wrec[:], wsum[:]))
                assert n[0] == ROUTE_STEPS
                if not (static(t) and t == 0):
                    dve.wait_ge(S["wts_stored"], 16 * t)
                dve.tensor_scalar(wts[:], wraw[:], wrec[:, 0:1], ROUTED_SCALE, ALU.mult, ALU.mult).then_inc(S["wts_ok"], 1)

            POS_STEPS = 7

            def place(t):
                step, n = steps("pos_step", POS_STEPS * t)
                dve.wait_ge(S["pos_ps"], t + 1)
                step(dve.tensor_tensor(pos[:], banks[1][:, 0:E], base[:], ALU.add))
                ins = dve.tensor_tensor(base[:], base[:], banks[1][:, E:2 * E], ALU.add)
                ins.then_inc(S["route0"], 1)
                dve.wait_ge(S["route0"], t + 1)
                dve.tensor_scalar(pos_m[:], pos[:], P - 1, None, ALU.bitwise_and)
                step(dve.tensor_scalar(pos_q[:], pos[:], P.bit_length() - 1, None, ALU.logical_shift_right))
                step(dve.tensor_tensor(pos_b[:], pos_q[:], e8[:], ALU.add))
                step(dve.scalar_tensor_tensor(out=dest[:], in0=pos_m[:], scalar=float(TAB), in1=pos_b[:], op0=ALU.mult, op1=ALU.add))
                step(dve.tensor_scalar(dest[:], dest[:], 1.0, None, ALU.add))
                step(dve.tensor_tensor(dest1[:], dest[:], chosen[:], ALU.mult))
                step(dve.max(dest8[:], dest1[:]))
                assert n[0] == POS_STEPS
                if not (static(t) and t == 0):
                    dve.wait_ge(S["listed"], 16 * TOP_K * t)
                dve.tensor_scalar(dest_i[:], dest8[:], -1.0, None, ALU.add).then_inc(S["dest_ok"], 1)

            dve.wait_ge(S["c_const"], 8)
            dve.memset(eps[:], LN_EPS).then_inc(S["var_ok"], 1)
            heads_lo(0)
            dve.wait_ge(S["c_loads"], 64)
            dve.wait_ge(S["wr_ok"], 1)
            dve.tensor_tensor(wr_lo[:], wr[:], wr_hi[:], ALU.subtract).then_inc(S["wr_ok"], 1)
            residual(0)
            heads_lo(1)
            layer_norm(0)
            residual(1)
            heads_lo(2)
            x1t_lo_of(0)
            layer_norm(1)
            route(0)
            for t in range(2, TT - 1):
                residual(t)
                heads_lo(t + 1)
                x1t_lo_of(t - 1)
                place(t - 2)
                layer_norm(t)
                route(t - 1)
            t = TT - 1
            residual(t)
            x1t_lo_of(t - 1)
            place(t - 2)
            layer_norm(t)
            route(t - 1)
            x1t_lo_of(t)
            place(t - 1)
            route(t)
            place(t)

            step, n = steps("pos_step", POS_STEPS * TT)
            u, v = nblk[0], nblk[1]
            step(dve.tensor_scalar(nblk_i[0][:], base[0:1, :], float(P - 1), None, ALU.add))
            step(dve.tensor_scalar(nblk_i[1][:], nblk_i[0][:], P.bit_length() - 1, None, ALU.logical_shift_right))
            step(dve.tensor_scalar(u[:], nblk_i[1][:], -1.0, 0.0, ALU.add, ALU.max))
            dve.tensor_copy(extra_n[:], u[:]).then_inc(S["extra_ok"], 1)
            shift = 1
            while shift < E:
                step(dve.tensor_copy(v[:, 0:shift], u[:, 0:shift]))
                step(dve.tensor_tensor(v[:, shift:E], u[:, shift:E], u[:, 0:E - shift], ALU.add))
                u, v = v, u
                shift *= 2
            step(dve.memset(extra_at[:], 0))
            dve.tensor_copy(extra_at[:, 1:E + 1], u[:]).then_inc(S["extra_ok"], 1)
            dve.wait_ge(S["extra_ok"], 2)

            def w_low(w, ks, n):
                for k in ks:
                    raw, hi, lo = piece(w, k)
                    dve.wait_ge(S["w_hi_ok"], PIECES * n + k + 1)
                    dve.tensor_tensor(lo, raw, hi, ALU.subtract).then_inc(S["w_lo_ok"], 1)

            w_low(0, range(PIECES), 0)
            dve.wait_ge(S["listed"], 16 * TT * TOP_K)
            dve.wait_ge(S["wts_stored"], 16 * TT)
            dve.wait_ge(S["x1_stored"], 16 * TT)

            def rows_lo(s, wait, n, done):
                dve.wait_ge(wait, n)
                dve.tensor_tensor(xb_lo[s][:], q_ps[:].rearrange("p (c t) -> p c t", c=DC), xb_hi[s][:], ALU.subtract).then_inc(done, 1)

            def h_of(wait, n, done):
                dve.wait_ge(wait, n)
                dve.tensor_tensor(hh[:], sg[:], banks[0][:, FF:2 * FF], ALU.mult).then_inc(done, 1)

            def h_lo(wait, n, done):
                dve.wait_ge(wait, n)
                dve.tensor_tensor(ht_lo[:], banks[1][:, 0:FF].rearrange("p (c t) -> p c t", c=FC), ht_hi[:], ALU.subtract).then_inc(done, 1)

            def block_main(b, par, w, nxt, e_next=None, last=False):
                if nxt is not None:
                    w_low(1 - w, range(0, 3), nxt)
                h_of(S["m_sg"], b + 1, S["m_h"])
                h_lo(S["m_hthi"], b + 1, S["m_htlo"])
                if not last:
                    if e_next is not None:
                        dve.wait_ge(S["m_y"], b)
                        dve.wait_ge(S["m_t"], b + 2)
                        dve.tensor_copy(wcol[1 - par][:], xg[1 - par][:, ds(D + e_next, 1)])
                    rows_lo(1 - par, S["m_xhi"], b + 2, S["m_xlo"])
                if nxt is not None:
                    w_low(1 - w, range(3, PIECES), nxt)

            def expert(e, par, last=False):
                b = SH + e
                block_main(b, par, 1 - par, None if last else e + 2, e + 1, last)
                n0 = dve.value_load(extra_at[0:1, ds(e, 1)], min_val=0, max_val=E * TAB_BLOCKS)
                n1 = dve.value_load(extra_at[0:1, ds(e + 1, 1)], min_val=0, max_val=E * TAB_BLOCKS)
                with dve.If(n1 > n0):
                    with dve.Fori(n0, n1) as i:
                        dve.wait_ge(S["x_t"], i + 1)
                        dve.wait_ge(S["x_y"], i + 1)
                        dve.tensor_copy(wcol[2][:], xg[2][:, ds(D + e, 1)])
                        rows_lo(2, S["x_xhi"], i + 1, S["x_xlo"])
                        h_of(S["x_sg"], i + 1, S["x_h"])
                        h_lo(S["x_hthi"], i + 1, S["x_htlo"])

            rows_lo(0, S["m_xhi"], 1, S["m_xlo"])
            for b in range(SH):
                block_main(b, b % 2, 0, 1 if b == SH - 1 else None, 0 if b == SH - 1 else None)
                dve.wait_ge(S["m_dn"], b + 1)
                if b >= 2:
                    dve.wait_ge(put[b % 2], 16 * (b // 2))
                dve.scalar_tensor_tensor(out=ys[b % 2][:], in0=xg[b % 2][:, 0:D], scalar=ALPHA, in1=k_ps[:], op0=ALU.mult,
                                         op1=ALU.add).then_inc(S["m_y"], 1)
            with dve.Fori(0, E // 2 - 1) as i:
                for par in range(2):
                    expert(2 * i + par, par)
            expert(E - 2, 0)
            expert(E - 1, 1, last=True)

            F_STEPS = 3
            step, n = steps("f_step", 0)
            dve.wait_ge(S["g2_in"], 32)
            dve.memset(feps[:], LN_EPS).then_inc(S["f_var"], 1)
            for t in range(TT + 1):
                if t < TT:
                    i = t % 2
                    dve.wait_ge(fin_in[i], 16 * (t // 2 + 1))
                    dve.bn_stats(fstat[i][:, 0, :], fin[i][:, 0:BANK])
                    step(dve.bn_stats(fstat[i][:, 1, :], fin[i][:, BANK:D]))
                    dve.bn_aggr(fmv[i][:], fstat[i][:]).then_inc(S["f_var"], 1)
                    if t >= 2:
                        dve.wait_ge(S["f_norm"], t - 1)
                    dve.wait_ge(S["f_std"], t + 1)
                    step(dve.reciprocal(frstd[i][:], fstd[i][:]))
                    dve.scalar_tensor_tensor(out=fnm[i][:], in0=fmv[i][:, 0:1], scalar=-1.0, in1=frstd[i][:], op0=ALU.mult,
                                             op1=ALU.mult).then_inc(S["f_mv"], 1)
                if t >= 1:
                    i = (t - 1) % 2
                    dve.wait_ge(S["f_norm"], t)
                    dve.tensor_tensor(fn[i][:], fn[i][:], g2[:], ALU.mult).then_inc(S["f_g"], 1)
                    dve.wait_ge(S["f_g"], t)
                    if t >= 3:
                        dve.wait_ge(stored[i], 16 * ((t - 1) // 2))
                    dve.tensor_tensor(fo[i][:], fn[i][:], b2[:], ALU.add).then_inc(S["f_out"], 1)


_INS = ["x", "fox_w_in", "fox_b_f", "fox_w_out", "ln1_g", "ln1_b", "moe_router", "moe_router_bias", "moe_w_gate", "moe_w_up",
        "moe_w_down", "moe_ws_gate", "moe_ws_up", "moe_ws_down", "ln2_g", "ln2_b"]
_ROWS = {"fox_b_f", "ln1_g", "ln1_b", "moe_router_bias", "ln2_g", "ln2_b"}


def kernel(**inputs):
    import numpy as _np
    import concourse.bacc as _bacc
    from concourse import mybir as _mybir
    from concourse.bass_utils import run_bass_kernel_spmd as _run

    nc = _bacc.Bacc("TRN2", target_bir_lowering=False, num_devices=1)
    arrays, args = {}, []
    for name in _INS:
        a = _np.ascontiguousarray(inputs[name])
        if name not in _ROWS:
            a = a[0]
        arrays[f"in_{name}_dram"] = a
        args.append(nc.dram_tensor(f"in_{name}_dram", a.shape, _mybir.dt.from_np(a.dtype), kind="ExternalInput").ap())
    args.append(nc.dram_tensor("out_dram", (T, D), F32, kind="ExternalOutput").ap())
    build(nc, *args)
    r = _run(nc, [arrays], core_ids=[0])
    return r.results[0]["out_dram"].reshape(1, T, D)
```

```python
from contextlib import ExitStack

import concourse.bass as bass
from concourse import mybir

P = 128
BANK = 512
ALU = mybir.AluOpType
ACT = mybir.ActivationFunctionType
F32 = mybir.dt.float32
F32R = mybir.dt.float32r
BF16 = mybir.dt.bfloat16
AX_X = mybir.AxisListType.X
NEVER = -1e30

T, D, HEADS, DH = 1024, 1024, 16, 64
TT = T // P
DC = D // P
PAIRS = HEADS // 2
VC = 256
NVC = D // VC
ONE_ROW, MAX_ROW = 64, 96
SCALE = DH ** -0.5

BY_QUERY = [(t, k0, min(BANK, (t + 1) * P - k0)) for t in range(TT) for k0 in range(0, (t + 1) * P, BANK)]
BY_KEY = []
for _t in range(TT):
    for _q0, _q1 in ((_t * P, BANK), (max(_t * P, BANK), T)):
        if _q0 < _q1:
            BY_KEY.append((_t, _q0, _q1 - _q0, sum(b[2] for b in BY_KEY)))
PROBS = sum(b[2] for b in BY_KEY)
NQ, NR, NK = len(BY_QUERY), 2, len(BY_KEY)
SLOTS = NQ + NR + NK


ALPHA = 2.0 ** 0.25
LN_EPS = 1e-5
E, GROUPS, TOP_GROUPS, TOP_K, FF = 64, 8, 4, 8, 256
GE = E // GROUPS
ROUTED_SCALE = 2.5
FC = FF // P
TAB_BLOCKS = T // P
TAB = E * TAB_BLOCKS
ROWS = T + P
ROW_W = D + E
STAGES = 6
OUT = -3e38
I32 = mybir.dt.int32
U32 = mybir.dt.uint32


def split_matmul(pe, out, w_hi, w_lo, m_hi, m_lo, start, stop):
    pe.matmul(out, w_hi, m_hi, start=start, stop=False, skip_group_check=True)
    pe.matmul(out, w_hi, m_lo, start=False, stop=False, skip_group_check=True)
    return pe.matmul(out, w_lo, m_hi, start=False, stop=stop, skip_group_check=True)


def build(nc, x, w_in, b_f, w_out, ln1_g, ln1_b, router, router_bias, w_gate, w_up, w_down, ws_gate, ws_up,
          ws_down, ln2_g, ln2_b, out):
    with ExitStack() as ctx:
        def sem(n):
            return ctx.enter_context(nc.semaphore(n))

        def sb(n, s, d=F32, c=ctx):
            return c.enter_context(nc.sbuf_tensor(n, s, d))

        banks = [ctx.enter_context(nc.psum_tensor(f"bank{i}", [P, BANK], F32)) for i in range(2)]
        out_ps = ctx.enter_context(nc.psum_tensor("out_ps", [P, T], F32))
        q_ps = ctx.enter_context(nc.psum_tensor("q_ps", [P, T], F32))
        k_ps = ctx.enter_context(nc.psum_tensor("k_ps", [P, T], F32))

        v_dram = nc.dram_tensor("v_scratch", (T, D), F32, kind="Internal").ap()
        c_dram = nc.dram_tensor("c_scratch", (2, HEADS, T), F32, kind="Internal").ap()

        rows_dram = nc.dram_tensor("rows_scratch", (ROWS, ROW_W), F32, kind="Internal").ap()
        sums = [nc.dram_tensor(f"sums_scratch{i}", (ROWS, D), F32, kind="Internal").ap() for i in range(3)]
        tab_dram = nc.dram_tensor("tab_scratch", (P * TAB, 1), I32, kind="Internal").ap()

        ident = sb("ident", [P, P])
        identb = sb("identb", [P, P], BF16)
        mask_qk = sb("mask_qk", [P, P], BF16)
        mask_kq = sb("mask_kq", [P, P], BF16)
        ones_b = sb("ones_b", [P, P], BF16)
        before = sb("before", [P, P], BF16)
        further = sb("further", [1, E], I32)
        earlier = sb("earlier", [1, E + 1], I32)
        with ExitStack() as early:
            attn = sb("xs", [P, PAIRS, T], c=early)
            xs = attn
            with ExitStack() as x1s:
                xt_hi = sb("xt_hi", [P, DC, T], F32R, c=x1s)
                xt_lo = sb("xt_lo", [P, DC, T], F32R, c=x1s)
                wqk = sb("wqk", [P, DC, 2, P], c=x1s)
                wqk_hi = sb("wqk_hi", [P, DC, 2, P], F32R, c=x1s)
                wqk_lo = sb("wqk_lo", [P, DC, 2, P], F32R, c=x1s)
                with ExitStack() as a:
                    wv = sb("wv", [P, 2, DC, VC], c=a)
                    wv_hi = sb("wv_hi", [P, 2, DC, VC], F32R, c=a)
                    wv_lo = sb("wv_lo", [P, 2, DC, VC], F32R, c=a)
                    v_out = sb("v_out", [P, 2, 2, VC], c=a)
                    wf = sb("wf", [P, DC, HEADS], c=a)
                    wf_hi = sb("wf_hi", [P, DC, HEADS], F32R, c=a)
                    wf_lo = sb("wf_lo", [P, DC, HEADS], F32R, c=a)
                    bf = sb("bf", [P, HEADS], c=a)
                    z = sb("z", [P, TT, HEADS], c=a)
                    zabs = sb("zabs", [P, TT, HEADS], c=a)
                    zexp = sb("zexp", [P, TT, HEADS], c=a)
                    zlog = sb("zlog", [P, TT, HEADS], c=a)
                    zmin = sb("zmin", [P, TT, HEADS], c=a)
                    gate8 = sb("gate8", [P, TT, HEADS], c=a)
                    upto = sb("upto", [P, T], c=a)
                    c_hi = sb("c_hi", [HEADS, T], F32R, c=a)
                    c_lo = sb("c_lo", [HEADS, T], F32R, c=a)
                with ExitStack() as b:
                    q_hi = [sb(f"q_hi{i}", [P, T], F32R, c=b) for i in range(2)]
                    q_lo = [sb(f"q_lo{i}", [P, T], F32R, c=b) for i in range(2)]
                    k_hi = [sb(f"k_hi{i}", [P, T], F32R, c=b) for i in range(2)]
                    k_lo = [sb(f"k_lo{i}", [P, T], F32R, c=b) for i in range(2)]
                    va = [sb(f"va{i}", [P, TT, P], c=b) for i in range(2)]
                    probs = sb("probs", [P, PROBS], c=b)
                    mx2 = sb("mx2", [P, TT, 2], c=b)
                    mx = sb("mx", [P, TT], c=b)
                    rec = sb("rec", [DH, T], c=b)
            with ExitStack() as d:
                wo_hi = sb("wo_hi", [P, DC, D], F32R, c=d)
                wo_lo = sb("wo_lo", [P, DC, D], F32R, c=d)
                wo = sb("wo", [P, STAGES, D], c=d)
                ot_hi = sb("ot_hi", [P, DC, P], F32R, c=d)
                ot_lo = sb("ot_lo", [P, DC, P], F32R, c=d)
                x_res = sb("x_res", [P, D], c=d)
                r1 = sb("r1", [P, D], c=d)
                xn = sb("xn", [P, D], c=d)
                xg1 = sb("xg1", [P, D], c=d)
                x1 = sb("x1", [P, D], c=d)
                ax = sb("ax", [P, D], c=d)
                x1t_hi = sb("x1t_hi", [P, DC, P], F32R, c=d)
                x1t_lo = sb("x1t_lo", [P, DC, P], F32R, c=d)
                g1 = sb("g1", [P, D], c=d)
                b1 = sb("b1", [P, D], c=d)
                wr = sb("wr", [P, DC, E], c=d)
                wr_hi = sb("wr_hi", [P, DC, E], F32R, c=d)
                wr_lo = sb("wr_lo", [P, DC, E], F32R, c=d)
                rb = sb("rb", [P, E], c=d)
                stat = sb("stat", [P, 2, 6], c=d)
                mv = sb("mv", [P, 2], c=d)
                rstd = sb("rstd", [P, 1], c=d)
                std = sb("std", [P, 1], c=d)
                eps = sb("eps", [P, 1], c=d)
                ex = sb("ex", [P, E], c=d)
                ex1 = sb("ex1", [P, E], c=d)
                score = sb("score_e", [P, E], c=d)
                sel = sb("sel", [P, E], c=d)
                top_g = sb("top_g", [P, GROUPS, 8], c=d)
                gsum = sb("gsum", [P, GROUPS], c=d)
                gsort = sb("gsort", [P, GROUPS], c=d)
                gtop = sb("gtop", [P, GROUPS], c=d)
                gleft = sb("gleft", [P, GROUPS], c=d)
                gpen = sb("gpen", [P, GROUPS], c=d)
                selm = sb("selm", [P, E], c=d)
                top8 = sb("top8", [P, 8], c=d)
                left = sb("left", [P, E], c=d)
                chosen = sb("chosen", [P, E], c=d)
                chosen_b = sb("chosen_b", [P, E], BF16, c=d)
                wraw = sb("wraw", [P, E], c=d)
                wsum = sb("wsum", [P, 1], c=d)
                wrec = sb("wrec", [P, 1], c=d)
                wts = sb("wts", [P, E], c=d)
                base = sb("base", [P, E], c=d)
                pos = sb("pos", [P, E], I32, c=d)
                pos_m = sb("pos_m", [P, E], I32, c=d)
                pos_q = sb("pos_q", [P, E], I32, c=d)
                pos_b = sb("pos_b", [P, E], c=d)
                dest = sb("dest", [P, E], c=d)
                dest1 = sb("dest1", [P, E], c=d)
                dest8 = sb("dest8", [P, 8], c=d)
                dest_i = sb("dest_i", [P, 8], I32, c=d)
                e8 = sb("e8", [P, E], c=d)
                tok_all = sb("tok_all", [P, TT], I32, c=d)
                tok = sb("tok", [P, 1], I32, c=d)
                tab0 = sb("tab0", [P, TAB], I32, c=d)
                zeros = sb("zeros", [P, ROW_W], c=d)
                nblk = [sb(f"nblk{i}", [1, E], c=d) for i in range(2)]
                nblk_i = [sb(f"nblk_i{i}", [1, E], I32, c=d) for i in range(2)]
        with ExitStack() as m:
            raw_gu = [sb(f"raw_gu{i}", [P, 2, DC, FF], c=m) for i in range(2)]
            raw_dn = [sb(f"raw_dn{i}", [P, FC, D], c=m) for i in range(2)]
            split = []
            for i in range(2):
                split.append((sb(f"gu_hi{i}", [P, 2, DC, FF], F32R, c=m), sb(f"gu_lo{i}", [P, 2, DC, FF], F32R, c=m),
                              sb(f"dn_hi{i}", [P, FC, D], F32R, c=m), sb(f"dn_lo{i}", [P, FC, D], F32R, c=m)))
            xg = [sb(f"x_rows{i}", [P, ROW_W], c=m) for i in range(3)]
            xb_hi = [sb(f"xb_hi{i}", [P, DC, P], F32R, c=m) for i in range(3)]
            xb_lo = [sb(f"xb_lo{i}", [P, DC, P], F32R, c=m) for i in range(3)]
            ys = [sb(f"ys{i}", [P, D], c=m) for i in range(3)]
            sg = sb("sg", [P, FF], c=m)
            hh = sb("hh", [P, FF], c=m)
            ht_hi = sb("ht_hi", [P, FC, P], F32R, c=m)
            ht_lo = sb("ht_lo", [P, FC, P], F32R, c=m)
            wcol = [sb(f"wcol{i}", [P, 1], c=m) for i in range(3)]
            tab = sb("tab", [P, TAB], I32, c=m)
            gidx = [sb(f"gidx{i}", [P, 1], I32, c=m) for i in range(3)]
            sidx = [sb(f"sidx{i}", [P, 1], I32, c=m) for i in range(3)]
        with ExitStack() as f:
            fin = [sb(f"fin{j}", [P, TT, D], c=f) for j in range(3)]
            g2 = sb("g2", [P, D], c=f)
            b2 = sb("b2", [P, D], c=f)
            fstat = [sb(f"fstat{i}", [P, 2, 6], c=f) for i in range(2)]
            fmv = [sb(f"fmv{i}", [P, 2], c=f) for i in range(2)]
            feps = sb("feps", [P, 1], c=f)
            fstd = [sb(f"fstd{i}", [P, 1], c=f) for i in range(2)]
            frstd = [sb(f"frstd{i}", [P, 1], c=f) for i in range(2)]
            fnm = [sb(f"fnm{i}", [P, 1], c=f) for i in range(2)]

        SH = TT
        G_PIECES, D_PIECES = 4, 2
        S = {}
        for n in ("consts masks xt_ps xt_hi_ok xt_lo_ok wf_in wf_ok bf_in z_ps z_ok zabs_ok zexp_ok zlog_ok zmin_ok gate_ok"
                  " c_ps c_hi_ok c_lo_ok c_stored wv_hi_ok wv_lo_ok v_ps v_ok aug aug0 mx20"
                  " wqk_in wqk_hi_ok wqk_lo_ok proj score maxed mx_ok r_hi r_lo exped pv rec_ok normed"
                  " wo_hi_ok wo_lo_ok c_loads wr_ok ot_hi_ok ot_lo_ok oproj r1_ok ln_step x1_ok x_res_in x1_stored wts_stored"
                  " x1t_ps x1t_hi_ok x1t_lo_ok logit_ps ex_ok route_step chosen_ok wts_ok pos_ps pos_step dest_ok c_const c_fill"
                  " tok_ok listed route0 extra_ok"
                  " g_hi_ok g_lo_ok d_hi_ok d_lo_ok tab_in started gated turned rows_hi_ok rows_lo_ok silu_ok h_ok ht_ps ht_hi_ok"
                  " ht_lo_ok downed scaled w_ok x_in x_turned x_rows_hi_ok x_rows_lo_ok x_w_ok ax_ok ax_stored summed"
                  " stands g2_in std_ok var_ok f_part f_sum f_var f_std f_step f_mv f_norm f_g f_out").split():
            S[n] = sem(n)
        tile_in = [sem(f"tile_in{t}") for t in range(TT)]
        wv_in = [sem(f"wv_in{i}") for i in range(2)]
        v_stored = [sem(f"v_stored{i}") for i in range(2)]
        c_in = [sem(f"c_in{i}") for i in range(2)]
        va_in = [sem(f"va_in{i}") for i in range(2)]
        ev_hi = [sem(f"ev_hi{i}") for i in range(2)]
        ev_lo = [sem(f"ev_lo{i}") for i in range(2)]
        wo_in = [sem(f"wo_in{i}") for i in range(STAGES)]
        g_raw = [[sem(f"g_raw{i}_{k}") for k in range(G_PIECES)] for i in range(2)]
        d_raw = [sem(f"d_raw{i}") for i in range(2)]
        got = [sem(f"got{i}") for i in range(2)]
        sent = [sem(f"sent{i}") for i in range(3)]
        SENT_0 = (16 * SH // 2, 16 * SH // 2, 16 * ROWS // P)
        stored = sem("stored")

        w_rows = w_in.rearrange("(c p) n -> p c n", p=P)
        v_rows = v_dram.rearrange("(t p) n -> p t n", p=P)
        NXT = DC * 2
        idx_ok = [sem(f"gidx_ok{i}") for i in range(3)]
        S["sidx_ok"] = sem("sidx_ok")

        def load_wqk(sp, p):
            for j in range(2):
                sp.dma_start(wqk[:, :, j, :], w_rows[:, :, bass.ds(j * D + p * P, P)]).then_inc(S["wqk_in"], 16)

        def load_c(sp, p, par):
            for j, k in enumerate((k_hi[par], k_lo[par])):
                sp.dma_start(k[ONE_ROW:ONE_ROW + 1, :].bitcast(F32), c_dram[j, bass.ds(2 * p + par, 1), :]).then_inc(c_in[par], 16)

        def load_v(sp, p, par):
            sp.dma_start(va[par][:, :, 0:DH], v_rows[:, :, bass.ds((2 * p + par) * DH, DH)]).then_inc(va_in[par], 16)

        ds = bass.ds

        def g_piece(w, k):
            return tuple(a[:, k // 2, (k % 2) * 4:(k % 2) * 4 + 4, :] for a in (raw_gu[w], split[w][0], split[w][1]))

        def d_piece(w, k):
            return tuple(a[:, k, :] for a in (raw_dn[w], split[w][2], split[w][3]))

        def strided(a):
            return a.rearrange("p (k c) -> p c k", k=P)

        def static(e):
            return isinstance(e, int)

        def stand(eng):
            eng.sem_inc(S["stands"], 1)

        block = ctx.enter_context(nc.Block())

        @block.sync
        def _(sp):
            for t in range(TT):
                sp.dma_start(xs[:, t, :], x[t * P:(t + 1) * P, :]).then_inc(tile_in[t], 16)
            sp.dma_start(wf[:], w_rows[:, :, 3 * D:3 * D + HEADS]).then_inc(S["wf_in"], 16)
            sp.dma_start(bf[:], b_f.to_broadcast([P, HEADS])).then_inc(S["bf_in"], 16)
            for n in range(NVC):
                if n >= 2:
                    sp.wait_ge(S["wv_lo_ok"], n - 1)
                sp.dma_start(wv[:, n % 2], w_rows[:, :, 2 * D + n * VC:2 * D + (n + 1) * VC]).then_inc(wv_in[n % 2], 16)
            load_wqk(sp, 0)
            for n in range(NVC * TT // 2):
                sp.wait_ge(S["v_ok"], n + 1)
                c, t = n // (TT // 2), n % (TT // 2)
                sp.dma_start(v_rows[:, 2 * t:2 * t + 2, c * VC:(c + 1) * VC], v_out[:, n % 2]).then_inc(v_stored[n % 2], 16)
            sp.wait_ge(S["c_lo_ok"], 2)
            sp.dma_start(c_dram[0], c_hi[:].bitcast(F32)).then_inc(S["c_stored"], 16)
            sp.dma_start(c_dram[1], c_lo[:].bitcast(F32)).then_inc(S["c_stored"], 16)
            sp.wait_ge(S["c_stored"], 32)
            for i in range(2):
                sp.wait_ge(v_stored[i], 16 * NVC * TT // 4)
            sp.wait_ge(S["wqk_lo_ok"], 1)
            load_wqk(sp, 1)
            sp.wait_ge(S["aug"], 2)
            for par in range(2):
                load_c(sp, 0, par)
                load_v(sp, 0, par)

            def pair(p):
                sp.wait_ge(S["score"], SLOTS * (2 * p + 1))
                load_c(sp, p + 1, 0)
                sp.wait_ge(S["pv"], 2 * p + 1)
                load_v(sp, p + 1, 0)
                sp.wait_ge(S["score"], SLOTS * (2 * p + 2))
                load_c(sp, p + 1, 1)
                sp.wait_ge(S["pv"], 2 * p + 2)
                load_v(sp, p + 1, 1)
            with sp.Fori(0, PAIRS - 2) as p:
                sp.wait_ge(S["wqk_lo_ok"], p + 2)
                load_wqk(sp, p + 2)
                pair(p)
            pair(PAIRS - 2)

            sp.wait_ge(S["proj"], PAIRS)
            for c in range(DC):
                if c >= STAGES:
                    sp.wait_ge(S["wo_lo_ok"], c - STAGES + 1)
                sp.dma_start(wo[:, c % STAGES], w_out[c * P:(c + 1) * P, :]).then_inc(wo_in[c % STAGES], 16)
            sp.wait_ge(S["normed"], HEADS)
            sp.dma_start(x_res[:], x[0:P, :]).then_inc(S["x_res_in"], 16)
            sp.dma_start(g1[:], ln1_g.to_broadcast([P, D])).then_inc(S["c_loads"], 16)
            sp.dma_start(b1[:], ln1_b.to_broadcast([P, D])).then_inc(S["c_loads"], 16)
            sp.dma_start(wr[:], router.rearrange("(c p) n -> p c n", p=P)).then_inc(S["c_loads"], 16)
            sp.dma_start(rb[:], router_bias.to_broadcast([P, E])).then_inc(S["c_loads"], 16)

            def tile(t):
                if not (static(t) and t == TT - 1):
                    sp.wait_ge(S["r1_ok"], t + 1)
                    sp.dma_start(x_res[:], x[ds(t * P + P, P), :]).then_inc(S["x_res_in"], 16)
                sp.wait_ge(S["x1_ok"], t + 1)
                sp.dma_start(rows_dram[ds(t * P, P), 0:D], x1[:]).then_inc(S["x1_stored"], 16)
                sp.wait_ge(S["ax_ok"], t + 1)
                sp.dma_start(sums[0][ds(t * P, P), :], ax[:]).then_inc(S["ax_stored"], 16)

            def weights_out(t):
                sp.wait_ge(S["wts_ok"], t + 1)
                sp.dma_start(rows_dram[ds(t * P, P), D:ROW_W], wts[:]).then_inc(S["wts_stored"], 16)
            tile(0)
            with sp.Fori(1, TT - 1) as t:
                tile(t)
                weights_out(t - 1)
            tile(TT - 1)
            weights_out(TT - 2)

            def load_gate_up(par, gate, up, left):
                for k in range(G_PIECES):
                    left(k)
                    chunks = slice(k % 2 * (DC // 2), (k % 2 + 1) * (DC // 2))
                    w = (gate, up)[k // 2].rearrange("(p c) n -> p c n", c=DC)[:, chunks]
                    sp.dma_start(raw_gu[par][:, k // 2, chunks], w).then_inc(g_raw[par][k], 16)

            def load_down(par, down, left):
                for k in range(D_PIECES):
                    left(k)
                    sp.dma_start(raw_dn[par][:, k], down.rearrange("(p c) n -> p c n", c=FC)[:, k]).then_inc(d_raw[par], 16)

            def next_gate_up(s, par):
                load_gate_up(par, *(w[ds(s - 1, 1)].rearrange("o k n -> (o k) n") for w in (w_gate, w_up)),
                             lambda k: sp.wait_ge(S["g_lo_ok"], G_PIECES * (s - 2) + k + 1))

            def next_down(s, par):
                load_down(par, w_down[ds(s - 1, 1)].rearrange("o k n -> (o k) n"),
                          lambda k: sp.wait_ge(S["d_lo_ok"], D_PIECES * (s - 2) + k + 1))

            def free(k):
                pass

            sp.wait_ge(S["ot_lo_ok"], TT)
            sp.wait_ge(S["oproj"], TT)
            load_gate_up(0, ws_gate, ws_up, free)
            load_down(0, ws_down, free)
            weights_out(TT - 1)
            load_gate_up(1, w_gate[0], w_up[0], free)
            load_down(1, w_down[0], free)
            sp.wait_ge(S["extra_ok"], 2)
            sp.wait_ge(S["listed"], 16 * TT * TOP_K)
            sp.wait_ge(S["c_fill"], 64)
            sp.wait_ge(S["x1_stored"], 16 * TT)
            sp.wait_ge(S["wts_stored"], 16 * TT)
            sp.dma_start(tab[:], tab_dram.rearrange("(p n) o -> p (n o)", p=P)).then_inc(S["tab_in"], 16)

            next_gate_up(2, 0)
            next_down(2, 0)
            next_gate_up(3, 1)
            with sp.Fori(0, E // 2 - 2) as i:
                for par in range(2):
                    next_gate_up(2 * i + (par + 4), par)
                    next_down(2 * i + (par + 3), 1 - par)
            next_gate_up(E, 0)
            next_down(E - 1, 1)
            next_down(E, 0)
            def load_sums(j, t):
                sp.dma_start(fin[j][:, t], sums[j][t * P:(t + 1) * P, :]).then_inc(tile_in[t], 16)
            sp.wait_ge(S["g_lo_ok"], G_PIECES * (E + 1))
            sp.wait_ge(sent[0], 8 * E + SENT_0[0])
            for t in range(TT):
                load_sums(0, t)
            sp.wait_ge(S["summed"], 1)
            for t in range(TT):
                load_sums(1, t)
                load_sums(2, t)
                if t == 0:
                    sp.dma_start(g2[:], ln2_g.to_broadcast([P, D])).then_inc(S["g2_in"], 16)
                    sp.dma_start(b2[:], ln2_b.to_broadcast([P, D])).then_inc(S["g2_in"], 16)
            for t in range(TT):
                sp.wait_ge(S["f_out"], t + 1)
                sp.dma_start(out[t * P:(t + 1) * P, :], fin[2][:, t]).then_inc(stored, 16)
            sp.wait_ge(stored, 16 * TT)

        @block.gpsimd
        def _(pool):
            g = nc.gpsimd
            g.memset(ident[:], 0.0).then_inc(S["consts"], 1)
            g.memset(mask_qk[:], 0.0).then_inc(S["consts"], 1)
            g.memset(mask_kq[:], 0.0).then_inc(S["consts"], 1)
            g.memset(upto[:], 1.0).then_inc(S["consts"], 1)
            pool.wait_ge(S["consts"], 4)
            g.affine_select(out=ident[:], in_=ident[:], compare_op=ALU.not_equal, fill=1.0, base=0,
                            pattern=[[-1, P]], channel_multiplier=1).then_inc(S["masks"], 1)
            pool.wait_ge(S["masks"], 1)
            g.tensor_copy(identb[:], ident[:]).then_inc(S["masks"], 1)
            g.affine_select(out=mask_qk[:], in_=mask_qk[:], compare_op=ALU.is_ge, fill=NEVER, base=0,
                            pattern=[[-1, P]], channel_multiplier=1).then_inc(S["masks"], 1)
            g.affine_select(out=mask_kq[:], in_=mask_kq[:], compare_op=ALU.is_ge, fill=NEVER, base=0,
                            pattern=[[1, P]], channel_multiplier=-1).then_inc(S["masks"], 1)
            g.affine_select(out=upto[:], in_=upto[:], compare_op=ALU.is_ge, fill=0.0, base=0,
                            pattern=[[1, T]], channel_multiplier=-1).then_inc(S["masks"], 1)
            pool.wait_ge(S["v_ok"], NVC * TT // 2)
            for i in range(2):
                pool.wait_ge(v_stored[i], 16 * NVC * TT // 4)
            pool.wait_ge(S["c_stored"], 32)
            pool.wait_ge(S["v_ps"], NVC * TT // 2)
            n = 0
            for par in range(2):
                for buf in (q_hi, q_lo, k_hi, k_lo):
                    g.memset(buf[par][DH:P, :].bitcast(F32), 0.0).then_inc(S["aug0"], 1)
                    n += 1
                    pool.wait_ge(S["aug0"], n)
                g.memset(va[par][:, :, DH:P], 1.0).then_inc(S["aug0"], 1)
                n += 1
                pool.wait_ge(S["aug0"], n)
                g.memset(q_hi[par][ONE_ROW:ONE_ROW + 1, :].bitcast(F32), 1.0).then_inc(S["aug0"], 1)
                n += 1
                pool.wait_ge(S["aug0"], n)
                g.memset(k_hi[par][MAX_ROW:MAX_ROW + 1, :].bitcast(F32), 1.0).then_inc(S["aug"], 1)
                pool.wait_ge(S["aug"], par + 1)
            g.memset(ones_b[:], 1.0).then_inc(S["c_const"], 1)
            pool.wait_ge(S["c_const"], 1)
            g.affine_select(out=before[:], in_=ones_b[:], compare_op=ALU.is_gt, fill=0.0, base=0,
                            pattern=[[1, P]], channel_multiplier=-1).then_inc(S["c_const"], 1)

            pool.wait_ge(S["normed"], HEADS)
            g.iota(e8[:], pattern=[[TAB_BLOCKS, E]], base=0, channel_multiplier=0, allow_small_or_imprecise_dtypes=True).then_inc(S["c_const"], 1)
            g.iota(tok_all[:], pattern=[[P, TT]], base=0, channel_multiplier=1).then_inc(S["c_const"], 1)
            g.iota(tab0[:], pattern=[[0, TAB]], base=T, channel_multiplier=1).then_inc(S["c_const"], 1)
            g.memset(zeros[:], 0.0).then_inc(S["c_const"], 1)
            g.memset(gtop[:], 3e38).then_inc(S["c_const"], 1)
            g.memset(base[:], 0.0).then_inc(S["c_const"], 1)
            pool.wait_ge(S["c_const"], 8)
            pool.dma_start(tab_dram.rearrange("(p n) o -> p (n o)", p=P), tab0[:]).then_inc(S["c_fill"], 16)
            pool.dma_start(rows_dram[T:ROWS, :], zeros[:]).then_inc(S["c_fill"], 16)
            for i in range(2):
                pool.dma_start(sums[i][T:ROWS, :], zeros[:, 0:D]).then_inc(S["c_fill"], 16)
            for t in range(ROWS // P):
                pool.dma_start(sums[2][t * P:(t + 1) * P, :], zeros[:, 0:D]).then_inc(sent[2], 16)
            pool.wait_ge(S["c_fill"], 64)

            def list_tokens(t):
                if not (static(t) and t == 0):
                    pool.wait_ge(S["listed"], 16 * TOP_K * t)
                g.tensor_copy(tok[:], tok_all[:, ds(t, 1)]).then_inc(S["tok_ok"], 1)
                pool.wait_ge(S["tok_ok"], t + 1)
                pool.wait_ge(S["dest_ok"], t + 1)
                for k in range(TOP_K):
                    g.indirect_dma_start(out=tab_dram, out_offset=bass.IndirectOffsetOnAxis(ap=dest_i[:, k:k + 1], axis=0),
                                         in_=tok[:], in_offset=None).then_inc(S["listed"], 16)
            list_tokens(0)
            for t in range(1, TT):
                list_tokens(t)

            def wait_routed():
                pool.wait_ge(S["listed"], 16 * TT * TOP_K)
                pool.wait_ge(S["extra_ok"], 2)
                pool.wait_ge(S["x1_stored"], 16 * TT)
                pool.wait_ge(S["wts_stored"], 16 * TT)

            def gather(i, e, k, count, done):
                stand(pool)
                g.tensor_copy(gidx[i][:], tab[:, ds(e * TAB_BLOCKS + k, 1)]).then_inc(idx_ok[i], 1)
                pool.wait_ge(idx_ok[i], count + 1)
                stand(pool)
                g.indirect_dma_start(out=xg[i][:], out_offset=None, in_=rows_dram,
                                     in_offset=bass.IndirectOffsetOnAxis(ap=gidx[i][:, 0:1], axis=0)).then_inc(done, 16)

            def scatter_add(i, e, k, b):
                stand(pool)
                g.tensor_copy(sidx[i][:], tab[:, ds(e * TAB_BLOCKS + k, 1)]).then_inc(S["sidx_ok"], 1)
                pool.wait_ge(S["sidx_ok"], b - SH + 1)
                stand(pool)
                g.indirect_dma_start(out=sums[i], out_offset=bass.IndirectOffsetOnAxis(ap=sidx[i][:, 0:1], axis=0),
                                     in_=ys[i][:], in_offset=None, compute_op=ALU.add).then_inc(sent[i], 16)

            def add_first(par, e, b):
                pool.wait_ge(S["scaled"], b + 1)
                pool.wait_ge(sent[par], 8 * (e - par) + SENT_0[par])
                scatter_add(par, e, 0, b)

            def add_further(e, k, b, xi):
                pool.wait_ge(S["scaled"], b + 1)
                pool.wait_ge(sent[2], 16 * (xi + k) + (SENT_0[2] - 16))
                scatter_add(2, e, k, b)

            def earlier_of(e):
                return pool.value_load(earlier[0:1, ds(e, 1)], min_val=0, max_val=E * TAB_BLOCKS)

            def further_of(e):
                return pool.value_load(further[0:1, ds(e, 1)], min_val=0, max_val=TAB_BLOCKS - 1)

            wait_routed()
            for b in range(2):
                pool.dma_start(xg[b][:], rows_dram[b * P:(b + 1) * P, :]).then_inc(got[b], 16)
            for b in range(SH):
                pool.wait_ge(S["turned"], b + 1)
                if b + 2 < SH:
                    pool.dma_start(xg[b % 2][:], rows_dram[(b + 2) * P:(b + 3) * P, :]).then_inc(got[b % 2], 16)
                else:
                    pool.wait_ge(S["tab_in"], 16)
                    gather(b % 2, b + 2 - SH, 0, 0, got[b % 2])
                if b >= 1:
                    pool.wait_ge(S["scaled"], b)
                    pool.dma_start(sums[1][(b - 1) * P:b * P, :], ys[(b - 1) % 2][:]).then_inc(sent[(b - 1) % 2], 16)
            f0 = further_of(0)
            with pool.If(f0 > 0):
                gather(2, 0, 1, earlier_of(0), S["x_in"])

            def retire(e, par, b0, xi, nx):
                with pool.If(nx < 2):
                    add_first(par, e, b0)
                with pool.If(nx > 0):
                    add_further(e, nx, b0 + nx, xi)

            def expert(e, par, pos):
                if pos != "last":
                    pool.wait_ge(S["w_ok"], e + 1)
                    gather(par, e + 2, 0, (e + 2 - par) // 2 if static(e) else (e + 2 - par) // 2, got[par])
                xi, nx = earlier_of(e), further_of(e)
                b0 = xi + e + SH

                def left_over():
                    if pos == "first":
                        pool.wait_ge(S["scaled"], SH)
                        pool.dma_start(sums[1][(SH - 1) * P:T, :], ys[(SH - 1) % 2][:]).then_inc(sent[(SH - 1) % 2], 16)
                        for i in range(2):
                            pool.wait_ge(sent[i], 16 * SH // 2)
                    else:
                        xp = earlier_of(e - 1)
                        retire(e - 1, 1 - par, xp + e + (SH - 1), xp, further_of(e - 1))
                with pool.If(nx > 1):
                    left_over()
                    add_first(par, e, b0)
                    with pool.Fori(1, nx) as k:
                        pool.wait_ge(S["x_w_ok"], xi + k)
                        gather(2, e, k + 1, xi + k, S["x_in"])
                        add_further(e, k, b0 + k, xi)
                if not (pos == "last" and par == 1):
                    f1 = further_of(e + 1)
                    with pool.If(f1 > 0):
                        pool.wait_ge(S["x_w_ok"], xi + nx + 1)
                        gather(2, e + 1, 1, xi + nx, S["x_in"])
                with pool.If(nx < 2):
                    left_over()
                return b0, xi, nx

            expert(0, 0, "first")
            expert(1, 1, "")
            with pool.Fori(1, E // 2 - 1) as i:
                for par in range(2):
                    expert(2 * i + par, par, "")
            expert(E - 2, 0, "last")
            b0, xi, nx = expert(E - 1, 1, "last")
            retire(E - 1, 1, b0, xi, nx)
            for i in range(2):
                pool.wait_ge(sent[i], 8 * E + SENT_0[i])
            pool.wait_ge(sent[2], 16 * (xi + nx) + SENT_0[2])
            stand(pool)
            pool.sem_inc(S["summed"], 1)
            for t in range(TT):
                pool.wait_ge(tile_in[t], 16 * 4)
                g.tensor_tensor(fin[1][:, t], fin[1][:, t], fin[2][:, t], ALU.add).then_inc(S["f_part"], 1)

        @block.tensor
        def _(pe):
            pe.wait_ge(S["masks"], 1)
            for g in range(NXT):
                c, half = g // 2, g % 2
                if c == 0:
                    for t in range(4):
                        pe.wait_ge(tile_in[half * 4 + t], 16)
                if g >= 2:
                    pe.wait_ge(S["xt_lo_ok"], g - 1)
                for t in range(4):
                    i = pe.transpose(banks[g % 2][:, t * P:(t + 1) * P], xs[:, half * 4 + t, c * P:(c + 1) * P], ident[:])
                i.then_inc(S["xt_ps"], 1)
            pe.wait_ge(S["xt_lo_ok"], NXT)
            pe.wait_ge(S["wf_ok"], 2)
            for t in range(TT):
                for c in range(DC):
                    i = split_matmul(pe, banks[0][:, t * HEADS:(t + 1) * HEADS], xt_hi[:, c, t * P:(t + 1) * P],
                                     xt_lo[:, c, t * P:(t + 1) * P], wf_hi[:, c], wf_lo[:, c], c == 0, c == DC - 1)
            i.then_inc(S["z_ps"], 1)

            def gate_sums():
                pe.wait_ge(S["gate_ok"], 1)
                pe.wait_ge(S["masks"], 5)
                for half in range(2):
                    last = 4 * half + 3
                    for j in range(last + 1):
                        t0 = max(half * BANK, j * P)
                        i = pe.matmul(q_ps[0:HEADS, t0:(half + 1) * BANK], gate8[:, j, :], upto[:, t0 - j * P:(half + 1) * BANK - j * P],
                                      start=j == 0, stop=j == last, skip_group_check=True)
                i.then_inc(S["c_ps"], 1)

            for n in range(NVC * TT // 2):
                c0, t2 = n // (TT // 2), n % (TT // 2)
                if n == 4:
                    gate_sums()
                if t2 == 0:
                    pe.wait_ge(S["wv_lo_ok"], c0 + 1)
                if n == 0:
                    pe.wait_ge(S["z_ok"], 1)
                if n >= 2:
                    pe.wait_ge(S["v_ok"], n - 1)
                for j in range(2):
                    t = 2 * t2 + j
                    for c in range(DC):
                        i = split_matmul(pe, banks[n % 2][:, j * VC:(j + 1) * VC], xt_hi[:, c, t * P:(t + 1) * P],
                                         xt_lo[:, c, t * P:(t + 1) * P], wv_hi[:, c0 % 2, c], wv_lo[:, c0 % 2, c], c == 0, c == DC - 1)
                i.then_inc(S["v_ps"], 1)

            def project(p):
                pe.wait_ge(S["wqk_lo_ok"], p + 1)
                for j, ps in enumerate((q_ps, k_ps)):
                    for half in range(2):
                        r = slice(half * BANK, (half + 1) * BANK)
                        for c in range(DC):
                            i = split_matmul(pe, ps[:, r], wqk_hi[:, c, j], wqk_lo[:, c, j], xt_hi[:, c, r], xt_lo[:, c, r],
                                             c == 0, c == DC - 1)
                i.then_inc(S["proj"], 1)

            def slot_free(h, n):
                m = n - 2
                if m < 0:
                    if not (isinstance(h, int) and h == 0):
                        pe.wait_ge(S["exped"], h * NK + m + 1)
                elif m < NQ:
                    pe.wait_ge(S["maxed"], h * NQ + m + 1)
                elif m < NQ + NR:
                    pe.wait_ge(S["r_lo"], h * NR + m - NQ + 1)
                else:
                    pe.wait_ge(S["exped"], h * NK + m - NQ - NR + 1)

            def scores_by_query(p, par):
                h = 2 * p + par
                pe.wait_ge(ev_lo[par], p + 1)
                pe.wait_ge(c_in[par], 32 * (p + 1))
                for n, (t, k0, w) in enumerate(BY_QUERY):
                    slot_free(h, n)
                    s = banks[n % 2]
                    diag = k0 + w == (t + 1) * P
                    q, k = slice(t * P, (t + 1) * P), slice(k0, k0 + w)
                    i = split_matmul(pe, s[:, 0:w], q_hi[par][0:MAX_ROW, q], q_lo[par][0:MAX_ROW, q],
                                     k_hi[par][0:MAX_ROW, k], k_lo[par][0:MAX_ROW, k], True, not diag)
                    if diag:
                        i = pe.matmul(s[:, w - P:w], identb[:], mask_qk[:], start=False, stop=True, skip_group_check=True)
                    i.then_inc(S["score"], 1)

            def max_rows(p, par):
                h = 2 * p + par
                pe.wait_ge(S["mx_ok"], h + 1)
                for n in range(NR):
                    slot_free(h, NQ + n)
                    for t in range(4):
                        i = pe.transpose(banks[n % 2][:, t * P:(t + 1) * P], mx[:, 4 * n + t:4 * n + t + 1].to_broadcast([P, P]), ident[:])
                    i.then_inc(S["score"], 1)

            def scores_by_key(p, par):
                h = 2 * p + par
                pe.wait_ge(S["r_lo"], h * NR + NR)
                for n, (t, q0, w, _) in enumerate(BY_KEY):
                    slot_free(h, NQ + NR + n)
                    s = banks[n % 2]
                    diag = q0 == t * P
                    q, k = slice(q0, q0 + w), slice(t * P, (t + 1) * P)
                    i = split_matmul(pe, s[:, 0:w], k_hi[par][0:MAX_ROW + 1, k], k_lo[par][0:MAX_ROW + 1, k],
                                     q_hi[par][0:MAX_ROW + 1, q], q_lo[par][0:MAX_ROW + 1, q], True, not diag)
                    if diag:
                        i = pe.matmul(s[:, 0:P], identb[:], mask_kq[:], start=False, stop=True, skip_group_check=True)
                    i.then_inc(S["score"], 1)

            def weigh_v(p, par, tiles):
                h = 2 * p + par
                if 0 in tiles:
                    pe.wait_ge(S["exped"], h * NK + NK)
                    pe.wait_ge(va_in[par], 16 * (p + 1))
                    if not (isinstance(h, int) and h == 0):
                        pe.wait_ge(S["normed"], h)
                for (t, q0, w, at) in BY_KEY:
                    if t in tiles:
                        i = pe.matmul(out_ps[:, q0:q0 + w], va[par][:, t, :], probs[:, at:at + w], start=t == 0,
                                      stop=t == (3 if q0 < BANK else TT - 1), skip_group_check=True)
                if TT - 1 in tiles:
                    i.then_inc(S["pv"], 1)

            def pair(p, first=False, last=False):
                scores_by_query(p, 0)
                if not first:
                    weigh_v(p - 1, 1, range(TT))
                max_rows(p, 0)
                if not last:
                    pe.wait_ge(ev_lo[1], p + 1)
                    project(p + 1)
                scores_by_key(p, 0)
                scores_by_query(p, 1)
                weigh_v(p, 0, range(0, 4))
                max_rows(p, 1)
                weigh_v(p, 0, range(4, TT))
                scores_by_key(p, 1)

            pe.wait_ge(S["c_lo_ok"], 2)
            project(0)
            pe.wait_ge(S["v_ok"], NVC * TT // 2)
            pe.wait_ge(S["aug"], 2)
            pair(0, first=True)
            with pe.Fori(1, PAIRS - 1) as p:
                pair(p)
            pair(PAIRS - 1, last=True)
            weigh_v(PAIRS - 1, 1, range(TT))

            def out_projection(t):
                pe.wait_ge(S["ot_lo_ok"], t + 1)
                if not (static(t) and t == 0):
                    pe.wait_ge(S["r1_ok"], t)
                else:
                    pe.wait_ge(S["wo_lo_ok"], DC)
                for half in range(2):
                    r = slice(half * BANK, (half + 1) * BANK)
                    for c in range(DC):
                        i = split_matmul(pe, q_ps[:, r], ot_hi[:, c], ot_lo[:, c], wo_hi[:, c, r], wo_lo[:, c, r], c == 0, c == DC - 1)
                i.then_inc(S["oproj"], 1)

            def turn_x1(t):
                pe.wait_ge(S["x1_ok"], t + 1)
                for c in range(DC):
                    i = pe.transpose(k_ps[:, c * P:(c + 1) * P], x1[:, c * P:(c + 1) * P], ident[:])
                i.then_inc(S["x1t_ps"], 1)

            def logits(t):
                pe.wait_ge(S["x1t_lo_ok"], t + 1)
                if static(t) and t == 0:
                    pe.wait_ge(S["wr_ok"], 2)
                else:
                    pe.wait_ge(S["ex_ok"], t)
                for c in range(DC):
                    i = split_matmul(pe, banks[0][:, 0:E], x1t_hi[:, c], x1t_lo[:, c], wr_hi[:, c], wr_lo[:, c], c == 0, c == DC - 1)
                i.then_inc(S["logit_ps"], 1)

            def places(t):
                pe.wait_ge(S["chosen_ok"], t + 1)
                if not (static(t) and t == 0):
                    pe.wait_ge(S["route0"], t)
                pe.matmul(banks[1][:, 0:E], before[:], chosen_b[:], start=True, stop=True, skip_group_check=True)
                pe.matmul(banks[1][:, E:2 * E], ones_b[:], chosen_b[:], start=True, stop=True, skip_group_check=True).then_inc(S["pos_ps"], 1)

            out_projection(0)
            out_projection(1)
            turn_x1(0)
            logits(0)
            for t in range(2, TT):
                out_projection(t)
                turn_x1(t - 1)
                places(t - 2)
                logits(t - 1)
            turn_x1(TT - 1)
            places(TT - 2)
            logits(TT - 1)
            places(TT - 1)

            def turn_rows(src, ps):
                v = strided(src[:, 0:D])
                for c in range(DC):
                    i = pe.transpose(ps[:, c * P:(c + 1) * P], v[:, c], ident[:])
                return i

            def gate_up(s, w):
                g_hi, g_lo = split[w][0:2]
                o3 = banks[0][:].rearrange("p (g f) -> p g f", g=2)
                for c in range(DC):
                    x_hi, x_lo, w_hi, w_lo = xb_hi[s][:, c], xb_lo[s][:, c], g_hi[:, :, c], g_lo[:, :, c]
                    i = pe.matmul(o3, x_hi, w_hi, start=c == 0, stop=False, skip_group_check=True)
                    if c == 0:
                        i.then_inc(S["started"], 1)
                    pe.matmul(o3, x_hi, w_lo, start=False, stop=False, skip_group_check=True)
                    i = pe.matmul(o3, x_lo, w_hi, start=False, stop=c == DC - 1, skip_group_check=True)
                i.then_inc(S["gated"], 1)

            def turn_h(b):
                pe.wait_ge(S["h_ok"], b + 1)
                v = strided(hh[:])
                for c in range(FC):
                    i = pe.transpose(banks[1][:, c * P:(c + 1) * P], v[:, c], ident[:])
                i.then_inc(S["ht_ps"], 1)

            def down(b, w, nset):
                d_hi, d_lo = split[w][2:4]
                pe.wait_ge(S["ht_lo_ok"], b + 1)
                pe.wait_ge(S["d_lo_ok"], D_PIECES * nset)
                if not (static(b) and b == 0):
                    pe.wait_ge(S["scaled"], b)
                for half in range(2):
                    r = slice(half * BANK, (half + 1) * BANK)
                    for c in range(FC):
                        i = split_matmul(pe, k_ps[:, r], ht_hi[:, c], ht_lo[:, c], d_hi[:, c, r], d_lo[:, c, r], c == 0, c == FC - 1)
                i.then_inc(S["downed"], 1)

            pe.wait_ge(got[0], 16)
            turn_rows(xg[0], q_ps).then_inc(S["turned"], 1)
            for b in range(SH):
                if b >= 1:
                    turn_h(b - 1)
                pe.wait_ge(S["rows_lo_ok"], b + 1)
                pe.wait_ge(S["g_lo_ok"], G_PIECES)
                gate_up(b % 2, 0)
                pe.wait_ge(got[(b + 1) % 2], 16 * ((b + 1) // 2 + 1))
                turn_rows(xg[(b + 1) % 2], q_ps).then_inc(S["turned"], 1)
                if b >= 1:
                    down(b - 1, 0, 1)

            def expert(e, par, last=False):
                w = 1 - par
                xi = pe.value_load(earlier[0:1, ds(e, 1)], min_val=0, max_val=E * TAB_BLOCKS)
                b0 = xi + e + SH
                turn_h(b0 - 1)
                pe.wait_ge(S["rows_lo_ok"], SH + e + 1)
                pe.wait_ge(S["g_lo_ok"], G_PIECES * (e + 2))
                gate_up(par, w)
                nx = pe.value_load(further[0:1, ds(e, 1)], min_val=0, max_val=TAB_BLOCKS - 1)
                with pe.If(nx > 0):
                    pe.wait_ge(S["x_in"], 16 * xi + 16)
                    turn_rows(xg[2], out_ps).then_inc(S["x_turned"], 1)
                if not last:
                    pe.wait_ge(got[1 - par], 8 * (SH + e + par) + 16)
                    turn_rows(xg[1 - par], q_ps).then_inc(S["turned"], 1)
                down(b0 - 1, par, e + 1)
                with pe.If(nx > 0):
                    turn_h(b0)
                    pe.wait_ge(S["x_rows_lo_ok"], xi + 1)
                    gate_up(2, w)
                    down(b0, w, e + 2)
                    with pe.If(nx > 1):
                        with pe.Fori(1, nx) as k:
                            turn_h(b0 + k)
                            down(b0 + k, w, e + 2)
                            pe.wait_ge(S["x_in"], 16 * (xi + k) + 16)
                            turn_rows(xg[2], out_ps).then_inc(S["x_turned"], 1)
                            pe.wait_ge(S["x_rows_lo_ok"], xi + k + 1)
                            gate_up(2, w)
                return b0, nx

            with pe.Fori(0, E // 2 - 1) as i:
                for par in range(2):
                    expert(2 * i + par, par)
            expert(E - 2, 0)
            b0, nx = expert(E - 1, 1, last=True)
            turn_h(b0 + nx)
            down(b0 + nx, 0, E + 1)

        @block.scalar
        def _(act):
            a = nc.scalar
            act.wait_ge(S["wf_in"], 16)
            a.copy(wf_hi[:], wf[:]).then_inc(S["wf_ok"], 1)
            for g in range(NXT):
                c, half = g // 2, g % 2
                act.wait_ge(S["xt_ps"], g + 1)
                a.copy(xt_hi[:, c, half * BANK:(half + 1) * BANK], banks[g % 2][:]).then_inc(S["xt_hi_ok"], 1)

            def split_wv(n):
                act.wait_ge(wv_in[n % 2], 16 * (n // 2 + 1))
                if n >= 2:
                    act.wait_ge(S["v_ps"], (n - 1) * TT // 2)
                a.copy(wv_hi[:, n % 2], wv[:, n % 2]).then_inc(S["wv_hi_ok"], 1)

            split_wv(0)
            split_wv(1)
            act.wait_ge(S["zabs_ok"], 1)
            a.activation(zexp[:], zabs[:], ACT.Exp, scale=-1.0).then_inc(S["zexp_ok"], 1)
            act.wait_ge(S["zexp_ok"], 2)
            a.activation(zlog[:], zexp[:], ACT.Ln).then_inc(S["zlog_ok"], 1)
            act.wait_ge(S["wqk_in"], 32)
            a.copy(wqk_hi[:], wqk[:]).then_inc(S["wqk_hi_ok"], 1)
            for n in range(NVC * TT // 2):
                if n and n % (TT // 2) == 0 and n // (TT // 2) + 1 < NVC:
                    split_wv(n // (TT // 2) + 1)
                if n == 5:
                    act.wait_ge(S["c_ps"], 1)
                    a.copy(c_hi[:], q_ps[0:HEADS, :]).then_inc(S["c_hi_ok"], 1)
                act.wait_ge(S["v_ps"], n + 1)
                if n >= 2:
                    act.wait_ge(v_stored[n % 2], 16 * (n // 2))
                a.copy(v_out[:, n % 2], banks[n % 2][:]).then_inc(S["v_ok"], 1)

            def take(p, par):
                act.wait_ge(S["proj"], p + 1)
                rows = slice(par * DH, (par + 1) * DH)
                a.copy(q_hi[par][0:DH, :], q_ps[rows, :])
                a.copy(k_hi[par][0:DH, :], k_ps[rows, :]).then_inc(ev_hi[par], 1)

            def max_row(p, par):
                h = 2 * p + par
                for n in range(NR):
                    act.wait_ge(S["score"], h * SLOTS + NQ + n + 1)
                    a.mul(q_hi[par][MAX_ROW:MAX_ROW + 1, n * BANK:(n + 1) * BANK], banks[n % 2][MAX_ROW:MAX_ROW + 1, :],
                          -1.0).then_inc(S["r_hi"], 1)

            def exponentials(p, par):
                h = 2 * p + par
                if not (isinstance(h, int) and h == 0):
                    act.wait_ge(S["pv"], h)
                for n, (_, _, w, at) in enumerate(BY_KEY):
                    act.wait_ge(S["score"], h * SLOTS + NQ + NR + n + 1)
                    a.activation(probs[:, at:at + w], banks[n % 2][:, 0:w], ACT.Exp, scale=SCALE).then_inc(S["exped"], 1)

            def pair(p, first=False, last=False):
                if not first:
                    act.wait_ge(S["score"], 2 * p * SLOTS)
                take(p, 1)
                if not last:
                    act.wait_ge(S["wqk_in"], 32 * (p + 2))
                    act.wait_ge(S["proj"], p + 1)
                    a.copy(wqk_hi[:], wqk[:]).then_inc(S["wqk_hi_ok"], 1)
                max_row(p, 0)
                exponentials(p, 0)
                if not last:
                    act.wait_ge(S["score"], (2 * p + 1) * SLOTS)
                    take(p + 1, 0)
                max_row(p, 1)
                exponentials(p, 1)

            act.wait_ge(S["aug"], 2)
            take(0, 0)
            pair(0, first=True)
            with act.Fori(1, PAIRS - 1) as p:
                pair(p)
            pair(PAIRS - 1, last=True)

            for c in range(DC):
                act.wait_ge(wo_in[c % STAGES], 16 * (c // STAGES + 1))
                a.copy(wo_hi[:, c], wo[:, c % STAGES]).then_inc(S["wo_hi_ok"], 1)
            act.wait_ge(S["normed"], HEADS)

            def heads_hi(t):
                if not (static(t) and t == 0):
                    act.wait_ge(S["oproj"], t)
                a.copy(ot_hi[:], attn[:, :, ds(t * P, P)]).then_inc(S["ot_hi_ok"], 1)

            def x1t_hi_of(t):
                act.wait_ge(S["x1t_ps"], t + 1)
                if not (static(t) and t == 0):
                    act.wait_ge(S["logit_ps"], t)
                a.copy(x1t_hi[:], k_ps[:].rearrange("p (c t) -> p c t", c=DC)).then_inc(S["x1t_hi_ok"], 1)

            def ax_of(t):
                act.wait_ge(S["x1_ok"], t + 1)
                if t:
                    act.wait_ge(S["ax_stored"], 16 * t)
                a.mul(ax[:], x1[:], ALPHA).then_inc(S["ax_ok"], 1)

            def exp_of(t):
                act.wait_ge(S["logit_ps"], t + 1)
                if not (static(t) and t == 0):
                    act.wait_ge(S["chosen_ok"], t)
                a.activation(ex[:], banks[0][:, 0:E], ACT.Exp, scale=-1.0).then_inc(S["ex_ok"], 1)

            def std_of(t):
                act.wait_ge(S["var_ok"], t + 2)
                a.activation(std[:], mv[:, 1:2], ACT.Sqrt, bias=eps[:, 0:1]).then_inc(S["std_ok"], 1)

            heads_hi(0)
            act.wait_ge(S["c_loads"], 64)
            a.copy(wr_hi[:], wr[:]).then_inc(S["wr_ok"], 1)
            heads_hi(1)
            std_of(0)
            for t in range(1, TT):
                if t < TT - 1:
                    heads_hi(t + 1)
                x1t_hi_of(t - 1)
                ax_of(t - 1)
                std_of(t)
                exp_of(t - 1)
            x1t_hi_of(TT - 1)
            ax_of(TT - 1)
            exp_of(TT - 1)

            def w_high(which, done, w, k):
                raw, hi, _ = which(w, k)
                a.copy(hi, raw).then_inc(S[done], 1)

            act.wait_ge(S["oproj"], TT)
            for k in range(G_PIECES):
                act.wait_ge(g_raw[0][k], 16)
                w_high(g_piece, "g_hi_ok", 0, k)
            act.wait_ge(d_raw[0], 16 * D_PIECES)
            for k in range(D_PIECES):
                w_high(d_piece, "d_hi_ok", 0, k)
            act.wait_ge(S["extra_ok"], 2)
            act.wait_ge(S["listed"], 16 * TT * TOP_K)
            act.wait_ge(S["wts_stored"], 16 * TT)
            act.wait_ge(S["x1_stored"], 16 * TT)
            act.wait_ge(S["ax_stored"], 16 * TT)

            def rows_hi(s, ps, wait, n, done):
                act.wait_ge(S[wait], n)
                a.copy(xb_hi[s][:], ps[:].rearrange("p (c t) -> p c t", c=DC)).then_inc(S[done], 1)

            def silu(b):
                act.wait_ge(S["gated"], b + 1)
                a.activation(sg[:], banks[0][:, 0:FF], ACT.Silu).then_inc(S["silu_ok"], 1)

            def h_hi(b):
                act.wait_ge(S["ht_ps"], b + 1)
                a.copy(ht_hi[:], banks[1][:, 0:FF].rearrange("p (c t) -> p c t", c=FC)).then_inc(S["ht_hi_ok"], 1)

            def scale_rows(i, b, added):
                act.wait_ge(S["downed"], b + 1)
                if not (static(added) and added == 0):
                    act.wait_ge(sent[i], added)
                if static(b):
                    a.copy(ys[i][:], k_ps[:]).then_inc(S["scaled"], 1)
                else:
                    a.activation(ys[i][:], k_ps[:], ACT.Copy, scale=wcol[i][:, 0:1]).then_inc(S["scaled"], 1)

            def next_gate_up(b, e, par):
                act.wait_ge(S["started"], b + 1)
                for k in range(G_PIECES):
                    act.wait_ge(g_raw[par][k], 8 * (e + 2 - par) + 16)
                    w_high(g_piece, "g_hi_ok", par, k)

            rows_hi(0, q_ps, "turned", 1, "rows_hi_ok")
            for b in range(SH):
                if b >= 1:
                    h_hi(b - 1)
                if b == SH - 1:
                    next_gate_up(b, -1, 1)
                silu(b)
                rows_hi((b + 1) % 2, q_ps, "turned", b + 2, "rows_hi_ok")
                if b >= 1:
                    scale_rows((b - 1) % 2, b - 1, 16 * ((b - 1) // 2))

            def expert(e, par, pos):
                xi = act.value_load(earlier[0:1, ds(e, 1)], min_val=0, max_val=E * TAB_BLOCKS)
                b0 = xi + e + SH
                nx = act.value_load(further[0:1, ds(e, 1)], min_val=0, max_val=TAB_BLOCKS - 1)
                if pos != "first":
                    np_ = act.value_load(further[0:1, ds(e - 1, 1)], min_val=0, max_val=TAB_BLOCKS - 1)
                h_hi(b0 - 1)
                if pos != "last":
                    next_gate_up(b0, e, par)
                silu(b0)
                with act.If(nx > 0):
                    rows_hi(2, out_ps, "x_turned", xi + 1, "x_rows_hi_ok")
                if pos != "last":
                    rows_hi(1 - par, q_ps, "turned", SH + e + 2, "rows_hi_ok")
                act.wait_ge(S["downed"], b0 - 1)
                act.wait_ge(d_raw[1 - par], 8 * D_PIECES * (e + par) + 16 * D_PIECES)
                for k in range(D_PIECES):
                    w_high(d_piece, "d_hi_ok", 1 - par, k)
                if pos == "first":
                    scale_rows(1, SH - 1, 16 * ((SH - 1) // 2))
                else:
                    with act.If(np_ > 0):
                        scale_rows(2, b0 - 1, 16 * xi + (SENT_0[2] - 16))
                    with act.If(np_ < 1):
                        scale_rows(1 - par, b0 - 1, 8 * (e + par) + (SENT_0[1 - par] - 16))
                with act.If(nx > 0):
                    h_hi(b0)
                    silu(b0 + 1)
                    scale_rows(par, b0, 8 * (e - par) + SENT_0[par])
                    with act.If(nx > 1):
                        with act.Fori(1, nx) as k:
                            h_hi(b0 + k)
                            scale_rows(2, b0 + k, 16 * (xi + k) + (SENT_0[2] - 16))
                            rows_hi(2, out_ps, "x_turned", xi + k + 1, "x_rows_hi_ok")
                            silu(b0 + k + 1)
                return b0, xi, nx
            expert(0, 0, "first")
            expert(1, 1, "")
            with act.Fori(1, E // 2 - 1) as i:
                for par in range(2):
                    expert(2 * i + par, par, "")
            expert(E - 2, 0, "")
            b0, xi, nx = expert(E - 1, 1, "last")
            h_hi(b0 + nx)
            with act.If(nx > 0):
                scale_rows(2, b0 + nx, 16 * (xi + nx) + (SENT_0[2] - 16))
            with act.If(nx < 1):
                scale_rows(1, b0 + nx, 8 * (E - 2) + SENT_0[1])

            for t in range(TT):
                act.wait_ge(S["f_var"], t + 2)
                a.activation(fstd[t % 2][:], fmv[t % 2][:, 1:2], ACT.Sqrt, bias=feps[:, 0:1]).then_inc(S["f_std"], 1)
                act.wait_ge(S["f_mv"], t + 1)
                a.activation(fin[1][:, t], fin[0][:, t], ACT.Identity, bias=fnm[t % 2][:, 0:1], scale=frstd[t % 2][:, 0:1]).then_inc(S["f_norm"], 1)

        @block.vector
        def _(dve):
            dve.wait_ge(S["wf_ok"], 1)
            dve.tensor_tensor(wf_lo[:], wf[:], wf_hi[:], ALU.subtract).then_inc(S["wf_ok"], 1)
            for g in range(NXT):
                c, half = g // 2, g % 2
                dve.wait_ge(S["xt_hi_ok"], g + 1)
                r = slice(half * BANK, (half + 1) * BANK)
                dve.tensor_tensor(xt_lo[:, c, r], banks[g % 2][:], xt_hi[:, c, r], ALU.subtract).then_inc(S["xt_lo_ok"], 1)

            def split_wv(n):
                dve.wait_ge(S["wv_hi_ok"], n + 1)
                dve.tensor_tensor(wv_lo[:, n % 2], wv[:, n % 2], wv_hi[:, n % 2], ALU.subtract).then_inc(S["wv_lo_ok"], 1)

            split_wv(0)
            dve.wait_ge(S["z_ps"], 1)
            dve.wait_ge(S["bf_in"], 16)
            dve.tensor_tensor(z[:], banks[0][:, 0:TT * HEADS].rearrange("p (t h) -> p t h", t=TT),
                              bf[:, None, :].to_broadcast([P, TT, HEADS]), ALU.add).then_inc(S["z_ok"], 1)
            dve.wait_ge(S["z_ok"], 1)
            dve.scalar_tensor_tensor(out=zabs[:], in0=z[:], scalar=-1.0, in1=z[:], op0=ALU.mult, op1=ALU.max).then_inc(S["zabs_ok"], 1)
            dve.tensor_scalar(zmin[:], z[:], 0.0, None, ALU.min).then_inc(S["zmin_ok"], 1)
            split_wv(1)
            dve.wait_ge(S["zexp_ok"], 1)
            dve.tensor_scalar(zexp[:], zexp[:], 1.0, None, ALU.add).then_inc(S["zexp_ok"], 1)
            dve.wait_ge(S["zlog_ok"], 1)
            dve.wait_ge(S["zmin_ok"], 1)
            dve.tensor_tensor(z[:], zlog[:], zmin[:], ALU.subtract).then_inc(S["z_ok"], 1)
            dve.wait_ge(S["z_ok"], 2)
            dve.tensor_scalar(gate8[:], z[:], 1.0 / SCALE, None, ALU.mult).then_inc(S["gate_ok"], 1)
            dve.wait_ge(S["wqk_hi_ok"], 1)
            dve.tensor_tensor(wqk_lo[:], wqk[:], wqk_hi[:], ALU.subtract).then_inc(S["wqk_lo_ok"], 1)
            split_wv(2)
            dve.wait_ge(S["c_hi_ok"], 1)
            for half in range(2):
                r = slice(half * BANK, (half + 1) * BANK)
                dve.tensor_tensor(c_lo[:, r], q_ps[0:HEADS, r], c_hi[:, r], ALU.subtract).then_inc(S["c_lo_ok"], 1)
            split_wv(3)
            dve.wait_ge(S["aug"], 2)
            dve.memset(mx2[:], -3e38).then_inc(S["mx20"], 1)
            dve.wait_ge(S["mx20"], 1)

            def take(p, par):
                dve.wait_ge(ev_hi[par], p + 1)
                rows = slice(par * DH, (par + 1) * DH)
                dve.tensor_tensor(q_lo[par][0:DH, :], q_ps[rows, :], q_hi[par][0:DH, :], ALU.subtract)
                dve.tensor_tensor(k_lo[par][0:DH, :], k_ps[rows, :], k_hi[par][0:DH, :], ALU.subtract).then_inc(ev_lo[par], 1)

            def maxima(p, par):
                h = 2 * p + par
                for n, (t, k0, w) in enumerate(BY_QUERY):
                    dve.wait_ge(S["score"], h * SLOTS + n + 1)
                    dve.tensor_reduce(mx2[:, t, k0 // BANK:k0 // BANK + 1], banks[n % 2][:, 0:w], AX_X, ALU.max).then_inc(S["maxed"], 1)
                dve.wait_ge(S["maxed"], h * NQ + NQ)
                dve.tensor_reduce(mx[:], mx2[:], AX_X, ALU.max).then_inc(S["mx_ok"], 1)

            def max_row(p, par):
                h = 2 * p + par
                for n in range(NR):
                    dve.wait_ge(S["r_hi"], h * NR + n + 1)
                    at = slice(n * BANK, (n + 1) * BANK)
                    dve.scalar_tensor_tensor(out=q_lo[par][MAX_ROW:MAX_ROW + 1, at], in0=banks[n % 2][MAX_ROW:MAX_ROW + 1, :], scalar=-1.0,
                                             in1=q_hi[par][MAX_ROW:MAX_ROW + 1, at], op0=ALU.mult, op1=ALU.subtract).then_inc(S["r_lo"], 1)

            def normalise(p, par):
                h = 2 * p + par
                dve.wait_ge(S["pv"], h + 1)
                dve.reciprocal(rec[:], out_ps[DH:P, :]).then_inc(S["rec_ok"], 1)
                dve.wait_ge(S["rec_ok"], h + 1)
                dve.tensor_tensor(attn[par * DH:(par + 1) * DH, bass.ds(p, 1), :], out_ps[0:DH, None, :], rec[:, None, :],
                                  ALU.mult).then_inc(S["normed"], 1)

            def pair(p, first=False, last=False):
                maxima(p, 0)
                take(p, 1)
                if not last:
                    dve.wait_ge(S["wqk_hi_ok"], p + 2)
                    dve.tensor_tensor(wqk_lo[:], wqk[:], wqk_hi[:], ALU.subtract).then_inc(S["wqk_lo_ok"], 1)
                max_row(p, 0)
                if not first:
                    normalise(p - 1, 1)
                maxima(p, 1)
                if not last:
                    take(p + 1, 0)
                max_row(p, 1)
                normalise(p, 0)

            take(0, 0)
            pair(0, first=True)
            with dve.Fori(1, PAIRS - 1) as p:
                pair(p)
            pair(PAIRS - 1, last=True)
            normalise(PAIRS - 1, 1)

            for c in range(DC):
                dve.wait_ge(S["wo_hi_ok"], c + 1)
                dve.tensor_tensor(wo_lo[:, c], wo[:, c % STAGES], wo_hi[:, c], ALU.subtract).then_inc(S["wo_lo_ok"], 1)

            def heads_lo(t):
                dve.wait_ge(S["ot_hi_ok"], t + 1)
                dve.tensor_tensor(ot_lo[:], attn[:, :, ds(t * P, P)], ot_hi[:], ALU.subtract).then_inc(S["ot_lo_ok"], 1)

            def steps(name, base_count):
                n = [0]

                def step(ins):
                    n[0] += 1
                    ins.then_inc(S[name], 1)
                    dve.wait_ge(S[name], base_count + n[0])
                return step, n

            def residual(t):
                dve.wait_ge(S["x_res_in"], 16 * (t + 1))
                dve.wait_ge(S["oproj"], t + 1)
                dve.scalar_tensor_tensor(out=r1[:], in0=x_res[:], scalar=ALPHA, in1=q_ps[:], op0=ALU.mult, op1=ALU.add).then_inc(S["r1_ok"], 1)

            LN_STEPS = 4

            def layer_norm(t):
                dve.wait_ge(S["r1_ok"], t + 1)
                step, n = steps("ln_step", LN_STEPS * t)
                dve.bn_stats(stat[:, 0, :], r1[:, 0:BANK])
                step(dve.bn_stats(stat[:, 1, :], r1[:, BANK:D]))
                dve.bn_aggr(mv[:], stat[:]).then_inc(S["var_ok"], 1)
                dve.wait_ge(S["std_ok"], t + 1)
                step(dve.reciprocal(rstd[:], std[:]))
                step(dve.tensor_scalar(xn[:], r1[:], mv[:, 0:1], rstd[:, 0:1], ALU.subtract, ALU.mult))
                if static(t) and t == 0:
                    dve.wait_ge(S["c_loads"], 64)
                step(dve.tensor_tensor(xg1[:], xn[:], g1[:], ALU.mult))
                assert n[0] == LN_STEPS
                if not (static(t) and t == 0):
                    dve.wait_ge(S["x1_stored"], 16 * t)
                    dve.wait_ge(S["x1t_ps"], t)
                dve.tensor_tensor(x1[:], xg1[:], b1[:], ALU.add).then_inc(S["x1_ok"], 1)

            def x1t_lo_of(t):
                dve.wait_ge(S["x1t_hi_ok"], t + 1)
                dve.tensor_tensor(x1t_lo[:], k_ps[:].rearrange("p (c t) -> p c t", c=DC), x1t_hi[:], ALU.subtract).then_inc(S["x1t_lo_ok"], 1)

            ROUTE_STEPS = 15

            def route(t):
                step, n = steps("route_step", ROUTE_STEPS * t)
                dve.wait_ge(S["ex_ok"], t + 1)
                step(dve.tensor_scalar(ex1[:], ex[:], 1.0, None, ALU.add))
                step(dve.reciprocal(score[:], ex1[:]))
                step(dve.tensor_tensor(sel[:], score[:], rb[:], ALU.add))
                for g in range(GROUPS):
                    i = dve.max(top_g[:, g, :], sel[:, g * GE:(g + 1) * GE])
                step(i)
                step(dve.tensor_tensor(gsum[:], top_g[:, :, 0], top_g[:, :, 1], ALU.add))
                step(dve.max(gsort[:], gsum[:]))
                step(dve.tensor_copy(gtop[:, 0:TOP_GROUPS], gsort[:, 0:TOP_GROUPS]))
                step(dve.match_replace(gleft[:], gtop[:], gsum[:], OUT))
                step(dve.tensor_scalar(gpen[:], gleft[:], OUT / 2, NEVER, ALU.is_ge, ALU.mult))
                step(dve.tensor_tensor(selm[:].rearrange("p (g e) -> p g e", g=GROUPS), sel[:].rearrange("p (g e) -> p g e", g=GROUPS),
                                       gpen[:, :, None].to_broadcast([P, GROUPS, GE]), ALU.add))
                step(dve.max(top8[:], selm[:]))
                step(dve.match_replace(left[:], top8[:], selm[:], OUT))
                step(dve.tensor_scalar(chosen[:], left[:], OUT / 2, None, ALU.is_lt))
                if not (static(t) and t == 0):
                    dve.wait_ge(S["pos_ps"], t)
                dve.tensor_copy(chosen_b[:], chosen[:]).then_inc(S["chosen_ok"], 1)
                step(dve.tensor_tensor_reduce(out=wraw[:], in0=score[:], in1=chosen[:], scale=1.0, scalar=0.0, op0=ALU.mult,
                                              op1=ALU.add, accum_out=wsum[:]))
                step(dve.reciprocal(wrec[:], wsum[:]))
                assert n[0] == ROUTE_STEPS
                if not (static(t) and t == 0):
                    dve.wait_ge(S["wts_stored"], 16 * t)
                dve.tensor_scalar(wts[:], wraw[:], wrec[:, 0:1], ROUTED_SCALE, ALU.mult, ALU.mult).then_inc(S["wts_ok"], 1)

            POS_STEPS = 7

            def place(t):
                step, n = steps("pos_step", POS_STEPS * t)
                dve.wait_ge(S["pos_ps"], t + 1)
                step(dve.tensor_tensor(pos[:], banks[1][:, 0:E], base[:], ALU.add))
                ins = dve.tensor_tensor(base[:], base[:], banks[1][:, E:2 * E], ALU.add)
                ins.then_inc(S["route0"], 1)
                dve.wait_ge(S["route0"], t + 1)
                dve.tensor_scalar(pos_m[:], pos[:], P - 1, None, ALU.bitwise_and)
                step(dve.tensor_scalar(pos_q[:], pos[:], P.bit_length() - 1, None, ALU.logical_shift_right))
                step(dve.tensor_tensor(pos_b[:], pos_q[:], e8[:], ALU.add))
                step(dve.scalar_tensor_tensor(out=dest[:], in0=pos_m[:], scalar=float(TAB), in1=pos_b[:], op0=ALU.mult, op1=ALU.add))
                step(dve.tensor_scalar(dest[:], dest[:], 1.0, None, ALU.add))
                step(dve.tensor_tensor(dest1[:], dest[:], chosen[:], ALU.mult))
                step(dve.max(dest8[:], dest1[:]))
                assert n[0] == POS_STEPS
                if not (static(t) and t == 0):
                    dve.wait_ge(S["listed"], 16 * TOP_K * t)
                dve.tensor_scalar(dest_i[:], dest8[:], -1.0, None, ALU.add).then_inc(S["dest_ok"], 1)

            dve.wait_ge(S["c_const"], 8)
            dve.memset(eps[:], LN_EPS).then_inc(S["var_ok"], 1)
            heads_lo(0)
            dve.wait_ge(S["c_loads"], 64)
            dve.wait_ge(S["wr_ok"], 1)
            dve.tensor_tensor(wr_lo[:], wr[:], wr_hi[:], ALU.subtract).then_inc(S["wr_ok"], 1)
            residual(0)
            heads_lo(1)
            layer_norm(0)
            residual(1)
            heads_lo(2)
            x1t_lo_of(0)
            layer_norm(1)
            route(0)
            for t in range(2, TT - 1):
                residual(t)
                heads_lo(t + 1)
                x1t_lo_of(t - 1)
                place(t - 2)
                layer_norm(t)
                route(t - 1)
            t = TT - 1
            residual(t)
            x1t_lo_of(t - 1)
            place(t - 2)
            layer_norm(t)
            route(t - 1)
            x1t_lo_of(t)
            place(t - 1)
            route(t)
            place(t)

            step, n = steps("pos_step", POS_STEPS * TT)
            u, v = nblk[0], nblk[1]
            step(dve.tensor_scalar(nblk_i[0][:], base[0:1, :], float(P - 1), None, ALU.add))
            step(dve.tensor_scalar(nblk_i[1][:], nblk_i[0][:], P.bit_length() - 1, None, ALU.logical_shift_right))
            step(dve.tensor_scalar(u[:], nblk_i[1][:], -1.0, 0.0, ALU.add, ALU.max))
            dve.tensor_copy(further[:], u[:]).then_inc(S["extra_ok"], 1)
            shift = 1
            while shift < E:
                step(dve.tensor_copy(v[:, 0:shift], u[:, 0:shift]))
                step(dve.tensor_tensor(v[:, shift:E], u[:, shift:E], u[:, 0:E - shift], ALU.add))
                u, v = v, u
                shift *= 2
            step(dve.memset(earlier[:], 0))
            dve.tensor_copy(earlier[:, 1:E + 1], u[:]).then_inc(S["extra_ok"], 1)
            dve.wait_ge(S["extra_ok"], 2)

            def w_low(which, hi_ok, lo_ok, w, n, k):
                raw, hi, lo = which(w, k)
                dve.wait_ge(S[hi_ok], n + k + 1)
                dve.tensor_tensor(lo, raw, hi, ALU.subtract).then_inc(S[lo_ok], 1)

            for k in range(G_PIECES):
                w_low(g_piece, "g_hi_ok", "g_lo_ok", 0, 0, k)
            for k in range(D_PIECES):
                w_low(d_piece, "d_hi_ok", "d_lo_ok", 0, 0, k)
            dve.wait_ge(S["listed"], 16 * TT * TOP_K)
            dve.wait_ge(S["wts_stored"], 16 * TT)
            dve.wait_ge(S["x1_stored"], 16 * TT)
            dve.wait_ge(S["ax_stored"], 16 * TT)
            dve.sem_inc(S["x_w_ok"], 1)

            def rows_lo(s, ps, wait, n, done):
                dve.wait_ge(S[wait], n)
                dve.tensor_tensor(xb_lo[s][:], ps[:].rearrange("p (c t) -> p c t", c=DC), xb_hi[s][:], ALU.subtract).then_inc(S[done], 1)

            def h_of(b):
                dve.wait_ge(S["silu_ok"], b + 1)
                dve.tensor_tensor(hh[:], sg[:], banks[0][:, FF:2 * FF], ALU.mult).then_inc(S["h_ok"], 1)

            def h_lo(b):
                dve.wait_ge(S["ht_hi_ok"], b + 1)
                dve.tensor_tensor(ht_lo[:], banks[1][:, 0:FF].rearrange("p (c t) -> p c t", c=FC), ht_hi[:], ALU.subtract).then_inc(S["ht_lo_ok"], 1)

            def token_weights(i, e, b, done):
                dve.wait_ge(S["scaled"], b - 1)
                stand(dve)
                dve.tensor_copy(wcol[i][:], xg[i][:, ds(D + e, 1)]).then_inc(S[done], 1)

            rows_lo(0, q_ps, "rows_hi_ok", 1, "rows_lo_ok")
            for b in range(SH):
                if b >= 1:
                    h_lo(b - 1)
                if b == SH - 1:
                    for k in range(G_PIECES):
                        w_low(g_piece, "g_hi_ok", "g_lo_ok", 1, G_PIECES, k)
                h_of(b)
                rows_lo((b + 1) % 2, q_ps, "rows_hi_ok", b + 2, "rows_lo_ok")

            def expert(e, par, last=False):
                xi = dve.value_load(earlier[0:1, ds(e, 1)], min_val=0, max_val=E * TAB_BLOCKS)
                b0 = xi + e + SH
                nx = dve.value_load(further[0:1, ds(e, 1)], min_val=0, max_val=TAB_BLOCKS - 1)
                h_lo(b0 - 1)
                token_weights(par, e, b0, "w_ok")
                if not last:
                    for k in range(G_PIECES - 1):
                        w_low(g_piece, "g_hi_ok", "g_lo_ok", par, G_PIECES * (e + 2), k)
                h_of(b0)
                with dve.If(nx > 0):
                    rows_lo(2, out_ps, "x_rows_hi_ok", xi + 1, "x_rows_lo_ok")
                if not last:
                    w_low(g_piece, "g_hi_ok", "g_lo_ok", par, G_PIECES * (e + 2), G_PIECES - 1)
                    rows_lo(1 - par, q_ps, "rows_hi_ok", SH + e + 2, "rows_lo_ok")
                for k in range(D_PIECES):
                    w_low(d_piece, "d_hi_ok", "d_lo_ok", 1 - par, D_PIECES * (e + 1), k)
                with dve.If(nx > 0):
                    h_lo(b0)
                    token_weights(2, e, b0 + 1, "x_w_ok")
                    h_of(b0 + 1)
                    with dve.If(nx > 1):
                        with dve.Fori(1, nx) as k:
                            h_lo(b0 + k)
                            rows_lo(2, out_ps, "x_rows_hi_ok", xi + k + 1, "x_rows_lo_ok")
                            token_weights(2, e, b0 + k + 2, "x_w_ok")
                            h_of(b0 + k + 1)
                return b0, nx
            with dve.Fori(0, E // 2 - 1) as i:
                for par in range(2):
                    expert(2 * i + par, par)
            expert(E - 2, 0)
            b0, nx = expert(E - 1, 1, last=True)
            h_lo(b0 + nx)

            step, n = steps("f_step", 0)
            dve.wait_ge(S["summed"], 1)
            dve.memset(feps[:], LN_EPS).then_inc(S["f_var"], 1)
            for t in range(TT + 1):
                i = t % 2
                if t < TT:
                    dve.wait_ge(S["f_part"], t + 1)
                    dve.tensor_tensor(fin[0][:, t], fin[0][:, t], fin[1][:, t], ALU.add).then_inc(S["f_sum"], 1)
                    dve.wait_ge(S["f_sum"], t + 1)
                    dve.bn_stats(fstat[i][:, 0, :], fin[0][:, t, 0:BANK])
                    step(dve.bn_stats(fstat[i][:, 1, :], fin[0][:, t, BANK:D]))
                    if t >= 2:
                        dve.wait_ge(S["f_norm"], t - 1)
                    dve.bn_aggr(fmv[i][:], fstat[i][:]).then_inc(S["f_var"], 1)
                if t >= 1:
                    if t == 1:
                        dve.wait_ge(S["g2_in"], 32)
                    dve.wait_ge(S["f_norm"], t)
                    dve.tensor_tensor(fin[1][:, t - 1], fin[1][:, t - 1], g2[:], ALU.mult).then_inc(S["f_g"], 1)
                    dve.wait_ge(S["f_g"], t)
                    dve.tensor_tensor(fin[2][:, t - 1], fin[1][:, t - 1], b2[:], ALU.add).then_inc(S["f_out"], 1)
                if t < TT:
                    dve.wait_ge(S["f_std"], t + 1)
                    step(dve.reciprocal(frstd[i][:], fstd[i][:]))
                    dve.scalar_tensor_tensor(out=fnm[i][:], in0=fmv[i][:, 0:1], scalar=-1.0, in1=frstd[i][:], op0=ALU.mult,
                                             op1=ALU.mult).then_inc(S["f_mv"], 1)


_INS = ["x", "fox_w_in", "fox_b_f", "fox_w_out", "ln1_g", "ln1_b", "moe_router", "moe_router_bias", "moe_w_gate", "moe_w_up",
        "moe_w_down", "moe_ws_gate", "moe_ws_up", "moe_ws_down", "ln2_g", "ln2_b"]
_ROWS = {"fox_b_f", "ln1_g", "ln1_b", "moe_router_bias", "ln2_g", "ln2_b"}


def kernel(**inputs):
    import numpy as _np
    import concourse.bacc as _bacc
    from concourse import mybir as _mybir
    from concourse.bass_utils import run_bass_kernel_spmd as _run

    nc = _bacc.Bacc("TRN2", target_bir_lowering=False, num_devices=1)
    arrays, args = {}, []
    for name in _INS:
        a = _np.ascontiguousarray(inputs[name])
        if name not in _ROWS:
            a = a[0]
        arrays[f"in_{name}_dram"] = a
        args.append(nc.dram_tensor(f"in_{name}_dram", a.shape, _mybir.dt.from_np(a.dtype), kind="ExternalInput").ap())
    args.append(nc.dram_tensor("out_dram", (T, D), F32, kind="ExternalOutput").ap())
    build(nc, *args)
    r = _run(nc, [arrays], core_ids=[0])
    return r.results[0]["out_dram"].reshape(1, T, D)
```

```python
from contextlib import ExitStack

import concourse.bass as bass
from concourse import mybir

P = 128
BANK = 512
ALU = mybir.AluOpType
ACT = mybir.ActivationFunctionType
F32 = mybir.dt.float32
F32R = mybir.dt.float32r
BF16 = mybir.dt.bfloat16
AX_X = mybir.AxisListType.X
NEVER = -1e30

T, D, HEADS, DH = 1024, 1024, 16, 64
TT = T // P
DC = D // P
PAIRS = HEADS // 2
VC = 256
NVC = D // VC
ONE_ROW, MAX_ROW = 64, 96
SCALE = DH ** -0.5

BY_QUERY = [(t, k0, min(BANK, (t + 1) * P - k0)) for t in range(TT) for k0 in range(0, (t + 1) * P, BANK)]
BY_KEY = []
for _t in range(TT):
    for _q0, _q1 in ((_t * P, BANK), (max(_t * P, BANK), T)):
        if _q0 < _q1:
            BY_KEY.append((_t, _q0, _q1 - _q0, sum(b[2] for b in BY_KEY)))
PROBS = sum(b[2] for b in BY_KEY)
NQ, NR, NK = len(BY_QUERY), 2, len(BY_KEY)
SLOTS = NQ + NR + NK
SLOT_BANK = [[(n + 2) % 4 for n in range(NQ)] + [n % 2 for n in range(NR)] + [n % (4, 2)[par] for n in range(NK)]
             for par in range(2)]
OUT_QUERIES = max(n for n in range(NQ) if SLOT_BANK[0][n] >= 2) + 1


ALPHA = 2.0 ** 0.25
LN_EPS = 1e-5
E, GROUPS, TOP_GROUPS, TOP_K, FF = 64, 8, 4, 8, 256
GE = E // GROUPS
ROUTED_SCALE = 2.5
FC = FF // P
TAB_BLOCKS = T // P
TAB = E * TAB_BLOCKS
ROWS = T + P
ROW_W = D + E
STAGES = 6
OUT = -3e38
I32 = mybir.dt.int32
U32 = mybir.dt.uint32


def split_matmul(pe, out, w_hi, w_lo, m_hi, m_lo, start, stop):
    pe.matmul(out, w_hi, m_hi, start=start, stop=False, skip_group_check=True)
    pe.matmul(out, w_hi, m_lo, start=False, stop=False, skip_group_check=True)
    return pe.matmul(out, w_lo, m_hi, start=False, stop=stop, skip_group_check=True)


def build(nc, x, w_in, b_f, w_out, ln1_g, ln1_b, router, router_bias, w_gate, w_up, w_down, ws_gate, ws_up,
          ws_down, ln2_g, ln2_b, out):
    with ExitStack() as ctx:
        def sem(n):
            return ctx.enter_context(nc.semaphore(n))

        def sb(n, s, d=F32, c=ctx):
            return c.enter_context(nc.sbuf_tensor(n, s, d))

        banks = [ctx.enter_context(nc.psum_tensor(f"bank{i}", [P, BANK], F32)) for i in range(2)]
        out_ps = ctx.enter_context(nc.psum_tensor("out_ps", [P, T], F32))
        q_ps = ctx.enter_context(nc.psum_tensor("q_ps", [P, T], F32))
        k_ps = ctx.enter_context(nc.psum_tensor("k_ps", [P, T], F32))

        slot_banks = [banks[0][:], banks[1][:], out_ps[:, 0:BANK], out_ps[:, BANK:T]]
        v_dram = nc.dram_tensor("v_scratch", (T, D), F32, kind="Internal").ap()
        c_dram = nc.dram_tensor("c_scratch", (2, HEADS, T), F32, kind="Internal").ap()

        rows_dram = nc.dram_tensor("rows_scratch", (ROWS, ROW_W), F32, kind="Internal").ap()
        sums = [nc.dram_tensor(f"sums_scratch{i}", (ROWS, D), F32, kind="Internal").ap() for i in range(3)]
        tab_dram = nc.dram_tensor("tab_scratch", (P * TAB, 1), I32, kind="Internal").ap()

        ident = sb("ident", [P, P])
        identb = sb("identb", [P, P], BF16)
        mask_qk = sb("mask_qk", [P, P], BF16)
        mask_kq = sb("mask_kq", [P, P], BF16)
        ones_b = sb("ones_b", [P, P], BF16)
        before = sb("before", [P, P], BF16)
        further = sb("further", [1, E], I32)
        earlier = sb("earlier", [1, E + 1], I32)
        with ExitStack() as early:
            attn = sb("xs", [P, PAIRS, T], c=early)
            xs = attn
            with ExitStack() as x1s:
                xt_hi = sb("xt_hi", [P, DC, T], F32R, c=x1s)
                xt_lo = sb("xt_lo", [P, DC, T], F32R, c=x1s)
                wqk = sb("wqk", [P, DC, 2, P], c=x1s)
                wqk_hi = sb("wqk_hi", [P, DC, 2, P], F32R, c=x1s)
                wqk_lo = sb("wqk_lo", [P, DC, 2, P], F32R, c=x1s)
                with ExitStack() as a:
                    wv = sb("wv", [P, 2, DC, VC], c=a)
                    wv_hi = sb("wv_hi", [P, 2, DC, VC], F32R, c=a)
                    wv_lo = sb("wv_lo", [P, 2, DC, VC], F32R, c=a)
                    v_out = sb("v_out", [P, 2, 2, VC], c=a)
                    wf = sb("wf", [P, DC, HEADS], c=a)
                    wf_hi = sb("wf_hi", [P, DC, HEADS], F32R, c=a)
                    wf_lo = sb("wf_lo", [P, DC, HEADS], F32R, c=a)
                    bf = sb("bf", [P, HEADS], c=a)
                    z = sb("z", [P, TT, HEADS], c=a)
                    zabs = sb("zabs", [P, TT, HEADS], c=a)
                    zexp = sb("zexp", [P, TT, HEADS], c=a)
                    zlog = sb("zlog", [P, TT, HEADS], c=a)
                    zmin = sb("zmin", [P, TT, HEADS], c=a)
                    gate8 = sb("gate8", [P, TT, HEADS], c=a)
                    upto = sb("upto", [P, T], c=a)
                    c_hi = sb("c_hi", [HEADS, T], F32R, c=a)
                    c_lo = sb("c_lo", [HEADS, T], F32R, c=a)
                with ExitStack() as b:
                    q_hi = [sb(f"q_hi{i}", [P, T], F32R, c=b) for i in range(2)]
                    q_lo = [sb(f"q_lo{i}", [P, T], F32R, c=b) for i in range(2)]
                    k_hi = [sb(f"k_hi{i}", [P, T], F32R, c=b) for i in range(2)]
                    k_lo = [sb(f"k_lo{i}", [P, T], F32R, c=b) for i in range(2)]
                    va = [sb(f"va{i}", [P, TT, P], c=b) for i in range(2)]
                    probs = sb("probs", [P, PROBS], c=b)
                    mx2 = sb("mx2", [P, TT, 2], c=b)
                    mx = sb("mx", [P, TT], c=b)
                    rec = sb("rec", [DH, T], c=b)
            with ExitStack() as d:
                wo_hi = sb("wo_hi", [P, DC, D], F32R, c=d)
                wo_lo = sb("wo_lo", [P, DC, D], F32R, c=d)
                wo = sb("wo", [P, STAGES, D], c=d)
                ot_hi = [sb(f"ot_hi{i}", [P, DC, P], F32R, c=d) for i in range(2)]
                ot_lo = [sb(f"ot_lo{i}", [P, DC, P], F32R, c=d) for i in range(2)]
                x_res = sb("x_res", [P, D], c=d)
                r1 = sb("r1", [P, D], c=d)
                xn = sb("xn", [P, D], c=d)
                xg1 = sb("xg1", [P, D], c=d)
                x1 = sb("x1", [P, D], c=d)
                ax = sb("ax", [P, D], c=d)
                x1t_hi = sb("x1t_hi", [P, DC, P], F32R, c=d)
                x1t_lo = sb("x1t_lo", [P, DC, P], F32R, c=d)
                g1 = sb("g1", [P, D], c=d)
                b1 = sb("b1", [P, D], c=d)
                wr = sb("wr", [P, DC, E], c=d)
                wr_hi = sb("wr_hi", [P, DC, E], F32R, c=d)
                wr_lo = sb("wr_lo", [P, DC, E], F32R, c=d)
                rb = sb("rb", [P, E], c=d)
                stat = sb("stat", [P, 2, 6], c=d)
                mv = sb("mv", [P, 2], c=d)
                rstd = sb("rstd", [P, 1], c=d)
                std = sb("std", [P, 1], c=d)
                eps = sb("eps", [P, 1], c=d)
                ex = sb("ex", [P, E], c=d)
                ex1 = sb("ex1", [P, E], c=d)
                score = sb("score_e", [P, E], c=d)
                sel = sb("sel", [P, E], c=d)
                top_g = sb("top_g", [P, GROUPS, 8], c=d)
                gsum = sb("gsum", [P, GROUPS], c=d)
                gsort = sb("gsort", [P, GROUPS], c=d)
                gtop = sb("gtop", [P, GROUPS], c=d)
                gleft = sb("gleft", [P, GROUPS], c=d)
                gpen = sb("gpen", [P, GROUPS], c=d)
                selm = sb("selm", [P, E], c=d)
                top8 = sb("top8", [P, 8], c=d)
                left = sb("left", [P, E], c=d)
                chosen = sb("chosen", [P, E], c=d)
                chosen_b = sb("chosen_b", [P, E], BF16, c=d)
                wraw = sb("wraw", [P, E], c=d)
                wsum = sb("wsum", [P, 1], c=d)
                wrec = sb("wrec", [P, 1], c=d)
                wts = sb("wts", [P, E], c=d)
                base = sb("base", [P, E], c=d)
                pos = sb("pos", [P, E], I32, c=d)
                pos_m = sb("pos_m", [P, E], I32, c=d)
                pos_q = sb("pos_q", [P, E], I32, c=d)
                pos_b = sb("pos_b", [P, E], c=d)
                dest = sb("dest", [P, E], c=d)
                dest1 = sb("dest1", [P, E], c=d)
                dest8 = sb("dest8", [P, 8], c=d)
                dest_i = sb("dest_i", [P, 8], I32, c=d)
                e8 = sb("e8", [P, E], c=d)
                tok_all = sb("tok_all", [P, TT], I32, c=d)
                tok = sb("tok", [P, 1], I32, c=d)
                tab0 = sb("tab0", [P, TAB], I32, c=d)
                zeros = sb("zeros", [P, ROW_W], c=d)
                nblk = [sb(f"nblk{i}", [1, E], c=d) for i in range(2)]
                nblk_i = [sb(f"nblk_i{i}", [1, E], I32, c=d) for i in range(2)]
        with ExitStack() as m:
            raw_gu = [sb(f"raw_gu{i}", [P, 2, DC, FF], c=m) for i in range(2)]
            raw_dn = [sb(f"raw_dn{i}", [P, FC, D], c=m) for i in range(2)]
            xg = [sb(f"x_rows{i}", [P, ROW_W], c=m) for i in range(3)]
            xb_hi = [sb(f"xb_hi{i}", [P, DC, P], F32R, c=m) for i in range(3)]
            xb_lo = [sb(f"xb_lo{i}", [P, DC, P], F32R, c=m) for i in range(3)]
            ys = [sb(f"ys{i}", [P, D], c=m) for i in range(3)]
            sg = sb("sg", [P, FF], c=m)
            hh = sb("hh", [P, FF], c=m)
            ht_hi = sb("ht_hi", [P, FC, P], F32R, c=m)
            ht_lo = sb("ht_lo", [P, FC, P], F32R, c=m)
            wcol = [sb(f"wcol{i}", [P, 1], c=m) for i in range(3)]
            tab = sb("tab", [P, TAB], I32, c=m)
            gidx = [sb(f"gidx{i}", [P, 1], I32, c=m) for i in range(3)]
            sidx = [sb(f"sidx{i}", [P, 1], I32, c=m) for i in range(3)]
            split = []
            for i in range(2):
                split.append((sb(f"gu_hi{i}", [P, 2, DC, FF], F32R, c=m), sb(f"gu_lo{i}", [P, 2, DC, FF], F32R, c=m),
                              sb(f"dn_hi{i}", [P, FC, D], F32R, c=m), sb(f"dn_lo{i}", [P, FC, D], F32R, c=m)))
        with ExitStack() as f:
            fin0 = sb("fin0", [P, TT, D], c=f)
            fin2 = sb("fin2", [P, TT, D], c=f)
            g2 = sb("g2", [P, D], c=f)
            b2 = sb("b2", [P, D], c=f)
            fstat = [sb(f"fstat{i}", [P, 2, 6], c=f) for i in range(2)]
            fmv = [sb(f"fmv{i}", [P, 2], c=f) for i in range(2)]
            feps = sb("feps", [P, 1], c=f)
            fstd = [sb(f"fstd{i}", [P, 1], c=f) for i in range(2)]
            frstd = [sb(f"frstd{i}", [P, 1], c=f) for i in range(2)]
            fnm = [sb(f"fnm{i}", [P, 1], c=f) for i in range(2)]

        SH = TT
        G_PIECES, D_PIECES = 4, 2
        S = {}
        for n in ("consts masks xt_ps xt_hi_ok xt_lo_ok wf_in wf_ok bf_in z_ps z_ok zabs_ok zexp_ok zlog_ok zmin_ok gate_ok"
                  " c_ps c_hi_ok c_lo_ok c_stored wv_hi_ok wv_lo_ok v_ps v_ok aug aug0 mx20"
                  " wqk_in wqk_hi_ok wqk_lo_ok proj score maxed mx_ok r_hi r_lo exped pv rec_ok normed"
                  " wo_hi_ok wo_lo_ok c_loads wr_ok ot_hi_ok ot_lo_ok oproj r1_ok ln_step x1_ok x_res_in x1_stored wts_stored"
                  " x1t_ps x1t_hi_ok x1t_lo_ok logit_ps ex_ok route_step chosen_ok wts_ok pos_ps pos_step dest_ok c_const c_fill"
                  " tok_ok listed route0 extra_ok"
                  " g_hi_ok g_lo_ok d_hi_ok d_lo_ok tab_in started gated turned rows_hi_ok rows_lo_ok silu_ok h_ok ht_ps ht_hi_ok"
                  " ht_lo_ok downed scaled w_ok x_in x_turned x_rows_hi_ok x_rows_lo_ok x_w_ok ax_ok ax_stored summed"
                  " stands g2_in std_ok var_ok f_part set_free f_sum f_var f_std f_step f_mv f_norm f_g f_out").split():
            S[n] = sem(n)
        tile_in = [sem(f"tile_in{t}") for t in range(TT)]
        wv_in = [sem(f"wv_in{i}") for i in range(2)]
        v_stored = [sem(f"v_stored{i}") for i in range(2)]
        c_in = [sem(f"c_in{i}") for i in range(2)]
        va_in = [sem(f"va_in{i}") for i in range(2)]
        ev_hi = [sem(f"ev_hi{i}") for i in range(2)]
        ev_lo = [sem(f"ev_lo{i}") for i in range(2)]
        wo_in = [sem(f"wo_in{i}") for i in range(STAGES)]
        g_raw = [[sem(f"g_raw{i}_{k}") for k in range(G_PIECES)] for i in range(2)]
        d_raw = [sem(f"d_raw{i}") for i in range(2)]
        rows_in = [sem(f"rows_in{i}") for i in range(2)]
        got = [sem(f"got{i}") for i in range(2)]
        sent = [sem(f"sent{i}") for i in range(3)]
        LAST_PARTS = 4
        NORMED = HEADS - 1 + LAST_PARTS
        SENT_0 = (16 * SH // 2, 16 * SH // 2, 16 * ROWS // P)
        stored = sem("stored")

        w_rows = w_in.rearrange("(c p) n -> p c n", p=P)
        v_rows = v_dram.rearrange("(t p) n -> p t n", p=P)
        NXT = DC * 2
        idx_ok = [sem(f"gidx_ok{i}") for i in range(3)]
        S["sidx_ok"] = sem("sidx_ok")

        def load_wqk(sp, p):
            for j in range(2):
                sp.dma_start(wqk[:, :, j, :], w_rows[:, :, bass.ds(j * D + p * P, P)]).then_inc(S["wqk_in"], 16)

        def load_c(sp, p, par):
            for j, k in enumerate((k_hi[par], k_lo[par])):
                sp.dma_start(k[ONE_ROW:ONE_ROW + 1, :].bitcast(F32), c_dram[j, bass.ds(2 * p + par, 1), :]).then_inc(c_in[par], 16)

        def load_v(sp, p, par):
            sp.dma_start(va[par][:, :, 0:DH], v_rows[:, :, bass.ds((2 * p + par) * DH, DH)]).then_inc(va_in[par], 16)

        ds = bass.ds

        def g_piece(w, k):
            return tuple(a[:, k // 2, (k % 2) * 4:(k % 2) * 4 + 4, :] for a in (raw_gu[w], split[w][0], split[w][1]))

        def d_piece(w, k):
            return tuple(a[:, k, :] for a in (raw_dn[w], split[w][2], split[w][3]))

        def fin1(t):
            return split[1][t // 4][:, t % 4 // 2, t % 2 * 4:t % 2 * 4 + 4, :].bitcast(F32).rearrange("p c n -> p (c n)")

        def strided(a):
            return a.rearrange("p (k c) -> p c k", k=P)

        def is_last(e):
            return isinstance(e, int) and e == E - 1

        def static(e):
            return isinstance(e, int)

        def stand(eng):
            eng.sem_inc(S["stands"], 1)

        block = ctx.enter_context(nc.Block())

        @block.sync
        def _(sp):
            for t in range(TT):
                sp.dma_start(xs[:, t, :], x[t * P:(t + 1) * P, :]).then_inc(tile_in[t], 16)
            sp.dma_start(wf[:], w_rows[:, :, 3 * D:3 * D + HEADS]).then_inc(S["wf_in"], 16)
            sp.dma_start(bf[:], b_f.to_broadcast([P, HEADS])).then_inc(S["bf_in"], 16)
            for n in range(NVC):
                if n >= 2:
                    sp.wait_ge(S["wv_lo_ok"], n - 1)
                sp.dma_start(wv[:, n % 2], w_rows[:, :, 2 * D + n * VC:2 * D + (n + 1) * VC]).then_inc(wv_in[n % 2], 16)
            load_wqk(sp, 0)
            for n in range(NVC * TT // 2):
                sp.wait_ge(S["v_ok"], n + 1)
                c, t = n // (TT // 2), n % (TT // 2)
                sp.dma_start(v_rows[:, 2 * t:2 * t + 2, c * VC:(c + 1) * VC], v_out[:, n % 2]).then_inc(v_stored[n % 2], 16)
            sp.wait_ge(S["c_lo_ok"], 2)
            sp.dma_start(c_dram[0], c_hi[:].bitcast(F32)).then_inc(S["c_stored"], 16)
            sp.dma_start(c_dram[1], c_lo[:].bitcast(F32)).then_inc(S["c_stored"], 16)
            sp.wait_ge(S["c_stored"], 32)
            for i in range(2):
                sp.wait_ge(v_stored[i], 16 * NVC * TT // 4)
            sp.wait_ge(S["wqk_lo_ok"], 1)
            load_wqk(sp, 1)
            sp.wait_ge(S["aug"], 2)
            for par in range(2):
                load_c(sp, 0, par)
                load_v(sp, 0, par)

            def pair(p):
                sp.wait_ge(S["score"], SLOTS * (2 * p + 1))
                load_c(sp, p + 1, 0)
                sp.wait_ge(S["pv"], 2 * p + 1)
                load_v(sp, p + 1, 0)
                sp.wait_ge(S["score"], SLOTS * (2 * p + 2))
                load_c(sp, p + 1, 1)
                sp.wait_ge(S["pv"], 2 * p + 2)
                load_v(sp, p + 1, 1)
            with sp.Fori(0, PAIRS - 2) as p:
                sp.wait_ge(S["wqk_lo_ok"], p + 2)
                load_wqk(sp, p + 2)
                pair(p)
            pair(PAIRS - 2)

            sp.wait_ge(S["proj"], PAIRS)
            for c in range(DC):
                if c >= STAGES:
                    sp.wait_ge(S["wo_lo_ok"], c - STAGES + 1)
                sp.dma_start(wo[:, c % STAGES], w_out[c * P:(c + 1) * P, :]).then_inc(wo_in[c % STAGES], 16)
            sp.wait_ge(S["pv"], HEADS)
            sp.dma_start(x_res[:], x[0:P, :]).then_inc(S["x_res_in"], 16)
            sp.wait_ge(S["normed"], NORMED)
            sp.dma_start(g1[:], ln1_g.to_broadcast([P, D])).then_inc(S["c_loads"], 16)
            sp.dma_start(b1[:], ln1_b.to_broadcast([P, D])).then_inc(S["c_loads"], 16)
            sp.dma_start(wr[:], router.rearrange("(c p) n -> p c n", p=P)).then_inc(S["c_loads"], 16)
            sp.dma_start(rb[:], router_bias.to_broadcast([P, E])).then_inc(S["c_loads"], 16)

            def tile(t):
                if not (static(t) and t == TT - 1):
                    sp.wait_ge(S["r1_ok"], t + 1)
                    sp.dma_start(x_res[:], x[ds(t * P + P, P), :]).then_inc(S["x_res_in"], 16)
                sp.wait_ge(S["x1_ok"], t + 1)
                sp.dma_start(rows_dram[ds(t * P, P), 0:D], x1[:]).then_inc(S["x1_stored"], 16)
                sp.wait_ge(S["ax_ok"], t + 1)
                sp.dma_start(sums[0][ds(t * P, P), :], ax[:]).then_inc(S["ax_stored"], 16)

            def weights_out(t):
                sp.wait_ge(S["wts_ok"], t + 1)
                sp.dma_start(rows_dram[ds(t * P, P), D:ROW_W], wts[:]).then_inc(S["wts_stored"], 16)
            tile(0)
            with sp.Fori(1, TT - 2) as t:
                tile(t)
                weights_out(t - 1)

            def load_gate_up(par, gate, up, left):
                for k in range(G_PIECES):
                    left(k)
                    chunks = slice(k % 2 * (DC // 2), (k % 2 + 1) * (DC // 2))
                    w = (gate, up)[k // 2].rearrange("(p c) n -> p c n", c=DC)[:, chunks]
                    sp.dma_start(raw_gu[par][:, k // 2, chunks], w).then_inc(g_raw[par][k], 16)

            def load_down(par, down, left):
                for k in range(D_PIECES):
                    left(k)
                    sp.dma_start(raw_dn[par][:, k], down.rearrange("(p c) n -> p c n", c=FC)[:, k]).then_inc(d_raw[par], 16)

            def next_gate_up(s, par):
                load_gate_up(par, *(w[ds(s - 1, 1)].rearrange("o k n -> (o k) n") for w in (w_gate, w_up)),
                             lambda k: sp.wait_ge(S["g_lo_ok"], G_PIECES * (s - 2) + k + 1))

            def next_down(s, par):
                load_down(par, w_down[ds(s - 1, 1)].rearrange("o k n -> (o k) n"),
                          lambda k: sp.wait_ge(S["d_lo_ok"], D_PIECES * (s - 2) + k + 1))

            def free(k):
                pass

            def load_rows(b):
                sp.dma_start(xg[b % 2][:, 0:D], rows_dram[b * P:(b + 1) * P, 0:D]).then_inc(rows_in[b % 2], 16)

            sp.wait_ge(S["ot_lo_ok"], TT)
            load_gate_up(0, ws_gate, ws_up, free)
            tile(TT - 2)
            weights_out(TT - 3)
            sp.wait_ge(S["oproj"], TT)
            for b in range(2):
                sp.wait_ge(S["x1_stored"], 16 * (b + 1))
                load_rows(b)
            load_down(0, ws_down, free)
            load_gate_up(1, w_gate[0], w_up[0], free)
            load_down(1, w_down[0], free)
            tile(TT - 1)
            weights_out(TT - 2)
            sp.wait_ge(S["x1_stored"], 16 * TT)
            for b in range(2, SH):
                sp.wait_ge(S["turned"], b - 1)
                load_rows(b)
                if b == 4:
                    weights_out(TT - 1)
                elif b == 5:
                    next_gate_up(2, 0)
                elif b == 6:
                    next_down(2, 0)
            sp.wait_ge(S["listed"], 16 * TT * TOP_K)
            sp.wait_ge(S["c_fill"], 64)
            sp.dma_start(tab[:], tab_dram.rearrange("(p n) o -> p (n o)", p=P)).then_inc(S["tab_in"], 16)

            next_gate_up(3, 1)
            with sp.Fori(0, E // 2 - 2) as i:
                for par in range(2):
                    next_gate_up(2 * i + (par + 4), par)
                    next_down(2 * i + (par + 3), 1 - par)
            next_gate_up(E, 0)
            next_down(E - 1, 1)
            next_down(E, 0)
            def load_sums(j, t):
                sp.dma_start((fin0[:, t], fin1(t), fin2[:, t])[j], sums[j][t * P:(t + 1) * P, :]).then_inc(tile_in[t], 16)
            sp.wait_ge(S["g_lo_ok"], G_PIECES * (E + 1))
            sp.wait_ge(sent[0], 8 * E + SENT_0[0])
            for t in range(TT):
                load_sums(0, t)
            sp.wait_ge(sent[1], 8 * (E - 2) + SENT_0[1])
            sp.wait_ge(S["set_free"], 1)
            for t in range(TT):
                if t >= 2:
                    sp.wait_ge(S["f_part"], t - 1)
                load_sums(1, t)
            sp.wait_ge(S["summed"], 1)
            for t in range(TT):
                sp.wait_ge(S["f_part"], t + 1)
                load_sums(2, t)
                if t == 0:
                    sp.dma_start(g2[:], ln2_g.to_broadcast([P, D])).then_inc(S["g2_in"], 16)
                    sp.dma_start(b2[:], ln2_b.to_broadcast([P, D])).then_inc(S["g2_in"], 16)
            for t in range(TT):
                sp.wait_ge(S["f_out"], t + 1)
                sp.dma_start(out[t * P:(t + 1) * P, :], fin2[:, t]).then_inc(stored, 16)
            sp.wait_ge(stored, 16 * TT)

        @block.gpsimd
        def _(pool):
            g = nc.gpsimd
            g.memset(ident[:], 0.0).then_inc(S["consts"], 1)
            g.memset(mask_qk[:], 0.0).then_inc(S["consts"], 1)
            g.memset(mask_kq[:], 0.0).then_inc(S["consts"], 1)
            g.memset(upto[:], 1.0).then_inc(S["consts"], 1)
            pool.wait_ge(S["consts"], 4)
            g.affine_select(out=ident[:], in_=ident[:], compare_op=ALU.not_equal, fill=1.0, base=0,
                            pattern=[[-1, P]], channel_multiplier=1).then_inc(S["masks"], 1)
            pool.wait_ge(S["masks"], 1)
            g.tensor_copy(identb[:], ident[:]).then_inc(S["masks"], 1)
            g.affine_select(out=mask_qk[:], in_=mask_qk[:], compare_op=ALU.is_ge, fill=NEVER, base=0,
                            pattern=[[-1, P]], channel_multiplier=1).then_inc(S["masks"], 1)
            g.affine_select(out=mask_kq[:], in_=mask_kq[:], compare_op=ALU.is_ge, fill=NEVER, base=0,
                            pattern=[[1, P]], channel_multiplier=-1).then_inc(S["masks"], 1)
            g.affine_select(out=upto[:], in_=upto[:], compare_op=ALU.is_ge, fill=0.0, base=0,
                            pattern=[[1, T]], channel_multiplier=-1).then_inc(S["masks"], 1)
            pool.wait_ge(S["v_ok"], NVC * TT // 2)
            for i in range(2):
                pool.wait_ge(v_stored[i], 16 * NVC * TT // 4)
            pool.wait_ge(S["c_stored"], 32)
            pool.wait_ge(S["v_ps"], NVC * TT // 2)
            n = 0
            for par in range(2):
                for buf in (q_hi, q_lo, k_hi, k_lo):
                    g.memset(buf[par][DH:P, :].bitcast(F32), 0.0).then_inc(S["aug0"], 1)
                    n += 1
                    pool.wait_ge(S["aug0"], n)
                g.memset(va[par][:, :, DH:P], 1.0).then_inc(S["aug0"], 1)
                n += 1
                pool.wait_ge(S["aug0"], n)
                g.memset(q_hi[par][ONE_ROW:ONE_ROW + 1, :].bitcast(F32), 1.0).then_inc(S["aug0"], 1)
                n += 1
                pool.wait_ge(S["aug0"], n)
                g.memset(k_hi[par][MAX_ROW:MAX_ROW + 1, :].bitcast(F32), 1.0).then_inc(S["aug"], 1)
                pool.wait_ge(S["aug"], par + 1)
            g.memset(ones_b[:], 1.0).then_inc(S["c_const"], 1)
            pool.wait_ge(S["c_const"], 1)
            g.affine_select(out=before[:], in_=ones_b[:], compare_op=ALU.is_gt, fill=0.0, base=0,
                            pattern=[[1, P]], channel_multiplier=-1).then_inc(S["c_const"], 1)

            pool.wait_ge(S["normed"], NORMED)
            g.iota(e8[:], pattern=[[TAB_BLOCKS, E]], base=0, channel_multiplier=0, allow_small_or_imprecise_dtypes=True).then_inc(S["c_const"], 1)
            g.iota(tok_all[:], pattern=[[P, TT]], base=0, channel_multiplier=1).then_inc(S["c_const"], 1)
            g.iota(tab0[:], pattern=[[0, TAB]], base=T, channel_multiplier=1).then_inc(S["c_const"], 1)
            g.memset(zeros[:], 0.0).then_inc(S["c_const"], 1)
            g.memset(gtop[:], 3e38).then_inc(S["c_const"], 1)
            g.memset(base[:], 0.0).then_inc(S["c_const"], 1)
            pool.wait_ge(S["c_const"], 8)
            pool.dma_start(tab_dram.rearrange("(p n) o -> p (n o)", p=P), tab0[:]).then_inc(S["c_fill"], 16)
            pool.dma_start(rows_dram[T:ROWS, :], zeros[:]).then_inc(S["c_fill"], 16)
            for i in range(2):
                pool.dma_start(sums[i][T:ROWS, :], zeros[:, 0:D]).then_inc(S["c_fill"], 16)
            for t in range(ROWS // P):
                pool.dma_start(sums[2][t * P:(t + 1) * P, :], zeros[:, 0:D]).then_inc(sent[2], 16)
            pool.wait_ge(S["c_fill"], 64)

            def list_tokens(t):
                if not (static(t) and t == 0):
                    pool.wait_ge(S["listed"], 16 * TOP_K * t)
                g.tensor_copy(tok[:], tok_all[:, ds(t, 1)]).then_inc(S["tok_ok"], 1)
                pool.wait_ge(S["tok_ok"], t + 1)
                pool.wait_ge(S["dest_ok"], t + 1)
                for k in range(TOP_K):
                    g.indirect_dma_start(out=tab_dram, out_offset=bass.IndirectOffsetOnAxis(ap=dest_i[:, k:k + 1], axis=0),
                                         in_=tok[:], in_offset=None).then_inc(S["listed"], 16)
            for t in range(TT - 1):
                list_tokens(t)

            def wait_routed():
                pool.wait_ge(S["listed"], 16 * TT * TOP_K)
                pool.wait_ge(S["extra_ok"], 2)
                pool.wait_ge(S["x1_stored"], 16 * TT)
                pool.wait_ge(S["wts_stored"], 16 * TT)

            def gather(i, e, k, count, done):
                stand(pool)
                g.tensor_copy(gidx[i][:], tab[:, ds(e * TAB_BLOCKS + k, 1)]).then_inc(idx_ok[i], 1)
                pool.wait_ge(idx_ok[i], count + 1)
                stand(pool)
                g.indirect_dma_start(out=xg[i][:], out_offset=None, in_=rows_dram,
                                     in_offset=bass.IndirectOffsetOnAxis(ap=gidx[i][:, 0:1], axis=0)).then_inc(done, 16)

            def scatter_add(i, e, k, b, to):
                stand(pool)
                g.tensor_copy(sidx[i][:], tab[:, ds(e * TAB_BLOCKS + k, 1)]).then_inc(S["sidx_ok"], 1)
                pool.wait_ge(S["sidx_ok"], b - SH + 1)
                stand(pool)
                g.indirect_dma_start(out=sums[to], out_offset=bass.IndirectOffsetOnAxis(ap=sidx[i][:, 0:1], axis=0),
                                     in_=ys[i][:], in_offset=None, compute_op=ALU.add).then_inc(sent[to], 16)

            def add_first(par, e, b):
                pool.wait_ge(S["scaled"], b + 1)
                pool.wait_ge(sent[par], 8 * (e - par) + SENT_0[par])
                scatter_add(par, e, 0, b, par)

            def add_last_first(b, xi):
                pool.wait_ge(S["scaled"], b + 1)
                pool.wait_ge(sent[2], 16 * xi + SENT_0[2])
                scatter_add(1, E - 1, 0, b, 2)

            def add_further(e, k, b, xi):
                pool.wait_ge(S["scaled"], b + 1)
                pool.wait_ge(sent[2], 16 * (xi + k) + (SENT_0[2] - (0 if is_last(e) else 16)))
                scatter_add(2, e, k, b, 2)

            def earlier_of(e):
                return pool.value_load(earlier[0:1, ds(e, 1)], min_val=0, max_val=E * TAB_BLOCKS)

            def further_of(e):
                return pool.value_load(further[0:1, ds(e, 1)], min_val=0, max_val=TAB_BLOCKS - 1)

            for b in range(SH):
                if b == 2:
                    list_tokens(TT - 1)
                if b + 2 >= SH:
                    if b + 2 == SH:
                        wait_routed()
                    pool.wait_ge(S["turned"], b + 1)
                    pool.wait_ge(S["tab_in"], 16)
                    gather(b % 2, b + 2 - SH, 0, 0, got[b % 2])
                if b >= 1:
                    pool.wait_ge(S["scaled"], b)
                    pool.dma_start(sums[1][(b - 1) * P:b * P, :], ys[(b - 1) % 2][:]).then_inc(sent[(b - 1) % 2], 16)
            f0 = further_of(0)
            with pool.If(f0 > 0):
                gather(2, 0, 1, earlier_of(0), S["x_in"])

            def retire(e, par, b0, xi, nx):
                with pool.If(nx < 2):
                    if is_last(e):
                        add_last_first(b0, xi)
                    else:
                        add_first(par, e, b0)
                with pool.If(nx > 0):
                    add_further(e, nx, b0 + nx, xi)

            def expert(e, par, pos):
                if pos != "last":
                    pool.wait_ge(S["w_ok"], e + 1)
                    gather(par, e + 2, 0, (e + 2 - par) // 2, got[par])
                xi, nx = earlier_of(e), further_of(e)
                b0 = xi + e + SH

                def left_over():
                    if pos == "first":
                        pool.wait_ge(S["scaled"], SH)
                        pool.dma_start(sums[1][(SH - 1) * P:T, :], ys[(SH - 1) % 2][:]).then_inc(sent[(SH - 1) % 2], 16)
                        for i in range(2):
                            pool.wait_ge(sent[i], 16 * SH // 2)
                    else:
                        xp = earlier_of(e - 1)
                        retire(e - 1, 1 - par, xp + e + (SH - 1), xp, further_of(e - 1))
                with pool.If(nx > 1):
                    left_over()
                    if is_last(e):
                        add_last_first(b0, xi)
                    else:
                        add_first(par, e, b0)
                    with pool.Fori(1, nx) as k:
                        pool.wait_ge(S["x_w_ok"], xi + k)
                        gather(2, e, k + 1, xi + k, S["x_in"])
                        add_further(e, k, b0 + k, xi)
                if not (pos == "last" and par == 1):
                    f1 = further_of(e + 1)
                    with pool.If(f1 > 0):
                        pool.wait_ge(S["x_w_ok"], xi + nx + 1)
                        gather(2, e + 1, 1, xi + nx, S["x_in"])
                with pool.If(nx < 2):
                    left_over()
                return b0, xi, nx

            expert(0, 0, "first")
            expert(1, 1, "")
            with pool.Fori(1, E // 2 - 1) as i:
                for par in range(2):
                    expert(2 * i + par, par, "")
            expert(E - 2, 0, "last")
            b0, xi, nx = expert(E - 1, 1, "last")
            retire(E - 1, 1, b0, xi, nx)
            pool.wait_ge(sent[2], 16 * (xi + nx) + (16 + SENT_0[2]))
            stand(pool)
            pool.sem_inc(S["summed"], 1)
            pool.wait_ge(S["g2_in"], 32)
            for t in range(TT):
                pool.wait_ge(S["f_g"], t + 1)
                g.tensor_tensor(fin2[:, t], fin0[:, t], b2[:], ALU.add).then_inc(S["f_out"], 1)

        @block.tensor
        def _(pe):
            pe.wait_ge(S["masks"], 1)
            for g in range(NXT):
                c, half = g // 2, g % 2
                if c == 0:
                    for t in range(4):
                        pe.wait_ge(tile_in[half * 4 + t], 16)
                if g >= 2:
                    pe.wait_ge(S["xt_lo_ok"], g - 1)
                for t in range(4):
                    i = pe.transpose(banks[g % 2][:, t * P:(t + 1) * P], xs[:, half * 4 + t, c * P:(c + 1) * P], ident[:])
                i.then_inc(S["xt_ps"], 1)
            pe.wait_ge(S["xt_lo_ok"], NXT)
            pe.wait_ge(S["wf_ok"], 2)
            for t in range(TT):
                for c in range(DC):
                    i = split_matmul(pe, banks[0][:, t * HEADS:(t + 1) * HEADS], xt_hi[:, c, t * P:(t + 1) * P],
                                     xt_lo[:, c, t * P:(t + 1) * P], wf_hi[:, c], wf_lo[:, c], c == 0, c == DC - 1)
            i.then_inc(S["z_ps"], 1)

            def gate_sums():
                pe.wait_ge(S["gate_ok"], 1)
                pe.wait_ge(S["masks"], 5)
                for half in range(2):
                    last = 4 * half + 3
                    for j in range(last + 1):
                        t0 = max(half * BANK, j * P)
                        i = pe.matmul(q_ps[0:HEADS, t0:(half + 1) * BANK], gate8[:, j, :], upto[:, t0 - j * P:(half + 1) * BANK - j * P],
                                      start=j == 0, stop=j == last, skip_group_check=True)
                i.then_inc(S["c_ps"], 1)

            for n in range(NVC * TT // 2):
                c0, t2 = n // (TT // 2), n % (TT // 2)
                if n == 4:
                    gate_sums()
                if t2 == 0:
                    pe.wait_ge(S["wv_lo_ok"], c0 + 1)
                if n == 0:
                    pe.wait_ge(S["z_ok"], 1)
                if n >= 2:
                    pe.wait_ge(S["v_ok"], n - 1)
                for j in range(2):
                    t = 2 * t2 + j
                    for c in range(DC):
                        i = split_matmul(pe, banks[n % 2][:, j * VC:(j + 1) * VC], xt_hi[:, c, t * P:(t + 1) * P],
                                         xt_lo[:, c, t * P:(t + 1) * P], wv_hi[:, c0 % 2, c], wv_lo[:, c0 % 2, c], c == 0, c == DC - 1)
                i.then_inc(S["v_ps"], 1)

            def project(p):
                pe.wait_ge(S["wqk_lo_ok"], p + 1)
                for j, ps in enumerate((q_ps, k_ps)):
                    for half in range(2):
                        r = slice(half * BANK, (half + 1) * BANK)
                        for c in range(DC):
                            i = split_matmul(pe, ps[:, r], wqk_hi[:, c, j], wqk_lo[:, c, j], xt_hi[:, c, r], xt_lo[:, c, r],
                                             c == 0, c == DC - 1)
                i.then_inc(S["proj"], 1)

            def slot_free(h, par, n):
                first_head = isinstance(h, int) and h == 0
                before = [m for m in range(n) if SLOT_BANK[par][m] == SLOT_BANK[par][n]]
                if before:
                    m, back = before[-1], 0
                elif not first_head:
                    m, back = max(m for m in range(SLOTS) if SLOT_BANK[1 - par][m] == SLOT_BANK[par][n]), 1
                else:
                    return
                if m < NQ:
                    pe.wait_ge(S["maxed"], h * NQ + (m + 1 - back * NQ))
                elif m < NQ + NR:
                    pe.wait_ge(S["r_lo"], h * NR + (m - NQ + 1 - back * NR))
                else:
                    pe.wait_ge(S["exped"], h * NK + (m - NQ - NR + 1 - back * NK))

            def outputs_left(heads):
                if not (isinstance(heads, int) and heads <= 0):
                    pe.wait_ge(S["normed"], heads)

            def scores_by_query(p, par):
                h = 2 * p + par
                pe.wait_ge(ev_lo[par], p + 1)
                pe.wait_ge(c_in[par], 32 * (p + 1))
                outputs_left(h - 1)
                for n, (t, k0, w) in enumerate(BY_QUERY):
                    slot_free(h, par, n)
                    s = slot_banks[SLOT_BANK[par][n]]
                    diag = k0 + w == (t + 1) * P
                    q, k = slice(t * P, (t + 1) * P), slice(k0, k0 + w)
                    i = split_matmul(pe, s[:, 0:w], q_hi[par][0:MAX_ROW, q], q_lo[par][0:MAX_ROW, q],
                                     k_hi[par][0:MAX_ROW, k], k_lo[par][0:MAX_ROW, k], True, not diag)
                    if diag:
                        i = pe.matmul(s[:, w - P:w], identb[:], mask_qk[:], start=False, stop=True, skip_group_check=True)
                    i.then_inc(S["score"], 1)

            def max_rows(p, par):
                h = 2 * p + par
                pe.wait_ge(S["mx_ok"], h + 1)
                for n in range(NR):
                    slot_free(h, par, NQ + n)
                    for t in range(4):
                        i = pe.transpose(banks[n % 2][:, t * P:(t + 1) * P], mx[:, 4 * n + t:4 * n + t + 1].to_broadcast([P, P]), ident[:])
                    i.then_inc(S["score"], 1)

            def scores_by_key(p, par):
                h = 2 * p + par
                pe.wait_ge(S["r_lo"], h * NR + NR)
                if par == 0:
                    outputs_left(h)
                for n, (t, q0, w, _) in enumerate(BY_KEY):
                    slot_free(h, par, NQ + NR + n)
                    s = slot_banks[SLOT_BANK[par][NQ + NR + n]]
                    diag = q0 == t * P
                    q, k = slice(q0, q0 + w), slice(t * P, (t + 1) * P)
                    i = split_matmul(pe, s[:, 0:w], k_hi[par][0:MAX_ROW + 1, k], k_lo[par][0:MAX_ROW + 1, k],
                                     q_hi[par][0:MAX_ROW + 1, q], q_lo[par][0:MAX_ROW + 1, q], True, not diag)
                    if diag:
                        i = pe.matmul(s[:, 0:P], identb[:], mask_kq[:], start=False, stop=True, skip_group_check=True)
                    i.then_inc(S["score"], 1)

            def weigh_v(p, par, tiles):
                h = 2 * p + par
                if 0 in tiles:
                    pe.wait_ge(S["exped"], h * NK + NK)
                    pe.wait_ge(va_in[par], 16 * (p + 1))
                    outputs_left(h)
                    if not (isinstance(p, int) and h == HEADS - 1):
                        pe.wait_ge(S["maxed"], h * NQ + (NQ + OUT_QUERIES))
                for (t, q0, w, at) in BY_KEY:
                    if t in tiles:
                        i = pe.matmul(out_ps[:, q0:q0 + w], va[par][:, t, :], probs[:, at:at + w], start=t == 0,
                                      stop=t == (3 if q0 < BANK else TT - 1), skip_group_check=True)
                if TT - 1 in tiles:
                    i.then_inc(S["pv"], 1)

            def pair(p, first=False, last=False):
                scores_by_query(p, 0)
                if not first:
                    weigh_v(p - 1, 1, range(TT))
                max_rows(p, 0)
                if not last:
                    pe.wait_ge(ev_lo[1], p + 1)
                    project(p + 1)
                scores_by_key(p, 0)
                scores_by_query(p, 1)
                weigh_v(p, 0, range(0, 4))
                max_rows(p, 1)
                weigh_v(p, 0, range(4, TT))
                scores_by_key(p, 1)

            pe.wait_ge(S["c_lo_ok"], 2)
            project(0)
            pe.wait_ge(S["v_ok"], NVC * TT // 2)
            pe.wait_ge(S["aug"], 2)
            pair(0, first=True)
            with pe.Fori(1, PAIRS - 1) as p:
                pair(p)
            pair(PAIRS - 1, last=True)
            weigh_v(PAIRS - 1, 1, range(TT))

            def out_projection(t):
                o = (q_ps, out_ps)[t % 2]
                pe.wait_ge(S["ot_lo_ok"], t + 1)
                if t == 0:
                    pe.wait_ge(S["wo_lo_ok"], DC)
                if t >= 2:
                    pe.wait_ge(S["r1_ok"], t - 1)
                for half in range(2):
                    r = slice(half * BANK, (half + 1) * BANK)
                    for c in range(DC):
                        i = split_matmul(pe, o[:, r], ot_hi[t % 2][:, c], ot_lo[t % 2][:, c], wo_hi[:, c, r], wo_lo[:, c, r],
                                         c == 0, c == DC - 1)
                    if half == 0 and t >= 1:
                        turn_x1(t - 1)
                i.then_inc(S["oproj"], 1)

            def turn_x1(t):
                pe.wait_ge(S["x1_ok"], t + 1)
                for c in range(DC):
                    i = pe.transpose(k_ps[:, c * P:(c + 1) * P], x1[:, c * P:(c + 1) * P], ident[:])
                i.then_inc(S["x1t_ps"], 1)

            def logits(t):
                pe.wait_ge(S["x1t_lo_ok"], t + 1)
                if static(t) and t == 0:
                    pe.wait_ge(S["wr_ok"], 2)
                else:
                    pe.wait_ge(S["ex_ok"], t)
                for c in range(DC):
                    i = split_matmul(pe, banks[0][:, 0:E], x1t_hi[:, c], x1t_lo[:, c], wr_hi[:, c], wr_lo[:, c], c == 0, c == DC - 1)
                i.then_inc(S["logit_ps"], 1)

            def places(t):
                pe.wait_ge(S["chosen_ok"], t + 1)
                if not (static(t) and t == 0):
                    pe.wait_ge(S["route0"], t)
                pe.matmul(banks[1][:, 0:E], before[:], chosen_b[:], start=True, stop=True, skip_group_check=True)
                pe.matmul(banks[1][:, E:2 * E], ones_b[:], chosen_b[:], start=True, stop=True, skip_group_check=True).then_inc(S["pos_ps"], 1)

            for t in range(TT):
                out_projection(t)
                if t >= 2:
                    places(t - 2)
                if t >= 1:
                    logits(t - 1)

            def turn_rows(src, ps):
                v = strided(src[:, 0:D])
                for c in range(DC):
                    i = pe.transpose(ps[:, c * P:(c + 1) * P], v[:, c], ident[:])
                return i

            def gate_up(s, w, names, n):
                g_hi, g_lo = split[w][0:2]
                o3 = banks[0][:].rearrange("p (g f) -> p g f", g=2)
                pe.wait_ge(S[names + "hi_ok"], n)
                for c in range(DC):
                    i = pe.matmul(o3, xb_hi[s][:, c], g_hi[:, :, c], start=c == 0, stop=False, skip_group_check=True)
                    if c == 0:
                        i.then_inc(S["started"], 1)
                    pe.matmul(o3, xb_hi[s][:, c], g_lo[:, :, c], start=False, stop=False, skip_group_check=True)
                pe.wait_ge(S[names + "lo_ok"], n)
                for c in range(DC):
                    i = pe.matmul(o3, xb_lo[s][:, c], g_hi[:, :, c], start=False, stop=c == DC - 1, skip_group_check=True)
                i.then_inc(S["gated"], 1)

            def turn_h(b):
                pe.wait_ge(S["h_ok"], b + 1)
                v = strided(hh[:])
                for c in range(FC):
                    i = pe.transpose(banks[1][:, c * P:(c + 1) * P], v[:, c], ident[:])
                i.then_inc(S["ht_ps"], 1)

            def down(b, w, nset):
                d_hi, d_lo = split[w][2:4]
                pe.wait_ge(S["ht_hi_ok"], b + 1)
                pe.wait_ge(S["d_lo_ok"], D_PIECES * nset)
                if not (static(b) and b == 0):
                    pe.wait_ge(S["scaled"], b)
                halves = [slice(half * BANK, (half + 1) * BANK) for half in range(2)]
                for r in halves:
                    for c in range(FC):
                        pe.matmul(k_ps[:, r], ht_hi[:, c], d_hi[:, c, r], start=c == 0, stop=False, skip_group_check=True)
                        pe.matmul(k_ps[:, r], ht_hi[:, c], d_lo[:, c, r], start=False, stop=False, skip_group_check=True)
                pe.wait_ge(S["ht_lo_ok"], b + 1)
                for r in halves:
                    for c in range(FC):
                        i = pe.matmul(k_ps[:, r], ht_lo[:, c], d_hi[:, c, r], start=False, stop=c == FC - 1, skip_group_check=True)
                i.then_inc(S["downed"], 1)

            pe.wait_ge(rows_in[0], 16)
            pe.wait_ge(S["r1_ok"], TT - 1)
            turn_rows(xg[0], q_ps).then_inc(S["turned"], 1)
            for b in range(SH):
                if b >= 1:
                    if b <= 3:
                        pe.wait_ge(S["route0"], TT - 3 + b)
                    turn_h(b - 1)
                pe.wait_ge(S["g_lo_ok"], G_PIECES)
                if b in (0, 2):
                    pe.wait_ge(S["ex_ok"], TT - 1 + b // 2)
                gate_up(b % 2, 0, "rows_", b + 1)
                if b + 1 < SH:
                    pe.wait_ge(rows_in[(b + 1) % 2], 16 * ((b + 1) // 2 + 1))
                else:
                    pe.wait_ge(got[0], 16)
                turn_rows(xg[(b + 1) % 2], q_ps).then_inc(S["turned"], 1)
                if b == 0:
                    turn_x1(TT - 1)
                if b == 1:
                    pe.wait_ge(S["x1t_lo_ok"], TT)
                if b >= 1:
                    down(b - 1, 0, 1)
                if b in (1, 2):
                    pe.wait_ge(S["ht_lo_ok"], b)
                    places(TT - 3 + b)
                if b == 1:
                    pe.wait_ge(S["h_ok"], b + 1)
                    logits(TT - 1)

            def expert(e, par, last=False):
                w = 1 - par
                xi = pe.value_load(earlier[0:1, ds(e, 1)], min_val=0, max_val=E * TAB_BLOCKS)
                b0 = xi + e + SH
                turn_h(b0 - 1)
                pe.wait_ge(S["g_lo_ok"], G_PIECES * (e + 2))
                gate_up(par, w, "rows_", SH + e + 1)
                nx = pe.value_load(further[0:1, ds(e, 1)], min_val=0, max_val=TAB_BLOCKS - 1)
                with pe.If(nx > 0):
                    pe.wait_ge(S["x_in"], 16 * xi + 16)
                    turn_rows(xg[2], out_ps).then_inc(S["x_turned"], 1)
                if not last:
                    pe.wait_ge(got[1 - par], 8 * (e + par) + 16)
                    turn_rows(xg[1 - par], q_ps).then_inc(S["turned"], 1)
                down(b0 - 1, par, e + 1)
                with pe.If(nx > 0):
                    turn_h(b0)
                    gate_up(2, w, "x_rows_", xi + 1)
                    down(b0, w, e + 2)
                    with pe.If(nx > 1):
                        with pe.Fori(1, nx) as k:
                            turn_h(b0 + k)
                            down(b0 + k, w, e + 2)
                            pe.wait_ge(S["x_in"], 16 * (xi + k) + 16)
                            turn_rows(xg[2], out_ps).then_inc(S["x_turned"], 1)
                            gate_up(2, w, "x_rows_", xi + k + 1)
                return b0, nx

            with pe.Fori(0, E // 2 - 1) as i:
                for par in range(2):
                    expert(2 * i + par, par)
            expert(E - 2, 0)
            b0, nx = expert(E - 1, 1, last=True)
            turn_h(b0 + nx)
            down(b0 + nx, 0, E + 1)

        @block.scalar
        def _(act):
            a = nc.scalar
            act.wait_ge(S["wf_in"], 16)
            a.copy(wf_hi[:], wf[:]).then_inc(S["wf_ok"], 1)
            for g in range(NXT):
                c, half = g // 2, g % 2
                act.wait_ge(S["xt_ps"], g + 1)
                a.copy(xt_hi[:, c, half * BANK:(half + 1) * BANK], banks[g % 2][:]).then_inc(S["xt_hi_ok"], 1)

            def split_wv(n):
                act.wait_ge(wv_in[n % 2], 16 * (n // 2 + 1))
                if n >= 2:
                    act.wait_ge(S["v_ps"], (n - 1) * TT // 2)
                a.copy(wv_hi[:, n % 2], wv[:, n % 2]).then_inc(S["wv_hi_ok"], 1)

            split_wv(0)
            split_wv(1)
            act.wait_ge(S["zabs_ok"], 1)
            a.activation(zexp[:], zabs[:], ACT.Exp, scale=-1.0).then_inc(S["zexp_ok"], 1)
            act.wait_ge(S["zexp_ok"], 2)
            a.activation(zlog[:], zexp[:], ACT.Ln).then_inc(S["zlog_ok"], 1)
            act.wait_ge(S["wqk_in"], 32)
            a.copy(wqk_hi[:], wqk[:]).then_inc(S["wqk_hi_ok"], 1)
            for n in range(NVC * TT // 2):
                if n and n % (TT // 2) == 0 and n // (TT // 2) + 1 < NVC:
                    split_wv(n // (TT // 2) + 1)
                if n == 5:
                    act.wait_ge(S["c_ps"], 1)
                    a.copy(c_hi[:], q_ps[0:HEADS, :]).then_inc(S["c_hi_ok"], 1)
                act.wait_ge(S["v_ps"], n + 1)
                if n >= 2:
                    act.wait_ge(v_stored[n % 2], 16 * (n // 2))
                a.copy(v_out[:, n % 2], banks[n % 2][:]).then_inc(S["v_ok"], 1)

            def take(p, par):
                act.wait_ge(S["proj"], p + 1)
                rows = slice(par * DH, (par + 1) * DH)
                a.copy(q_hi[par][0:DH, :], q_ps[rows, :])
                a.copy(k_hi[par][0:DH, :], k_ps[rows, :]).then_inc(ev_hi[par], 1)

            def max_row(p, par):
                h = 2 * p + par
                for n in range(NR):
                    act.wait_ge(S["score"], h * SLOTS + NQ + n + 1)
                    a.mul(q_hi[par][MAX_ROW:MAX_ROW + 1, n * BANK:(n + 1) * BANK], banks[n % 2][MAX_ROW:MAX_ROW + 1, :],
                          -1.0).then_inc(S["r_hi"], 1)

            def exponentials(p, par):
                h = 2 * p + par
                if not (isinstance(h, int) and h == 0):
                    act.wait_ge(S["pv"], h)
                for n, (_, _, w, at) in enumerate(BY_KEY):
                    act.wait_ge(S["score"], h * SLOTS + NQ + NR + n + 1)
                    a.activation(probs[:, at:at + w], slot_banks[SLOT_BANK[par][NQ + NR + n]][:, 0:w], ACT.Exp, scale=SCALE).then_inc(S["exped"], 1)

            def split_wo(pieces):
                for c in pieces:
                    act.wait_ge(wo_in[c % STAGES], 16 * (c // STAGES + 1))
                    a.copy(wo_hi[:, c], wo[:, c % STAGES]).then_inc(S["wo_hi_ok"], 1)

            def pair(p, first=False, last=False):
                if not first:
                    act.wait_ge(S["score"], 2 * p * SLOTS)
                take(p, 1)
                if not last:
                    act.wait_ge(S["wqk_in"], 32 * (p + 2))
                    act.wait_ge(S["proj"], p + 1)
                    a.copy(wqk_hi[:], wqk[:]).then_inc(S["wqk_hi_ok"], 1)
                else:
                    split_wo(range(2))
                max_row(p, 0)
                exponentials(p, 0)
                if not last:
                    act.wait_ge(S["score"], (2 * p + 1) * SLOTS)
                    take(p + 1, 0)
                else:
                    split_wo(range(2, DC))
                max_row(p, 1)
                exponentials(p, 1)

            act.wait_ge(S["aug"], 2)
            take(0, 0)
            pair(0, first=True)
            with act.Fori(1, PAIRS - 1) as p:
                pair(p)
            pair(PAIRS - 1, last=True)

            def heads_hi(t):
                act.wait_ge(S["normed"], HEADS + t * LAST_PARTS // TT)
                if t >= 2:
                    act.wait_ge(S["oproj"], t - 1)
                a.copy(ot_hi[t % 2][:], attn[:, :, t * P:(t + 1) * P]).then_inc(S["ot_hi_ok"], 1)

            def x1t_hi_of(t):
                act.wait_ge(S["x1t_ps"], t + 1)
                if not (static(t) and t == 0):
                    act.wait_ge(S["logit_ps"], t)
                a.copy(x1t_hi[:], k_ps[:].rearrange("p (c t) -> p c t", c=DC)).then_inc(S["x1t_hi_ok"], 1)

            def ax_of(t):
                act.wait_ge(S["x1_ok"], t + 1)
                if t:
                    act.wait_ge(S["ax_stored"], 16 * t)
                a.mul(ax[:], x1[:], ALPHA).then_inc(S["ax_ok"], 1)

            def exp_of(t):
                act.wait_ge(S["logit_ps"], t + 1)
                if not (static(t) and t == 0):
                    act.wait_ge(S["chosen_ok"], t)
                a.activation(ex[:], banks[0][:, 0:E], ACT.Exp, scale=-1.0).then_inc(S["ex_ok"], 1)

            def std_of(t):
                act.wait_ge(S["var_ok"], t + 2)
                a.activation(std[:], mv[:, 1:2], ACT.Sqrt, bias=eps[:, 0:1]).then_inc(S["std_ok"], 1)

            def w_high(which, done, w, k):
                raw, hi, _ = which(w, k)
                a.copy(hi, raw).then_inc(S[done], 1)

            heads_hi(0)
            heads_hi(1)
            act.wait_ge(S["c_loads"], 64)
            a.copy(wr_hi[:], wr[:]).then_inc(S["wr_ok"], 1)
            for t in range(TT - 1):
                std_of(t)
                if t >= 1:
                    exp_of(t - 1)
                if t + 2 < TT:
                    heads_hi(t + 2)
                ax_of(t)
                x1t_hi_of(t)
            for k in range(G_PIECES):
                act.wait_ge(g_raw[0][k], 16)
                w_high(g_piece, "g_hi_ok", 0, k)

            def rows_hi(s, ps, wait, n, done):
                act.wait_ge(S[wait], n)
                a.copy(xb_hi[s][:], ps[:].rearrange("p (c t) -> p c t", c=DC)).then_inc(S[done], 1)

            def silu(b):
                act.wait_ge(S["gated"], b + 1)
                a.activation(sg[:], banks[0][:, 0:FF], ACT.Silu).then_inc(S["silu_ok"], 1)

            def h_hi(b):
                act.wait_ge(S["ht_ps"], b + 1)
                a.copy(ht_hi[:], banks[1][:, 0:FF].rearrange("p (c t) -> p c t", c=FC)).then_inc(S["ht_hi_ok"], 1)

            def scale_rows(i, b, added):
                act.wait_ge(S["downed"], b + 1)
                if not (static(added) and added == 0):
                    act.wait_ge(sent[i], added)
                if static(b):
                    a.copy(ys[i][:], k_ps[:]).then_inc(S["scaled"], 1)
                else:
                    a.activation(ys[i][:], k_ps[:], ACT.Copy, scale=wcol[i][:, 0:1]).then_inc(S["scaled"], 1)

            def next_gate_up(b, e, par):
                act.wait_ge(S["started"], b + 1)
                for k in range(G_PIECES):
                    act.wait_ge(g_raw[par][k], 8 * (e + 2 - par) + 16)
                    w_high(g_piece, "g_hi_ok", par, k)

            rows_hi(0, q_ps, "turned", 1, "rows_hi_ok")
            exp_of(TT - 2)
            std_of(TT - 1)
            ax_of(TT - 1)
            for b in range(SH):
                if b >= 1:
                    h_hi(b - 1)
                if b == SH - 1:
                    act.wait_ge(S["extra_ok"], 2)
                    act.wait_ge(S["listed"], 16 * TT * TOP_K)
                    act.wait_ge(S["wts_stored"], 16 * TT)
                    act.wait_ge(S["x1_stored"], 16 * TT)
                    act.wait_ge(S["ax_stored"], 16 * TT)
                    act.wait_ge(S["c_fill"], 64)
                    act.wait_ge(sent[2], SENT_0[2])
                    next_gate_up(b, -1, 1)
                silu(b)
                rows_hi((b + 1) % 2, q_ps, "turned", b + 2, "rows_hi_ok")
                if b >= 1:
                    scale_rows((b - 1) % 2, b - 1, 16 * ((b - 1) // 2))
                if b == 0:
                    x1t_hi_of(TT - 1)
                    act.wait_ge(d_raw[0], 16 * D_PIECES)
                    for k in range(D_PIECES):
                        w_high(d_piece, "d_hi_ok", 0, k)
                if b == 1:
                    exp_of(TT - 1)

            def expert(e, par, pos):
                xi = act.value_load(earlier[0:1, ds(e, 1)], min_val=0, max_val=E * TAB_BLOCKS)
                b0 = xi + e + SH
                nx = act.value_load(further[0:1, ds(e, 1)], min_val=0, max_val=TAB_BLOCKS - 1)
                if pos != "first":
                    np_ = act.value_load(further[0:1, ds(e - 1, 1)], min_val=0, max_val=TAB_BLOCKS - 1)
                h_hi(b0 - 1)
                if pos != "last":
                    next_gate_up(b0, e, par)
                silu(b0)
                with act.If(nx > 0):
                    rows_hi(2, out_ps, "x_turned", xi + 1, "x_rows_hi_ok")
                if pos != "last":
                    rows_hi(1 - par, q_ps, "turned", SH + e + 2, "rows_hi_ok")
                act.wait_ge(S["downed"], b0 - 1)
                act.wait_ge(d_raw[1 - par], 8 * D_PIECES * (e + par) + 16 * D_PIECES)
                for k in range(D_PIECES):
                    w_high(d_piece, "d_hi_ok", 1 - par, k)
                if pos == "first":
                    scale_rows(1, SH - 1, 16 * ((SH - 1) // 2))
                else:
                    with act.If(np_ > 0):
                        scale_rows(2, b0 - 1, 16 * xi + (SENT_0[2] - 16))
                    with act.If(np_ < 1):
                        scale_rows(1 - par, b0 - 1, 8 * (e + par) + (SENT_0[1 - par] - 16))
                    if pos == "last":
                        act.sem_inc(S["set_free"], 1)
                with act.If(nx > 0):
                    h_hi(b0)
                    silu(b0 + 1)
                    scale_rows(par, b0, 8 * (e - par) + SENT_0[par])
                    with act.If(nx > 1):
                        with act.Fori(1, nx) as k:
                            h_hi(b0 + k)
                            scale_rows(2, b0 + k, 16 * (xi + k) + (SENT_0[2] - (0 if is_last(e) else 16)))
                            rows_hi(2, out_ps, "x_turned", xi + k + 1, "x_rows_hi_ok")
                            silu(b0 + k + 1)
                return b0, xi, nx
            expert(0, 0, "first")
            expert(1, 1, "")
            with act.Fori(1, E // 2 - 1) as i:
                for par in range(2):
                    expert(2 * i + par, par, "")
            expert(E - 2, 0, "")
            b0, xi, nx = expert(E - 1, 1, "last")
            h_hi(b0 + nx)
            with act.If(nx > 0):
                scale_rows(2, b0 + nx, 16 * (xi + nx) + SENT_0[2])
            with act.If(nx < 1):
                scale_rows(1, b0 + nx, 8 * (E - 2) + SENT_0[1])

            for t in range(TT):
                act.wait_ge(S["f_var"], t + 2)
                a.activation(fstd[t % 2][:], fmv[t % 2][:, 1:2], ACT.Sqrt, bias=feps[:, 0:1]).then_inc(S["f_std"], 1)
                act.wait_ge(S["f_mv"], t + 1)
                a.activation(fin2[:, t], fin0[:, t], ACT.Identity, bias=fnm[t % 2][:, 0:1], scale=frstd[t % 2][:, 0:1]).then_inc(S["f_norm"], 1)

        @block.vector
        def _(dve):
            dve.wait_ge(S["wf_ok"], 1)
            dve.tensor_tensor(wf_lo[:], wf[:], wf_hi[:], ALU.subtract).then_inc(S["wf_ok"], 1)
            for g in range(NXT):
                c, half = g // 2, g % 2
                dve.wait_ge(S["xt_hi_ok"], g + 1)
                r = slice(half * BANK, (half + 1) * BANK)
                dve.tensor_tensor(xt_lo[:, c, r], banks[g % 2][:], xt_hi[:, c, r], ALU.subtract).then_inc(S["xt_lo_ok"], 1)

            def split_wv(n):
                dve.wait_ge(S["wv_hi_ok"], n + 1)
                dve.tensor_tensor(wv_lo[:, n % 2], wv[:, n % 2], wv_hi[:, n % 2], ALU.subtract).then_inc(S["wv_lo_ok"], 1)

            split_wv(0)
            dve.wait_ge(S["z_ps"], 1)
            dve.wait_ge(S["bf_in"], 16)
            dve.tensor_tensor(z[:], banks[0][:, 0:TT * HEADS].rearrange("p (t h) -> p t h", t=TT),
                              bf[:, None, :].to_broadcast([P, TT, HEADS]), ALU.add).then_inc(S["z_ok"], 1)
            dve.wait_ge(S["z_ok"], 1)
            dve.scalar_tensor_tensor(out=zabs[:], in0=z[:], scalar=-1.0, in1=z[:], op0=ALU.mult, op1=ALU.max).then_inc(S["zabs_ok"], 1)
            dve.tensor_scalar(zmin[:], z[:], 0.0, None, ALU.min).then_inc(S["zmin_ok"], 1)
            split_wv(1)
            dve.wait_ge(S["zexp_ok"], 1)
            dve.tensor_scalar(zexp[:], zexp[:], 1.0, None, ALU.add).then_inc(S["zexp_ok"], 1)
            dve.wait_ge(S["zlog_ok"], 1)
            dve.wait_ge(S["zmin_ok"], 1)
            dve.tensor_tensor(z[:], zlog[:], zmin[:], ALU.subtract).then_inc(S["z_ok"], 1)
            dve.wait_ge(S["z_ok"], 2)
            dve.tensor_scalar(gate8[:], z[:], 1.0 / SCALE, None, ALU.mult).then_inc(S["gate_ok"], 1)
            dve.wait_ge(S["wqk_hi_ok"], 1)
            dve.tensor_tensor(wqk_lo[:], wqk[:], wqk_hi[:], ALU.subtract).then_inc(S["wqk_lo_ok"], 1)
            split_wv(2)
            dve.wait_ge(S["c_hi_ok"], 1)
            for half in range(2):
                r = slice(half * BANK, (half + 1) * BANK)
                dve.tensor_tensor(c_lo[:, r], q_ps[0:HEADS, r], c_hi[:, r], ALU.subtract).then_inc(S["c_lo_ok"], 1)
            split_wv(3)
            dve.wait_ge(S["aug"], 2)
            dve.memset(mx2[:], -3e38).then_inc(S["mx20"], 1)
            dve.wait_ge(S["mx20"], 1)

            def take(p, par):
                dve.wait_ge(ev_hi[par], p + 1)
                rows = slice(par * DH, (par + 1) * DH)
                dve.tensor_tensor(q_lo[par][0:DH, :], q_ps[rows, :], q_hi[par][0:DH, :], ALU.subtract)
                dve.tensor_tensor(k_lo[par][0:DH, :], k_ps[rows, :], k_hi[par][0:DH, :], ALU.subtract).then_inc(ev_lo[par], 1)

            def maxima(p, par):
                h = 2 * p + par
                for n, (t, k0, w) in enumerate(BY_QUERY):
                    dve.wait_ge(S["score"], h * SLOTS + n + 1)
                    dve.tensor_reduce(mx2[:, t, k0 // BANK:k0 // BANK + 1], slot_banks[SLOT_BANK[par][n]][:, 0:w], AX_X, ALU.max).then_inc(S["maxed"], 1)
                dve.wait_ge(S["maxed"], h * NQ + NQ)
                dve.tensor_reduce(mx[:], mx2[:], AX_X, ALU.max).then_inc(S["mx_ok"], 1)

            def max_row(p, par):
                h = 2 * p + par
                for n in range(NR):
                    dve.wait_ge(S["r_hi"], h * NR + n + 1)
                    at = slice(n * BANK, (n + 1) * BANK)
                    dve.scalar_tensor_tensor(out=q_lo[par][MAX_ROW:MAX_ROW + 1, at], in0=banks[n % 2][MAX_ROW:MAX_ROW + 1, :], scalar=-1.0,
                                             in1=q_hi[par][MAX_ROW:MAX_ROW + 1, at], op0=ALU.mult, op1=ALU.subtract).then_inc(S["r_lo"], 1)

            def normalise(p, par, part=0, parts=1):
                h = 2 * p + par
                r = slice(part * T // parts, (part + 1) * T // parts)
                dve.wait_ge(S["pv"], h + 1)
                dve.reciprocal(rec[:, r], out_ps[DH:P, r]).then_inc(S["rec_ok"], 1)
                dve.wait_ge(S["rec_ok"], h + 1 + part)
                dve.tensor_tensor(attn[par * DH:(par + 1) * DH, bass.ds(p, 1), r], out_ps[0:DH, None, r], rec[:, None, r],
                                  ALU.mult).then_inc(S["normed"], 1)

            def split_wo(pieces):
                for c in pieces:
                    dve.wait_ge(S["wo_hi_ok"], c + 1)
                    dve.tensor_tensor(wo_lo[:, c], wo[:, c % STAGES], wo_hi[:, c], ALU.subtract).then_inc(S["wo_lo_ok"], 1)

            def pair(p, first=False, last=False):
                maxima(p, 0)
                take(p, 1)
                if not last:
                    dve.wait_ge(S["wqk_hi_ok"], p + 2)
                    dve.tensor_tensor(wqk_lo[:], wqk[:], wqk_hi[:], ALU.subtract).then_inc(S["wqk_lo_ok"], 1)
                else:
                    split_wo(range(2))
                max_row(p, 0)
                if not first:
                    normalise(p - 1, 1)
                maxima(p, 1)
                if not last:
                    take(p + 1, 0)
                max_row(p, 1)
                normalise(p, 0)

            take(0, 0)
            pair(0, first=True)
            with dve.Fori(1, PAIRS - 1) as p:
                pair(p)
            pair(PAIRS - 1, last=True)
            split_wo(range(2, DC))

            def heads_lo(t):
                dve.wait_ge(S["ot_hi_ok"], t + 1)
                dve.tensor_tensor(ot_lo[t % 2][:], attn[:, :, t * P:(t + 1) * P], ot_hi[t % 2][:], ALU.subtract).then_inc(S["ot_lo_ok"], 1)

            for part in range(LAST_PARTS):
                normalise(PAIRS - 1, 1, part, LAST_PARTS)
                if part in (1, 2):
                    heads_lo(part - 1)

            def steps(name, base_count):
                n = [0]

                def step(ins):
                    n[0] += 1
                    ins.then_inc(S[name], 1)
                    dve.wait_ge(S[name], base_count + n[0])
                return step, n

            def residual(t):
                dve.wait_ge(S["x_res_in"], 16 * (t + 1))
                dve.wait_ge(S["oproj"], t + 1)
                dve.scalar_tensor_tensor(out=r1[:], in0=x_res[:], scalar=ALPHA, in1=(q_ps, out_ps)[t % 2][:], op0=ALU.mult, op1=ALU.add).then_inc(S["r1_ok"], 1)

            LN_STEPS = 4

            def layer_norm(t):
                dve.wait_ge(S["r1_ok"], t + 1)
                step, n = steps("ln_step", LN_STEPS * t)
                dve.bn_stats(stat[:, 0, :], r1[:, 0:BANK])
                step(dve.bn_stats(stat[:, 1, :], r1[:, BANK:D]))
                dve.bn_aggr(mv[:], stat[:]).then_inc(S["var_ok"], 1)
                dve.wait_ge(S["std_ok"], t + 1)
                step(dve.reciprocal(rstd[:], std[:]))
                step(dve.tensor_scalar(xn[:], r1[:], mv[:, 0:1], rstd[:, 0:1], ALU.subtract, ALU.mult))
                if static(t) and t == 0:
                    dve.wait_ge(S["c_loads"], 64)
                step(dve.tensor_tensor(xg1[:], xn[:], g1[:], ALU.mult))
                assert n[0] == LN_STEPS
                if not (static(t) and t == 0):
                    dve.wait_ge(S["x1_stored"], 16 * t)
                    dve.wait_ge(S["x1t_ps"], t)
                    dve.wait_ge(S["ax_ok"], t)
                dve.tensor_tensor(x1[:], xg1[:], b1[:], ALU.add).then_inc(S["x1_ok"], 1)

            def x1t_lo_of(t):
                dve.wait_ge(S["x1t_hi_ok"], t + 1)
                dve.tensor_tensor(x1t_lo[:], k_ps[:].rearrange("p (c t) -> p c t", c=DC), x1t_hi[:], ALU.subtract).then_inc(S["x1t_lo_ok"], 1)

            ROUTE_STEPS = 15

            def route(t):
                step, n = steps("route_step", ROUTE_STEPS * t)
                dve.wait_ge(S["ex_ok"], t + 1)
                step(dve.tensor_scalar(ex1[:], ex[:], 1.0, None, ALU.add))
                step(dve.reciprocal(score[:], ex1[:]))
                step(dve.tensor_tensor(sel[:], score[:], rb[:], ALU.add))
                for g in range(GROUPS):
                    i = dve.max(top_g[:, g, :], sel[:, g * GE:(g + 1) * GE])
                step(i)
                step(dve.tensor_tensor(gsum[:], top_g[:, :, 0], top_g[:, :, 1], ALU.add))
                step(dve.max(gsort[:], gsum[:]))
                step(dve.tensor_copy(gtop[:, 0:TOP_GROUPS], gsort[:, 0:TOP_GROUPS]))
                step(dve.match_replace(gleft[:], gtop[:], gsum[:], OUT))
                step(dve.tensor_scalar(gpen[:], gleft[:], OUT / 2, NEVER, ALU.is_ge, ALU.mult))
                step(dve.tensor_tensor(selm[:].rearrange("p (g e) -> p g e", g=GROUPS), sel[:].rearrange("p (g e) -> p g e", g=GROUPS),
                                       gpen[:, :, None].to_broadcast([P, GROUPS, GE]), ALU.add))
                step(dve.max(top8[:], selm[:]))
                step(dve.match_replace(left[:], top8[:], selm[:], OUT))
                step(dve.tensor_scalar(chosen[:], left[:], OUT / 2, None, ALU.is_lt))
                if not (static(t) and t == 0):
                    dve.wait_ge(S["pos_ps"], t)
                dve.tensor_copy(chosen_b[:], chosen[:]).then_inc(S["chosen_ok"], 1)
                step(dve.tensor_tensor_reduce(out=wraw[:], in0=score[:], in1=chosen[:], scale=1.0, scalar=0.0, op0=ALU.mult,
                                              op1=ALU.add, accum_out=wsum[:]))
                step(dve.reciprocal(wrec[:], wsum[:]))
                assert n[0] == ROUTE_STEPS
                if not (static(t) and t == 0):
                    dve.wait_ge(S["wts_stored"], 16 * t)
                dve.tensor_scalar(wts[:], wraw[:], wrec[:, 0:1], ROUTED_SCALE, ALU.mult, ALU.mult).then_inc(S["wts_ok"], 1)

            POS_STEPS = 7

            def place(t):
                step, n = steps("pos_step", POS_STEPS * t)
                dve.wait_ge(S["pos_ps"], t + 1)
                step(dve.tensor_tensor(pos[:], banks[1][:, 0:E], base[:], ALU.add))
                ins = dve.tensor_tensor(base[:], base[:], banks[1][:, E:2 * E], ALU.add)
                ins.then_inc(S["route0"], 1)
                dve.wait_ge(S["route0"], t + 1)
                dve.tensor_scalar(pos_m[:], pos[:], P - 1, None, ALU.bitwise_and)
                step(dve.tensor_scalar(pos_q[:], pos[:], P.bit_length() - 1, None, ALU.logical_shift_right))
                step(dve.tensor_tensor(pos_b[:], pos_q[:], e8[:], ALU.add))
                step(dve.scalar_tensor_tensor(out=dest[:], in0=pos_m[:], scalar=float(TAB), in1=pos_b[:], op0=ALU.mult, op1=ALU.add))
                step(dve.tensor_scalar(dest[:], dest[:], 1.0, None, ALU.add))
                step(dve.tensor_tensor(dest1[:], dest[:], chosen[:], ALU.mult))
                step(dve.max(dest8[:], dest1[:]))
                assert n[0] == POS_STEPS
                if not (static(t) and t == 0):
                    dve.wait_ge(S["listed"], 16 * TOP_K * t)
                dve.tensor_scalar(dest_i[:], dest8[:], -1.0, None, ALU.add).then_inc(S["dest_ok"], 1)

            dve.wait_ge(S["c_const"], 8)
            dve.memset(eps[:], LN_EPS).then_inc(S["var_ok"], 1)
            dve.wait_ge(S["c_loads"], 64)
            dve.wait_ge(S["wr_ok"], 1)
            dve.tensor_tensor(wr_lo[:], wr[:], wr_hi[:], ALU.subtract).then_inc(S["wr_ok"], 1)
            for t in range(TT - 1):
                residual(t)
                layer_norm(t)
                if t >= 2:
                    place(t - 2)
                if t >= 1:
                    route(t - 1)
                if t + 2 < TT:
                    heads_lo(t + 2)
                x1t_lo_of(t)

            def count_blocks():
                step, n = steps("pos_step", POS_STEPS * TT)
                u, v = nblk[0], nblk[1]
                step(dve.tensor_scalar(nblk_i[0][:], base[0:1, :], float(P - 1), None, ALU.add))
                step(dve.tensor_scalar(nblk_i[1][:], nblk_i[0][:], P.bit_length() - 1, None, ALU.logical_shift_right))
                step(dve.tensor_scalar(u[:], nblk_i[1][:], -1.0, 0.0, ALU.add, ALU.max))
                dve.tensor_copy(further[:], u[:]).then_inc(S["extra_ok"], 1)
                shift = 1
                while shift < E:
                    step(dve.tensor_copy(v[:, 0:shift], u[:, 0:shift]))
                    step(dve.tensor_tensor(v[:, shift:E], u[:, shift:E], u[:, 0:E - shift], ALU.add))
                    u, v = v, u
                    shift *= 2
                step(dve.memset(earlier[:], 0))
                dve.tensor_copy(earlier[:, 1:E + 1], u[:]).then_inc(S["extra_ok"], 1)

            def w_low(which, hi_ok, lo_ok, w, n, k):
                raw, hi, lo = which(w, k)
                dve.wait_ge(S[hi_ok], n + k + 1)
                dve.tensor_tensor(lo, raw, hi, ALU.subtract).then_inc(S[lo_ok], 1)

            def rows_lo(s, ps, wait, n, done):
                dve.wait_ge(S[wait], n)
                dve.tensor_tensor(xb_lo[s][:], ps[:].rearrange("p (c t) -> p c t", c=DC), xb_hi[s][:], ALU.subtract).then_inc(S[done], 1)

            def h_of(b):
                dve.wait_ge(S["silu_ok"], b + 1)
                dve.tensor_tensor(hh[:], sg[:], banks[0][:, FF:2 * FF], ALU.mult).then_inc(S["h_ok"], 1)

            def h_lo(b):
                dve.wait_ge(S["ht_hi_ok"], b + 1)
                dve.tensor_tensor(ht_lo[:], banks[1][:, 0:FF].rearrange("p (c t) -> p c t", c=FC), ht_hi[:], ALU.subtract).then_inc(S["ht_lo_ok"], 1)

            def token_weights(i, e, b, done):
                dve.wait_ge(S["scaled"], b - 1)
                stand(dve)
                dve.tensor_copy(wcol[i][:], xg[i][:, ds(D + e, 1)]).then_inc(S[done], 1)

            dve.wait_ge(S["oproj"], TT)
            for k in range(G_PIECES):
                w_low(g_piece, "g_hi_ok", "g_lo_ok", 0, 0, k)
            rows_lo(0, q_ps, "rows_hi_ok", 1, "rows_lo_ok")
            residual(TT - 1)
            layer_norm(TT - 1)
            place(TT - 3)
            for b in range(SH):
                if b >= 1:
                    h_lo(b - 1)
                if b == SH - 1:
                    dve.wait_ge(S["extra_ok"], 2)
                    dve.wait_ge(S["listed"], 16 * TT * TOP_K)
                    dve.wait_ge(S["wts_stored"], 16 * TT)
                    dve.wait_ge(S["x1_stored"], 16 * TT)
                    dve.wait_ge(S["ax_stored"], 16 * TT)
                    dve.wait_ge(S["c_fill"], 64)
                    dve.wait_ge(sent[2], SENT_0[2])
                    for k in range(G_PIECES):
                        w_low(g_piece, "g_hi_ok", "g_lo_ok", 1, G_PIECES, k)
                h_of(b)
                rows_lo((b + 1) % 2, q_ps, "rows_hi_ok", b + 2, "rows_lo_ok")
                if b == 0:
                    route(TT - 2)
                    x1t_lo_of(TT - 1)
                    for k in range(D_PIECES):
                        w_low(d_piece, "d_hi_ok", "d_lo_ok", 0, 0, k)
                if b == 1:
                    place(TT - 2)
                    route(TT - 1)
                if b == 2:
                    place(TT - 1)
                if b == 3:
                    count_blocks()
            dve.sem_inc(S["x_w_ok"], 1)

            def expert(e, par, last=False):
                xi = dve.value_load(earlier[0:1, ds(e, 1)], min_val=0, max_val=E * TAB_BLOCKS)
                b0 = xi + e + SH
                nx = dve.value_load(further[0:1, ds(e, 1)], min_val=0, max_val=TAB_BLOCKS - 1)
                h_lo(b0 - 1)
                token_weights(par, e, b0, "w_ok")
                if not last:
                    for k in range(G_PIECES - 1):
                        w_low(g_piece, "g_hi_ok", "g_lo_ok", par, G_PIECES * (e + 2), k)
                h_of(b0)
                with dve.If(nx > 0):
                    rows_lo(2, out_ps, "x_rows_hi_ok", xi + 1, "x_rows_lo_ok")
                if not last:
                    w_low(g_piece, "g_hi_ok", "g_lo_ok", par, G_PIECES * (e + 2), G_PIECES - 1)
                    rows_lo(1 - par, q_ps, "rows_hi_ok", SH + e + 2, "rows_lo_ok")
                for k in range(D_PIECES):
                    w_low(d_piece, "d_hi_ok", "d_lo_ok", 1 - par, D_PIECES * (e + 1), k)
                with dve.If(nx > 0):
                    h_lo(b0)
                    token_weights(2, e, b0 + 1, "x_w_ok")
                    h_of(b0 + 1)
                    with dve.If(nx > 1):
                        with dve.Fori(1, nx) as k:
                            h_lo(b0 + k)
                            rows_lo(2, out_ps, "x_rows_hi_ok", xi + k + 1, "x_rows_lo_ok")
                            token_weights(2, e, b0 + k + 2, "x_w_ok")
                            h_of(b0 + k + 1)
                return b0, nx
            with dve.Fori(0, E // 2 - 1) as i:
                for par in range(2):
                    expert(2 * i + par, par)
            expert(E - 2, 0)
            b0, nx = expert(E - 1, 1, last=True)
            h_lo(b0 + nx)

            step, n = steps("f_step", 0)
            for t in range(TT):
                dve.wait_ge(tile_in[t], 16 * 3)
                dve.tensor_tensor(fin0[:, t], fin0[:, t], fin1(t), ALU.add).then_inc(S["f_part"], 1)
            dve.wait_ge(S["summed"], 1)
            dve.memset(feps[:], LN_EPS).then_inc(S["f_var"], 1)
            for t in range(TT + 1):
                i = t % 2
                if t < TT:
                    dve.wait_ge(S["f_part"], t + 1)
                    dve.wait_ge(tile_in[t], 16 * 4)
                    dve.tensor_tensor(fin0[:, t], fin0[:, t], fin2[:, t], ALU.add).then_inc(S["f_sum"], 1)
                    dve.wait_ge(S["f_sum"], t + 1)
                    dve.bn_stats(fstat[i][:, 0, :], fin0[:, t, 0:BANK])
                    step(dve.bn_stats(fstat[i][:, 1, :], fin0[:, t, BANK:D]))
                    if t >= 2:
                        dve.wait_ge(S["f_norm"], t - 1)
                    dve.bn_aggr(fmv[i][:], fstat[i][:]).then_inc(S["f_var"], 1)
                if t >= 1:
                    if t == 1:
                        dve.wait_ge(S["g2_in"], 32)
                    dve.wait_ge(S["f_norm"], t)
                    dve.tensor_tensor(fin0[:, t - 1], fin2[:, t - 1], g2[:], ALU.mult).then_inc(S["f_g"], 1)
                if t < TT:
                    dve.wait_ge(S["f_std"], t + 1)
                    step(dve.reciprocal(frstd[i][:], fstd[i][:]))
                    dve.scalar_tensor_tensor(out=fnm[i][:], in0=fmv[i][:, 0:1], scalar=-1.0, in1=frstd[i][:], op0=ALU.mult,
                                             op1=ALU.mult).then_inc(S["f_mv"], 1)


_INS = ["x", "fox_w_in", "fox_b_f", "fox_w_out", "ln1_g", "ln1_b", "moe_router", "moe_router_bias", "moe_w_gate", "moe_w_up",
        "moe_w_down", "moe_ws_gate", "moe_ws_up", "moe_ws_down", "ln2_g", "ln2_b"]
_ROWS = {"fox_b_f", "ln1_g", "ln1_b", "moe_router_bias", "ln2_g", "ln2_b"}


def kernel(**inputs):
    import numpy as _np
    import concourse.bacc as _bacc
    from concourse import mybir as _mybir
    from concourse.bass_utils import run_bass_kernel_spmd as _run

    nc = _bacc.Bacc("TRN2", target_bir_lowering=False, num_devices=1)
    arrays, args = {}, []
    for name in _INS:
        a = _np.ascontiguousarray(inputs[name])
        if name not in _ROWS:
            a = a[0]
        arrays[f"in_{name}_dram"] = a
        args.append(nc.dram_tensor(f"in_{name}_dram", a.shape, _mybir.dt.from_np(a.dtype), kind="ExternalInput").ap())
    args.append(nc.dram_tensor("out_dram", (T, D), F32, kind="ExternalOutput").ap())
    build(nc, *args)
    r = _run(nc, [arrays], core_ids=[0])
    return r.results[0]["out_dram"].reshape(1, T, D)
```
